# Optimizing a Trainium2 kernel written in Bass

```python
import math
import jax, jax.numpy as jnp
from jax import lax
import numpy as np

D_MODEL = 2048
BATCH = 1
SEQ = 512
DEPTH = 1

GRID_W = 64
NA_HEADS = 16
NA_HEAD_DIM = 64
NA_WIDTH = NA_HEADS * NA_HEAD_DIM
NA_WIN_ROWS = 8
NA_WIN_COLS = 16
NA_QBLOCK_COLS = 16
NA_KBLOCK_COLS = NA_QBLOCK_COLS + NA_WIN_COLS
ML_HEADS = 4
ML_HEAD_DIM = 256
ML_WIDTH = ML_HEADS * ML_HEAD_DIM
ML_CHUNK = 128
CONV_WIDTH = 3
D_FF = 5504
LN_EPS = 1e-5
NEG_BIG = -1e30
DEEPNORM_ALPHA = (2 * DEPTH) ** 0.25
DEEPNORM_BETA = (8 * DEPTH) ** -0.25
IN_SIZES = (3 * NA_WIDTH, ML_WIDTH, ML_WIDTH, ML_WIDTH, ML_WIDTH, 4 * ML_HEADS, 2 * D_MODEL)
IN_WIDTH = sum(IN_SIZES)
IN_SPLIT_POINTS = tuple(int(v) for v in np.cumsum(IN_SIZES)[:-1])

kernel_name = "hybrid_natten_mlstm_convglu_deepnorm"

def layer_norm(x, g, b):
    xf = x.astype(jnp.float32)
    mu = jnp.mean(xf, axis=-1, keepdims=True)
    var = jnp.mean(jnp.square(xf - mu), axis=-1, keepdims=True)
    y = (xf - mu) * lax.rsqrt(var + LN_EPS)
    return (y * g + b).astype(x.dtype)

def dwconv_centred(x, w, b):
    s = x.shape[1]
    pad = CONV_WIDTH // 2
    xp = jnp.pad(x, ((0, 0), (pad, pad), (0, 0)))
    y = xp[:, 0:s] * w[0]
    for i in range(1, CONV_WIDTH):
        y = y + xp[:, i:i + s] * w[i]
    return y + b

def neighborhood_attention(q, k, v, rpb):
    bsz, s, h, d = q.shape
    rows = s // GRID_W
    kh = min(NA_WIN_ROWS, rows)
    nqb = GRID_W // NA_QBLOCK_COLS

    def to_grid(t):
        return t.reshape(bsz, rows, GRID_W, h, d).transpose(0, 3, 1, 2, 4)

    qg = to_grid(q) * (d ** -0.5)
    kg = to_grid(k)
    vg = to_grid(v)

    qcol = np.arange(GRID_W).reshape(nqb, NA_QBLOCK_COLS)
    kstart = np.clip(qcol[:, 0] - NA_WIN_COLS // 2, 0, GRID_W - NA_KBLOCK_COLS)
    kcol = kstart[:, None] + np.arange(NA_KBLOCK_COLS)
    wstart = np.clip(qcol - NA_WIN_COLS // 2, 0, GRID_W - NA_WIN_COLS)
    col_valid = (kcol[:, None, :] >= wstart[..., None]) & (kcol[:, None, :] < wstart[..., None] + NA_WIN_COLS)
    dc_idx = np.clip(kcol[:, None, :] - qcol[:, :, None] + NA_WIN_COLS - 1, 0, 2 * NA_WIN_COLS - 2)
    col_bias = rpb[:, :, dc_idx]
    valid = jnp.asarray(col_valid)[:, :, None, :]

    def row_step(r):
        rs = jnp.clip(r - kh // 2, 0, rows - kh)
        krows = lax.dynamic_slice_in_dim(kg, rs, kh, axis=2)
        vrows = lax.dynamic_slice_in_dim(vg, rs, kh, axis=2)
        kb = krows[:, :, :, kcol, :]
        vb = vrows[:, :, :, kcol, :]
        qr = lax.dynamic_index_in_dim(qg, r, axis=2, keepdims=False).reshape(bsz, h, nqb, NA_QBLOCK_COLS, d)
        sc = jnp.einsum('bhjqd,bhrjkd->bhjqrk', qr, kb).astype(jnp.float32)
        dr_idx = rs + jnp.arange(kh) - r + (NA_WIN_ROWS - 1)
        bias = jnp.take(col_bias, dr_idx, axis=1).transpose(0, 2, 3, 1, 4)
        sc = jnp.where(valid, sc + bias.astype(jnp.float32), NEG_BIG)
        p = jax.nn.softmax(sc.reshape(bsz, h, nqb, NA_QBLOCK_COLS, kh * NA_KBLOCK_COLS), axis=-1)
        p = p.reshape(sc.shape).astype(vb.dtype)
        o = jnp.einsum('bhjqrk,bhrjkd->bhjqd', p, vb)
        return o.reshape(bsz, h, GRID_W, d)

    out = lax.map(row_step, jnp.arange(rows))
    return out.transpose(1, 0, 3, 2, 4).reshape(bsz, s, h * d)

def mlstm_chunkwise(q, k, v, logi, logf):
    g, bsz, h, s, dk = q.shape
    dv = v.shape[-1]
    nc = s // ML_CHUNK

    def chunks(t):
        return jnp.moveaxis(t.reshape(t.shape[:3] + (nc, ML_CHUNK) + t.shape[4:]), 3, 0)

    tri = jnp.tril(jnp.ones((ML_CHUNK, ML_CHUNK), dtype=bool))

    def step(carry, xs):
        c_st, n_st, m_st = carry
        qc, kc, vc, li, lf = xs
        b = jnp.cumsum(lf, axis=-1)
        dlog = jnp.where(tri, b[..., :, None] - b[..., None, :] + li[..., None, :], NEG_BIG)
        inter = b + m_st[..., None]
        m_t = jnp.maximum(jnp.max(dlog, axis=-1), inter)
        dw = jnp.exp(dlog - m_t[..., None])
        w_inter = jnp.exp(inter - m_t)
        sqk = jnp.einsum('gbhtd,gbhsd->gbhts', qc, kc) * dw
        num = w_inter[..., None] * jnp.einsum('gbhtd,gbhde->gbhte', qc, c_st) + jnp.einsum('gbhts,gbhse->gbhte', sqk, vc)
        den = w_inter * jnp.einsum('gbhtd,gbhd->gbht', qc, n_st) + jnp.sum(sqk, axis=-1)
        hc = num / jnp.maximum(jnp.abs(den), jnp.exp(-m_t))[..., None]
        b_last = b[..., -1]
        logw = b_last[..., None] - b + li
        m_new = jnp.maximum(b_last + m_st, jnp.max(logw, axis=-1))
        ws = jnp.exp(logw - m_new[..., None])
        decay = jnp.exp(b_last + m_st - m_new)
        kw = kc * ws[..., None]
        c_new = decay[..., None, None] * c_st + jnp.einsum('gbhsd,gbhse->gbhde', kw, vc)
        n_new = decay[..., None] * n_st + jnp.sum(kw, axis=-2)
        return (c_new, n_new, m_new), hc

    init = (jnp.zeros((g, bsz, h, dk, dv), jnp.float32),
            jnp.zeros((g, bsz, h, dk), jnp.float32),
            jnp.full((g, bsz, h), NEG_BIG, jnp.float32))
    _, hs = lax.scan(step, init, (chunks(q), chunks(k), chunks(v), chunks(logi), chunks(logf)))
    return jnp.moveaxis(hs, 0, 3).reshape(g, bsz, h, s, dv)

def mlstm_branch(q_pre, k_pre, v_in, o_pre, gate_pre, conv_w, conv_b, igate_b, fgate_b, norm_w):
    bsz, s, _ = q_pre.shape
    qk = jax.nn.silu(dwconv_centred(jnp.concatenate([q_pre, k_pre], axis=-1), conv_w, conv_b))
    q, k = jnp.split(qk, 2, axis=-1)

    def heads(t):
        return t.reshape(bsz, s, ML_HEADS, ML_HEAD_DIM).transpose(0, 2, 1, 3).astype(jnp.float32)

    q = heads(q)
    k = heads(k) * (ML_HEAD_DIM ** -0.5)
    v = heads(v_in)
    gp = gate_pre.astype(jnp.float32)
    ig = (gp[..., :2 * ML_HEADS] + igate_b).reshape(bsz, s, 2, ML_HEADS).transpose(2, 0, 3, 1)
    fg = (gp[..., 2 * ML_HEADS:] + fgate_b).reshape(bsz, s, 2, ML_HEADS).transpose(2, 0, 3, 1)
    logf = jax.nn.log_sigmoid(fg)
    flip = lambda t: jnp.flip(t, axis=2)
    q2 = jnp.stack([q, flip(q)])
    k2 = jnp.stack([k, flip(k)])
    v2 = jnp.stack([v, flip(v)])
    li2 = jnp.stack([ig[0], flip(ig[1])])
    lf2 = jnp.stack([logf[0], flip(logf[1])])
    h2 = mlstm_chunkwise(q2, k2, v2, li2, lf2)
    hsum = h2[0] + jnp.flip(h2[1], axis=2)
    mu = jnp.mean(hsum, axis=-1, keepdims=True)
    var = jnp.mean(jnp.square(hsum - mu), axis=-1, keepdims=True)
    hn = (hsum - mu) * lax.rsqrt(var + LN_EPS) * norm_w.reshape(ML_HEADS, 1, ML_HEAD_DIM)
    hn = hn.transpose(0, 2, 1, 3).reshape(bsz, s, ML_WIDTH).astype(q_pre.dtype)
    return hn * jax.nn.sigmoid(o_pre)

def conv_glu(x, w_up, conv_w, conv_b, w_down):
    u = x @ w_up
    gate, val = jnp.split(u, 2, axis=-1)
    a = jax.nn.gelu(dwconv_centred(gate, conv_w, conv_b), approximate=False)
    return (a * val) @ w_down

def setup_inputs(seed: int = 0) -> dict:
    key = jax.random.key(seed)
    ks = jax.random.split(key, 20)
    f32 = jnp.float32
    nrm = lambda k, shape, sc: jax.random.normal(k, shape, f32) * sc
    L = DEPTH
    return {
        "x": nrm(ks[0], (BATCH, SEQ, D_MODEL), 1.0),
        "w_in": nrm(ks[1], (L, D_MODEL, IN_WIDTH), D_MODEL ** -0.5),
        "na_rpb": nrm(ks[2], (L, NA_HEADS, 2 * NA_WIN_ROWS - 1, 2 * NA_WIN_COLS - 1), 0.1),
        "ml_conv_w": nrm(ks[3], (L, CONV_WIDTH, 2 * ML_WIDTH), CONV_WIDTH ** -0.5),
        "ml_conv_b": nrm(ks[4], (L, 2 * ML_WIDTH), 0.02),
        "ml_igate_b": nrm(ks[5], (L, 2 * ML_HEADS), 0.1),
        "ml_fgate_b": jnp.linspace(3.0, 6.0, 2 * ML_HEADS, dtype=f32)[None, :] + nrm(ks[6], (L, 2 * ML_HEADS), 0.1),
        "ml_norm_w": 1.0 + nrm(ks[7], (L, ML_WIDTH), 0.1),
        "w_branch_na": nrm(ks[8], (L, NA_WIDTH, D_MODEL), NA_WIDTH ** -0.5),
        "w_branch_ml": nrm(ks[9], (L, ML_WIDTH, D_MODEL), ML_WIDTH ** -0.5),
        "w_out": nrm(ks[10], (L, D_MODEL, D_MODEL), D_MODEL ** -0.5 * DEEPNORM_BETA),
        "ln1_g": 1.0 + nrm(ks[11], (L, D_MODEL), 0.1),
        "ln1_b": nrm(ks[12], (L, D_MODEL), 0.02),
        "ffn_w_up": nrm(ks[13], (L, D_MODEL, 2 * D_FF), D_MODEL ** -0.5),
        "ffn_conv_w": nrm(ks[14], (L, CONV_WIDTH, D_FF), CONV_WIDTH ** -0.5),
        "ffn_conv_b": nrm(ks[15], (L, D_FF), 0.02),
        "ffn_w_down": nrm(ks[16], (L, D_FF, D_MODEL), D_FF ** -0.5 * DEEPNORM_BETA),
        "ln2_g": 1.0 + nrm(ks[17], (L, D_MODEL), 0.1),
        "ln2_b": nrm(ks[18], (L, D_MODEL), 0.02),
    }

def reference(x, w_in, na_rpb, ml_conv_w, ml_conv_b, ml_igate_b, ml_fgate_b, ml_norm_w,
              w_branch_na, w_branch_ml, w_out, ln1_g, ln1_b, ffn_w_up, ffn_conv_w, ffn_conv_b,
              ffn_w_down, ln2_g, ln2_b):
    bsz, s, _ = x.shape
    for l in range(DEPTH):
        hproj = x @ w_in[l]
        na_qkv, ml_q, ml_k, ml_v, ml_o, ml_gates, merge_g = jnp.split(hproj, IN_SPLIT_POINTS, axis=-1)
        na_qkv = na_qkv.reshape(bsz, s, 3, NA_HEADS, NA_HEAD_DIM)
        y_na = neighborhood_attention(na_qkv[:, :, 0], na_qkv[:, :, 1], na_qkv[:, :, 2], na_rpb[l])
        y_ml = mlstm_branch(ml_q, ml_k, ml_v, ml_o, ml_gates, ml_conv_w[l], ml_conv_b[l],
                            ml_igate_b[l], ml_fgate_b[l], ml_norm_w[l])
        g_na, g_ml = jnp.split(jax.nn.sigmoid(merge_g), 2, axis=-1)
        mixed = g_na * (y_na @ w_branch_na[l]) + g_ml * (y_ml @ w_branch_ml[l])
        x = layer_norm(DEEPNORM_ALPHA * x + mixed @ w_out[l], ln1_g[l], ln1_b[l])
        f = conv_glu(x, ffn_w_up[l], ffn_conv_w[l], ffn_conv_b[l], ffn_w_down[l])
        x = layer_norm(DEEPNORM_ALPHA * x + f, ln2_g[l], ln2_b[l])
    return x


_drawn_inputs = setup_inputs


def setup_inputs(seed=0):
    import zlib

    import numpy as np

    out = dict(_drawn_inputs(seed))
    spreads = {}
    factors = {'na_rpb': 8.0,
     'ml_conv_b': 8.0,
     'ml_igate_b': 46.005,
     'ml_norm_w': 3.755,
     'ln1_b': 2.775,
     'ffn_conv_b': 8.0,
     'ln2_b': 2.856}
    for name, (base, spread) in spreads.items():
        noise = np.random.default_rng([zlib.crc32(name.encode()), seed]).standard_normal(out[name].shape)
        drawn = base * np.exp(spread * noise) if base else spread * noise
        out[name] = __import__('jax').numpy.asarray(drawn.astype(out[name].dtype))
    for name, factor in factors.items():
        out[name] = (out[name] * factor).astype(out[name].dtype)
    return out
```

```python
import math
import numpy as np
import concourse.bass as bass
from concourse import mybir
from contextlib import ExitStack

F32 = mybir.dt.float32
F32R = mybir.dt.float32r
ACT = mybir.ActivationFunctionType
ALU = mybir.AluOpType
AX = mybir.AxisListType

P = 128
S = 512
D = 2048
KB = D // P
TT = S // P
GRID_W = 64
ROWS = S // GRID_W
QCOLS = 16
KCOLS = 32
WIN_COLS = 16
STRIP = 8
NJ = GRID_W // QCOLS
KSTART = [min(max(QCOLS * j - WIN_COLS // 2, 0), GRID_W - KCOLS) for j in range(NJ)]
NA_W = 1024
NA_H = 16
ML_W = 1024
ML_H = 4
DFF = 5504
FB = DFF // P
G = 8
NG = FB // G
TAIL = FB - NG * G
RPB_R, RPB_C = 15, 31
RPB_HEAD = RPB_R * RPB_C
TABLE = 7 * RPB_C + KCOLS + WIN_COLS
PAD = 16
NEG = -1e30
EPS = 1e-5
ALPHA = 2 ** 0.25
RAW, HL = 8, 4

C_MLQ, C_MLK, C_MLV, C_MLO = 3072, 4096, 5120, 6144
C_GATE, C_MERGE = 7168, 7184

U_ML = 0
U_NA = U_ML + ML_H * 32
U_MG = U_NA + 4 * 24
U_WO = U_MG + 16 * 12
U_FF = U_WO + 4 * KB
U_TL = U_FF + NG * (8 * G + 4 * G)
U_END = U_TL + TAIL * 8 + 4 * TAIL

PAR_MLW, PAR_MLB, PAR_NW, PAR_G1, PAR_B1 = 0, 48, 64, 72, 88
PAR_FW, PAR_FB = 128, 128 + 3 * FB
PAR_OFF = (0, PAR_FW, PAR_FW + 2 * FB)


def build(nc, x, w_in, na_rpb, ml_conv_w, ml_conv_b, ml_igate_b, ml_fgate_b, ml_norm_w, w_bna, w_bml,
          w_out, ln1_g, ln1_b, w_up, ffn_conv_w, ffn_conv_b, w_down, ln2_g, ln2_b, consts, out):
    ctx = ExitStack()
    with ctx:
        K = 1024
        ARENA = 16640

        def sb(name, shape, offset, dt=F32):
            return nc.alloc_sbuf_tensor_at(name, shape, dt, offset=ARENA + int(offset))

        def sem(name):
            return ctx.enter_context(nc.semaphore(name))

        raw = sb("raw", [P, RAW, 512], 0)
        whi = sb("whi", [P, HL, 512], 16 * K, F32R)
        wlo = sb("wlo", [P, HL, 512], 24 * K, F32R)
        xt_hi = sb("xt_hi", [P, KB, S], 32 * K, F32R)
        xt_lo = sb("xt_lo", [P, KB, S], 64 * K, F32R)
        yml_hi = sb("yml_hi", [P, 8, S], 96 * K, F32R)
        yml_lo = sb("yml_lo", [P, 8, S], 112 * K, F32R)
        yna_hi = sb("yna_hi", [P, 8, S], 128 * K, F32R)
        yna_lo = sb("yna_lo", [P, 8, S], 144 * K, F32R)
        x_tok = sb("x_tok", [P, TT, D], 96 * K)
        row_a = sb("row_a", [ML_H, 2, 4, S], 128 * K)
        li = sb("li", [ML_H, 2, S], 144 * K)
        lf = sb("lf", [ML_H, 2, S], 148 * K)
        mrow = sb("mrow", [ML_H, 2, S], 152 * K)
        bl = sb("bl", [ML_H, 2, S], 156 * K)
        fx = sb("fx", [ML_H, 2, S], 160 * K)
        ex = sb("ex", [ML_H, 2, S], 164 * K)
        rrow = sb("rrow", [ML_H, 2, S], 168 * K)
        ones4 = sb("ones4", [ML_H, P], 172 * K)
        gtok = sb("gtok", [P, TT, 16], 173 * K)
        wg = sb("wg", [P, KB, 16], 174 * K)
        wg_hi = sb("wg_hi", [P, KB, 16], 175 * K, F32R)
        wg_lo = sb("wg_lo", [P, KB, 16], 176 * K, F32R)
        prow = sb("prow", [P, 3, P], 177 * K)
        wmat = sb("wmat", [P, 2, 10 * P], 128 * K)
        qt = sb("qt", [P, 2, S], 160 * K)
        kt = sb("kt", [P, 2, S], 164 * K)
        vt = sb("vt", [P, 2, S], 168 * K)
        ot = sb("ot", [P, 2, S], 172 * K)
        vtok = sb("vtok", [P, TT, 258], 176 * K)
        rbc = sb("rbc", [P, 2, S], 181 * K)
        rmask = sb("rmask", [P, 2, S], 185 * K)
        htok = sb("htok", [P, TT, 256], 189 * K)
        cv = sb("cv", [P, 2, S], 193 * K)
        sg = sb("sg", [P, 2, S], 197 * K)
        qk = sb("qk", [P, 2, S], 160 * K)
        nvt = sb("nvt", [P, 2, S], 164 * K)
        v7 = sb("v7", [P, 7, 256], 168 * K)
        table = sb("table", [P, 4, TABLE + 1], 175 * K)
        sc = sb("sc", [P, 2, NJ, 256], 180 * K)
        pt = sb("pt", [P, 2, 8, P], 188 * K)
        namask = sb("namask", [P, NJ, 256], 196 * K)
        mixed = sb("mixed", [P, KB, S], 160 * K)
        mg = sb("mg", [P, 2, S], 192 * K)
        mt = sb("mt", [P, 2, S], 196 * K)
        mx_hi = sb("mx_hi", [P, KB, S], 32 * K, F32R)
        mx_lo = sb("mx_lo", [P, KB, S], 64 * K, F32R)
        res = sb("res", [P, TT, D], 96 * K)
        ht_hi = sb("ht_hi", [P, KB, S], 128 * K, F32R)
        ht_lo = sb("ht_lo", [P, KB, S], 160 * K, F32R)
        ac_hi = sb("ac_hi", [P, G, S], 32 * K, F32R)
        ac_lo = sb("ac_lo", [P, G, S], 48 * K, F32R)
        g1b = sb("g1b", [P, D], 64 * K)
        b1b = sb("b1b", [P, D], 72 * K)
        g2b = sb("g2b", [P, D], 80 * K)
        b2b = sb("b2b", [P, D], 88 * K)
        ft = sb("ft", [P, 2, S], 192 * K)
        fg = sb("fg", [P, 2, S], 196 * K)
        ident = sb("ident", [P, P], 201 * K)
        tri = sb("tri", [P, 2, P], 201 * K + 512)
        par = sb("par", [P, 3 * P], 202 * K + 512)
        bias_s = sb("bias_s", [P, 160], 204 * K)
        st = sb("st", [P, TT, 4, 6], 204 * K + 640)
        mv = sb("mv", [P, TT, 2], 204 * K + 1024)
        rstd = sb("rstd", [P, TT], 204 * K + 1056)
        nmu = sb("nmu", [P, TT], 204 * K + 1088)
        dn = sb("dn", [P, 2], 204 * K + 1120)
        smax = sb("smax", [P, 2, NJ], 204 * K + 1152)
        ssum = sb("ssum", [P, 2, NJ], 204 * K + 1184)
        gb = sb("gb", [ML_H, 4], 204 * K + 1216)
        zpad = sb("zpad", [1, PAD], 204 * K + 1248)
        veps = sb("veps", [P, TT], 204 * K + 1312)
        rpb_pad = nc.dram_tensor("rpb_pad", [PAD + NA_H * RPB_HEAD + PAD], F32)
        rdram = nc.dram_tensor("rdram", [ML_H, 2 * S], F32)

        def blk_of(tile, n):
            return tile[:, :, :].rearrange("p k s -> p (k s)")[:, bass.ds(n * S, S)]

        def by_strip(ap):
            return ap.rearrange("p (r b e) -> p b r e", r=ROWS, e=STRIP)

        def strips(ap):
            return ap.rearrange("p (b r e) -> p b r e", r=ROWS, e=STRIP)

        ps = ctx.enter_context(nc.psum_tensor("ps", [P, 8, 512], F32))

        x_in = [sem(f"x_in{n}") for n in range(4)]
        weights_in = [sem(f"weights_in{i}") for i in range(RAW)]
        w_hi_ready, w_lo_ready, unit_used = sem("w_hi_ready"), sem("w_lo_ready"), sem("unit_used")
        names = """const_in par_in wg_in gb_in rscr_out xt_ps xt_hi_done xt_lo_done par_ps par_done wg_hi_done
            wg_lo_done gate_ps gate_tok gate_rows neg_fx exp_fx log_fx rows_a em_row cols_ps ones_set pad_out
            pad_zero r_in conv_a conv_b conv_sg free_v free_o qk_done vtr_done vtok_done rmask_done e_done
            w_done qkt_done pv_done pv_free var_done std_done hn_done yps_done y_mul yhi_done ylo_done
            na_v_done na_vt_ps na_v7 na_qk_done s_done smx_done pexp_done p_done pt_ps pt_done ypv_done yna_h
            yna_l table_in merge_sg mix_done mxhi_done mxlo_done res_in wo_free ln1_var ln1_std ln1_hn ht_ps
            ht_hi_d ht_lo_d gb_bc res_acc u_conv u_conv2 u_gelu u_mul u_hi act_done d_free ln2_var ln2_std
            ln2_hn ln2_y out_done link_x link_ml link_na link_mg link_wo link_u hn_cols link_pool link_ff
            link_y hn_rows gate_end sp_mark dve_mark""".split()
        s = {n: sem(n) for n in names}

        STARTS_AT_ONE = """w_done qk_done ylo_done vtr_done y_mul pv_done na_vt_ps mix_done qkt_done pv_free
            free_v free_o na_qk_done yna_l merge_sg wo_free d_free""".split()

        class Chain:
            def __init__(self, eng, semaphore):
                self.eng, self.sem, self.base, self.k = eng, semaphore, 0, 0

            def loop(self, base):
                self.base, self.k = base, 0

            def __call__(self, instruction):
                self.k += 1
                instruction.then_inc(self.sem, 1)
                self.eng.wait_ge(self.sem, self.base + self.k)

        block = ctx.enter_context(nc.Block())
        win = w_in[0]

        @block.sync
        def _(sp):
            def unit(src, shape, u, n, **dims):
                sp.wait_ge(w_lo_ready, u + n + 1)
                sp.sem_inc(s["sp_mark"], 1)
                dst = raw[:, n % RAW, :]
                if shape:
                    dst = dst.rearrange(shape, **dims)
                sp.dma_start(dst, src).then_inc(weights_in[n % RAW], 16)

            for n in range(4):
                sp.dma_start(x_tok[:, :, n * 512:(n + 1) * 512],
                             x[0].rearrange("(t p) c -> p t c", p=P)[:, :, n * 512:(n + 1) * 512]).then_inc(x_in[n], 16)
            wk = win.rearrange("(k p) c -> p k c", p=P)
            with sp.Fori(0, ML_H) as h:
                for c, col in enumerate((C_MLQ, C_MLK, C_MLV, C_MLO)):
                    for k in range(8):
                        unit(wk[:, 2 * k:2 * k + 2, bass.ds(h * 256 + col, 256)], "p (k c) -> p k c",
                             U_ML + h * 32, 8 * c + k, k=2)
            with sp.Fori(0, 4) as i:
                for k in range(8):
                    unit(wk[:, 2 * k:2 * k + 2, bass.ds(i * 256 + 2 * NA_W, 256)], "p (k c) -> p k c",
                         U_NA + i * 24, k, k=2)
                for pr in range(2):
                    for k in range(8):
                        unit(wk[:, 4 * (k % 4):4 * (k % 4) + 4, bass.ds(i * 256 + (pr * P + NA_W * (k // 4)), P)], "p (k c) -> p k c",
                             U_NA + i * 24, 8 + 8 * pr + k, k=4)
            wbn = w_bna[0].rearrange("(k p) c -> p k c", p=P)
            wbm = w_bml[0].rearrange("(k p) c -> p k c", p=P)
            with sp.Fori(0, KB // 2) as i:
                for half in range(2):
                    for k in range(8):
                        unit(wk[:, 4 * (k % 4):4 * (k % 4) + 4, bass.ds(i * 256 + (half * P + C_MERGE + D * (k // 4)), P)],
                             "p (k c) -> p k c", U_MG + i * 24, 12 * half + k, k=4)
                    for k in range(4):
                        w = (wbn, wbm)[k // 2]
                        unit(w[:, 4 * (k % 2):4 * (k % 2) + 4, bass.ds(i * 256 + half * P, P)], "p (k c) -> p k c",
                             U_MG + i * 24, 12 * half + 8 + k, k=4)
            with sp.Fori(0, 2) as i:
                for half in range(2):
                    for k in range(KB):
                        unit(w_out[0][k * P:(k + 1) * P, bass.ds(i * 1024 + half * 512, 512)], None,
                             U_WO + i * 32, 16 * half + k)
            wup = w_up[0].rearrange("(k p) c -> p k c", p=P)
            with sp.Fori(0, NG) as g:
                with sp.Fori(0, 2) as i:
                    for c in range(4):
                        for k in range(8):
                            unit(wup[:, 4 * (k % 4):4 * (k % 4) + 4, bass.ds(g * (G * P) + i * 512 + (c * P + DFF * (k // 4)), P)],
                                 "p (k c) -> p k c", U_FF + g * 96 + i * 32, 8 * c + k, k=4)
                with sp.Fori(0, 2) as i:
                    for half in range(2):
                        for k in range(G):
                            unit(w_down[0][bass.ds(g * (G * P) + k * P, P), bass.ds(i * 1024 + half * 512, 512)],
                                 None, U_FF + g * 96 + 64 + i * 16, 8 * half + k)
            for c in range(TAIL):
                for k in range(8):
                    j = NG * G + c
                    first = j * P + DFF * (k // 4)
                    unit(wup[:, 4 * (k % 4):4 * (k % 4) + 4, first:first + P], "p (k c) -> p k c", U_TL, 8 * c + k, k=4)
            for n in range(4):
                for k in range(TAIL):
                    j = NG * G + k
                    unit(w_down[0][j * P:(j + 1) * P, n * 512:(n + 1) * 512], None, U_TL, 8 * TAIL + n * TAIL + k)
            for t in range(TT):
                sp.wait_ge(s["ln2_y"], t + 1)
                sp.dma_start(out[0, t * P:(t + 1) * P, :], res[:, t, :]).then_inc(s["out_done"], 16)
            sp.wait_ge(s["out_done"], 16 * TT)

        @block.gpsimd
        def _(pool):
            pool.sem_inc(w_lo_ready, RAW)
            pool.sem_inc(unit_used, HL)
            for n in STARTS_AT_ONE + ["wo_free", "d_free"]:
                pool.sem_inc(s[n], 1)
            pool.sem_inc(s["u_mul"], 4)
            pool.sem_inc(s["act_done"], 2)
            pool.dma_start(ident[:, :], consts[:, 0:P]).then_inc(s["const_in"], 16)
            pool.dma_start(tri[:, :, :], consts[:, P:3 * P].rearrange("p (d c) -> p d c", d=2)).then_inc(s["const_in"], 16)
            pool.dma_start(wg[:, :, :], win[:, C_GATE:C_GATE + 16].rearrange("(k p) c -> p k c", p=P)).then_inc(s["wg_in"], 16)
            loads = [(0, PAR_MLW, ml_conv_w[0].rearrange("w (b p) -> w b p", p=P), 3, 16),
                     (0, PAR_MLB, ml_conv_b[0].rearrange("(b p) -> b p", p=P), 0, 16),
                     (0, PAR_NW, ml_norm_w[0].rearrange("(b p) -> b p", p=P), 0, 8),
                     (0, PAR_G1, ln1_g[0].rearrange("(b p) -> b p", p=P), 0, 16),
                     (0, PAR_B1, ln1_b[0].rearrange("(b p) -> b p", p=P), 0, 16),
                     (1, 0, ffn_conv_w[0].rearrange("w (b p) -> w b p", p=P)[0:2], 2, FB),
                     (2, 0, ffn_conv_w[0].rearrange("w (b p) -> w b p", p=P)[2:3], 1, FB),
                     (2, FB, ffn_conv_b[0].rearrange("(b p) -> b p", p=P), 0, FB)]
            for tile, r0, src, w, nb in loads:
                for i in range(max(w, 1)):
                    pool.dma_start(prow[r0 + i * nb:r0 + (i + 1) * nb, tile, :], src[i] if w else src).then_inc(s["par_in"], 16)
            for n, b in enumerate((ml_igate_b, ml_fgate_b)):
                for d in range(2):
                    pool.dma_start(gb[:, 2 * n + d:2 * n + d + 1],
                                   b[0, 4 * d:4 * d + 4].rearrange("(h o) -> h o", o=1)).then_inc(s["gb_in"], 16)
            pool.memset(zpad[:, :], 0.0).then_inc(s["pad_zero"], 1)
            pool.wait_ge(s["pad_zero"], 1)
            rp = rpb_pad.ap()
            end = PAD + NA_H * RPB_HEAD
            pool.dma_start(rp[0:PAD].rearrange("(o n) -> o n", o=1), zpad[:, :]).then_inc(s["pad_out"], 16)
            pool.dma_start(rp[end:end + PAD].rearrange("(o n) -> o n", o=1), zpad[:, :]).then_inc(s["pad_out"], 16)
            pool.dma_start(rp[PAD:end].rearrange("(h n) -> h n", h=NA_H),
                           na_rpb[0].rearrange("h r c -> h (r c)")).then_inc(s["pad_out"], 16)
            pool.memset(ones4[:, :], 1.0).then_inc(s["ones_set"], 1)
            pool.wait_ge(s["rows_a"], 1)
            pool.dma_start(rdram.ap().rearrange("h (d s) -> h d s", d=2), rrow[:, :, :]).then_inc(s["rscr_out"], 16)
            pool.wait_ge(s["rscr_out"], 16)
            pool.wait_ge(s["gate_end"], 1)
            with pool.Fori(0, ML_H) as h:
                pool.wait_ge(s["w_done"], h * 4 + 1)
                src = bass.AP(rdram, h * (2 * S), [[0, P], [1, 2 * S]])
                pool.dma_start(rbc[:, :, :].rearrange("p d s -> p (d s)"), src).then_inc(s["r_in"], 16)
            pool.wait_ge(s["pad_out"], 48)
            pool.wait_ge(s["ylo_done"], 8 + 1)
            pool.dma_start(namask[:, :, :], consts[:, 3 * P:3 * P + NJ * 256].rearrange("p (j c) -> p j c", j=NJ)).then_inc(s["const_in"], 16)
            for i in range(4):
                if i:
                    pool.wait_ge(s["smx_done"], 4 * i)
                for b in range(2):
                    for qr in range(ROWS):
                        p0 = (b * ROWS + qr) * STRIP
                        first = PAD + 4 * i * RPB_HEAD + (7 - qr) * RPB_C - STRIP * b - STRIP
                        pool.dma_start(table[p0:p0 + STRIP, :, 0:TABLE],
                                       bass.AP(rpb_pad, first, [[1, STRIP], [RPB_HEAD, 4], [1, TABLE]])).then_inc(s["table_in"], 16)
            pool.wait_ge(unit_used, U_WO + HL)
            pool.dma_start(res[:, :, :], x[0].rearrange("(t p) c -> p t c", p=P)).then_inc(s["res_in"], 16)
            pool.wait_ge(unit_used, U_FF + HL)
            for tile, src in ((g1b, ln1_g), (b1b, ln1_b), (g2b, ln2_g), (b2b, ln2_b)):
                pool.dma_start(tile[:, :], bass.AP(src.tensor, 0, [[0, P], [1, D]])).then_inc(s["gb_bc"], 16)
            pool.wait_ge(s["gb_bc"], 64)
            link = Chain(pool, s["link_pool"])
            link(nc.gpsimd.tensor_scalar(g1b[:, :], g1b[:, :], ALPHA, None, ALU.mult))
            link(nc.gpsimd.tensor_scalar(b1b[:, :], b1b[:, :], ALPHA, None, ALU.mult))
            pool.wait_ge(s["ht_ps"], KB)
            for t in range(TT):
                link(nc.gpsimd.tensor_tensor(res[:, t, :], res[:, t, :], g1b[:, :], ALU.mult))
                nc.gpsimd.tensor_tensor(res[:, t, :], res[:, t, :], b1b[:, :], ALU.add).then_inc(s["res_acc"], 1)

        @block.scalar
        def _(act):
            def hi(ub, u8, k):
                if isinstance(ub, int) and ub + k >= U_END:
                    return
                act.wait_ge(weights_in[k % RAW], (u8 + k // RAW + 1) * 16)
                act.wait_ge(unit_used, ub + k + 1)
                nc.scalar.activation(whi[:, k % HL, :], raw[:, k % RAW, :], ACT.Copy).then_inc(w_hi_ready, 1)

            for kb in range(KB):
                act.wait_ge(s["xt_ps"], kb + 1)
                nc.scalar.activation(xt_hi[:, kb, :], ps[:, kb % 8, :], ACT.Copy).then_inc(s["xt_hi_done"], 1)
            for k in range(HL):
                hi(U_ML, U_ML // 8, k)
            act.wait_ge(s["wg_in"], 16)
            nc.scalar.activation(wg_hi[:, :, :], wg[:, :, :], ACT.Copy).then_inc(s["wg_hi_done"], 1)
            act.wait_ge(s["gate_ps"], 1)
            nc.scalar.activation(gtok[:, :, :], ps[:, 0, 0:TT * 16].rearrange("p (t c) -> p t c", t=TT), ACT.Copy).then_inc(s["gate_tok"], 1)
            act.wait_ge(s["neg_fx"], 1)
            nc.scalar.activation(ex[:, :, :], ex[:, :, :], ACT.Exp).then_inc(s["exp_fx"], 1)
            act.wait_ge(s["exp_fx"], 1)
            nc.scalar.activation(ex[:, :, :], ex[:, :, :], ACT.Ln, bias=1.0).then_inc(s["log_fx"], 1)
            act.wait_ge(s["rows_a"], 1)
            nc.scalar.activation(ex[:, :, :], mrow[:, :, :], ACT.Exp, scale=-1.0).then_inc(s["em_row"], 1)

            with act.Fori(0, ML_H) as h:
                ub, u8 = h * 32 + U_ML, h * 4 + U_ML // 8

                def chunk(c):
                    for k in range(8):
                        hi(ub, u8, 8 * c + k + HL)
                    act.wait_ge(unit_used, ub + 8 * (c + 1) + HL)

                for c in range(2):
                    chunk(c)
                    for b in range(2):
                        blk = h * 2 + (8 * c + b)
                        act.wait_ge(s["qk_done"], h * 4 + (1 + b if c else 0) + 1)
                        act.wait_ge(s["ylo_done"], h * 2 + 1)
                        nc.scalar.activation(cv[:, b, :], ps[:, 2 * c + b, :], ACT.Identity,
                                             scale=par[:, bass.ds(blk + (PAR_MLW + 16), 1)],
                                             bias=par[:, bass.ds(blk + PAR_MLB, 1)]).then_inc(s["conv_a"], 1)
                        act.wait_ge(s["conv_b"], h * 4 + (2 * c + b + 1))
                        nc.scalar.activation(sg[:, b, :], cv[:, b, :], ACT.Sigmoid).then_inc(s["conv_sg"], 1)
                chunk(2)
                act.wait_ge(s["vtr_done"], h + 1)
                nc.scalar.activation(vt[:, :, :], ps[:, 0:2, :], ACT.Copy).then_inc(s["free_v"], 1)
                chunk(3)
                act.wait_ge(s["y_mul"], h * 2 + 1)
                nc.scalar.activation(ot[:, :, :], ps[:, 2:4, :], ACT.Sigmoid).then_inc(s["free_o"], 1)
                act.wait_ge(s["vtr_done"], h + 1 + 1)
                act.wait_ge(s["pv_done"], h * 4 + 1)
                nc.scalar.activation(vtok[:, :, 0:256], ps[:, 4:6, :].rearrange("p b (t c) -> p (b t) c", t=2),
                                     ACT.Copy).then_inc(s["vtok_done"], 1)
                act.wait_ge(s["rmask_done"], h + 1)
                for c in range(4):
                    fo = (0, 4, 7, 9)[c]
                    bo = (0, 1, 3, 6)[c]
                    work = [(0, c, 0, fo)] + [(0, tc, tc - c, fo + tc - c) for tc in range(c + 1, 4)] \
                        + [(1, tc, c - tc, bo + tc) for tc in range(c)] + [(1, c, 0, bo + c)]
                    for n, (d, tc, dist, slot) in enumerate(work):
                        src = rmask if dist == 0 else rbc
                        e = nc.scalar.activation(wmat[:, d, slot * P:(slot + 1) * P], src[:, d, tc * P:(tc + 1) * P], ACT.Exp,
                                                 bias=bias_s[:, bass.ds(h + ((d * 4 + c) * 4 + dist) * 4, 1)])
                        if n == len(work) - 1:
                            e.then_inc(s["e_done"], 1)
                act.wait_ge(s["var_done"], h + 1)
                nc.scalar.activation(rstd[:, :], veps[:, :], ACT.Sqrt).then_inc(s["std_done"], 1)
                for b in range(2):
                    act.wait_ge(s["y_mul"], h * 2 + (b + 1) + 1)
                    nc.scalar.activation(blk_of(yml_hi, h * 2 + b), cv[:, b, :], ACT.Copy).then_inc(s["yhi_done"], 1)

            with act.Fori(0, 4) as i:
                ub, u8 = i * 24 + U_NA, i * 3 + U_NA // 8
                for k in range(8):
                    hi(ub, u8, k + HL)
                act.wait_ge(unit_used, ub + 8 + HL)
                act.wait_ge(s["na_vt_ps"], i + 1)
                for b in range(2):
                    e = nc.scalar.activation(strips(nvt[:, b, :]), by_strip(ps[:, b, :]), ACT.Copy)
                e.then_inc(s["na_v_done"], 1)
                act.wait_ge(s["na_vt_ps"], i + 1 + 1)
                nc.scalar.activation(v7[:, :, :].rearrange("p i c -> p (i c)"),
                                     ps[:, 4:8, :].rearrange("p b c -> p (b c)")[:, 0:7 * 256], ACT.Copy).then_inc(s["na_v7"], 1)
                for pr in range(2):
                    for k in range(8):
                        hi(ub, u8, 8 + 8 * pr + k + HL)
                    b0 = (2, 0)[pr]
                    act.wait_ge(unit_used, ub + 8 * (pr + 2) + HL)
                    nc.scalar.activation(strips(qk[:, 0, :]), by_strip(ps[:, b0, :])[:, :, :, ::-1], ACT.Copy, scale=0.125)
                    nc.scalar.activation(strips(qk[:, 1, :]), by_strip(ps[:, b0 + 1, :]), ACT.Copy).then_inc(s["na_qk_done"], 1)
                    for hh in range(2):
                        act.wait_ge(s["smx_done"], i * 4 + (2 * pr + hh + 1))
                        for j in range(NJ):
                            e = nc.scalar.activation(sc[:, hh, j, :], sc[:, hh, j, :], ACT.Exp, bias=smax[:, hh, j:j + 1],
                                                     accum_out=ssum[:, hh, j:j + 1])
                        e.then_inc(s["pexp_done"], 1)
                    for hh in range(2):
                        act.wait_ge(s["pt_ps"], i * 4 + (2 * pr + hh + 1))
                        nc.scalar.activation(pt[:, hh, :, :].rearrange("p a b -> p (a b)"),
                                             ps[:, 4 + 2 * hh:6 + 2 * hh, :].rearrange("p a b -> p (a b)"), ACT.Copy).then_inc(s["pt_done"], 1)
                    act.wait_ge(s["ypv_done"], i * 2 + (pr + 1))
                    nc.scalar.activation(
                        by_strip(blk_of(yna_hi, i * 2 + pr)), strips(ps[:, 4, :])[:, :, :, ::-1], ACT.Copy).then_inc(s["yna_h"], 1)

            with act.Fori(0, KB // 2) as i:
                ub, u8 = i * 24 + U_MG, i * 3 + U_MG // 8
                for half in range(2):
                    for k in range(8):
                        hi(ub, u8, 12 * half + k + HL)
                    act.wait_ge(unit_used, ub + 12 * half + 8 + HL)
                    act.wait_ge(s["mix_done"], i * 2 + half + 1)
                    nc.scalar.activation(mg[:, :, :], ps[:, 0:2, :], ACT.Sigmoid).then_inc(s["merge_sg"], 1)
                    for k in range(8, 12):
                        hi(ub, u8, 12 * half + k + HL)
            for kb in range(KB):
                act.wait_ge(s["mix_done"], KB + 1)
                act.wait_ge(unit_used, U_WO + HL)
                nc.scalar.activation(mx_hi[:, kb, :], mixed[:, kb, :], ACT.Copy).then_inc(s["mxhi_done"], 1)
            with act.Fori(0, 2) as i:
                for k in range(32):
                    hi(i * 32 + U_WO, i * 4 + U_WO // 8, k + HL)
            act.wait_ge(s["ln1_var"], 1)
            nc.scalar.activation(rstd[:, :], veps[:, :], ACT.Sqrt).then_inc(s["ln1_std"], 1)
            for n in range(4):
                act.wait_ge(s["ln1_hn"], 1)
                for t in range(TT):
                    e = nc.scalar.activation(res[:, t, n * 512:(n + 1) * 512], res[:, t, n * 512:(n + 1) * 512], ACT.Identity,
                                             scale=rstd[:, t:t + 1], bias=nmu[:, t:t + 1])
                e.then_inc(s["hn_cols"], 1)
            for kb in range(KB):
                act.wait_ge(s["ht_ps"], kb + 1)
                nc.scalar.activation(ht_hi[:, kb, :], ps[:, 4 + kb % 4, :], ACT.Identity,
                                     scale=par[:, PAR_G1 + kb:PAR_G1 + kb + 1],
                                     bias=par[:, PAR_B1 + kb:PAR_B1 + kb + 1]).then_inc(s["ht_hi_d"], 1)

            def ffn_block(n, c, par_w, par_b, slot):
                act.wait_ge(s["act_done"], n + 1)
                nc.scalar.activation(ft[:, c % 2, :], ps[:, 2 * c, :], ACT.Identity, scale=par_w, bias=par_b).then_inc(s["u_conv"], 1)
                act.wait_ge(s["u_conv2"], n + 1)
                nc.scalar.activation(fg[:, c % 2, :], ft[:, c % 2, :], ACT.Gelu).then_inc(s["u_gelu"], 1)
                act.wait_ge(s["u_mul"], n + 5)
                nc.scalar.activation(blk_of(ac_hi, slot), ft[:, c % 2, :], ACT.Copy).then_inc(s["u_hi"], 1)

            with act.Fori(0, NG) as g:
                with act.Fori(0, 2) as i:
                    for c in range(4):
                        for k in range(8):
                            hi(g * 96 + i * 32 + U_FF, g * 12 + i * 4 + U_FF // 8, 8 * c + k + HL)
                        blk = g * 8 + i * 4 + c
                        act.wait_ge(unit_used, g * 96 + i * 32 + (U_FF + 8 * (c + 1) + HL))
                        ffn_block(blk, c, par[:, bass.ds(blk + (PAR_FW + FB), 1)], par[:, bass.ds(blk + PAR_FB, 1)],
                                  i * 4 + c)
                with act.Fori(0, 2) as i:
                    for k in range(16):
                        hi(g * 96 + i * 16 + (U_FF + 64), g * 12 + i * 2 + (U_FF + 64) // 8, k + HL)
            for c in range(TAIL):
                for k in range(8):
                    hi(U_TL, U_TL // 8, 8 * c + k + HL)
                blk = NG * G + c
                act.wait_ge(unit_used, U_TL + 8 * (c + 1) + HL)
                ffn_block(blk, c, par[:, PAR_FW + FB + blk:PAR_FW + FB + blk + 1], par[:, PAR_FB + blk:PAR_FB + blk + 1],
                          c)
            for k in range(4 * TAIL):
                hi(U_TL, U_TL // 8, 8 * TAIL + k + HL)
            act.wait_ge(s["ln2_var"], 1)
            nc.scalar.activation(rstd[:, :], veps[:, :], ACT.Sqrt).then_inc(s["ln2_std"], 1)
            act.wait_ge(s["ln2_hn"], 1)
            for t in range(TT):
                nc.scalar.activation(res[:, t, :], res[:, t, :], ACT.Identity, scale=rstd[:, t:t + 1],
                                     bias=nmu[:, t:t + 1]).then_inc(s["hn_rows"], 1)

        @block.vector
        def _(dve):
            def lo(ub, k):
                if isinstance(ub, int) and ub + k >= U_END:
                    return
                dve.wait_ge(w_hi_ready, ub + k + 1)
                nc.vector.tensor_tensor(wlo[:, k % HL, :], raw[:, k % RAW, :], whi[:, k % HL, :].bitcast(F32),
                                        ALU.subtract).then_inc(w_lo_ready, 1)

            for kb in range(KB):
                dve.wait_ge(s["xt_hi_done"], kb + 1)
                nc.vector.tensor_tensor(xt_lo[:, kb, :], ps[:, kb % 8, :], xt_hi[:, kb, :].bitcast(F32),
                                        ALU.subtract).then_inc(s["xt_lo_done"], 1)
            for k in range(HL):
                lo(U_ML, k)
            dve.wait_ge(s["wg_hi_done"], 1)
            nc.vector.tensor_tensor(wg_lo[:, :, :], wg[:, :, :], wg_hi[:, :, :].bitcast(F32), ALU.subtract).then_inc(s["wg_lo_done"], 1)
            dve.wait_ge(s["par_ps"], 1)
            for i, w in enumerate((PAR_B1 + 16, 2 * FB, 2 * FB)):
                nc.vector.tensor_copy(par[:, PAR_OFF[i]:PAR_OFF[i] + w], ps[:, 7, i * P:i * P + w]).then_inc(s["par_done"], 1)
            link = Chain(dve, s["link_x"])
            link(nc.vector.memset(row_a[:, :, :, :], 0.0))
            dve.wait_ge(s["gb_in"], 64)
            dve.wait_ge(s["ones_set"], 1)
            dve.wait_ge(s["gate_rows"], 1)
            for d in range(2):
                nc.vector.tensor_scalar(li[:, d, :], ps[0:ML_H, 1 + d, :], gb[:, d:d + 1], None, ALU.add)
                link(nc.vector.tensor_scalar(fx[:, d, :], ps[0:ML_H, 3 + d, :], gb[:, 2 + d:3 + d], None, ALU.add))
            nc.vector.scalar_tensor_tensor(ex[:, :, :], fx[:, :, :], -1.0, fx[:, :, :], ALU.mult, ALU.min).then_inc(s["neg_fx"], 1)
            dve.wait_ge(s["log_fx"], 1)
            link(nc.vector.scalar_tensor_tensor(lf[:, :, :].rearrange("p d s -> p (d s)"), fx[:, :, :].rearrange("p d s -> p (d s)"),
                                                0.0, ex[:, :, :].rearrange("p d s -> p (d s)"), ALU.min, ALU.subtract))

            def way(ap, d):
                return ap if d == 0 else ap[:, ::-1]

            for d in range(2):
                nc.vector.tensor_tensor_scan(way(mrow[:, d, :], d), way(lf[:, d, :], d), way(li[:, d, :], d), NEG, ALU.add, ALU.max)
                for c in range(4):
                    cs = slice(c * P, (c + 1) * P)
                    ins = nc.vector.tensor_tensor_scan(way(bl[:, d, cs], d), ones4[:, :], way(lf[:, d, cs], d), 0.0, ALU.mult, ALU.add)
                link(ins)
                link(nc.vector.tensor_tensor(row_a[:, d, 0, :], li[:, d, :], bl[:, d, :], ALU.subtract))
                for dist in range(1, 4):
                    for c in range(4):
                        tc = c + dist if d == 0 else c - dist
                        if not 0 <= tc < 4:
                            continue
                        mid = tc - 1 if d == 0 else tc + 1
                        at = mid * P + P - 1 if d == 0 else mid * P
                        cs = slice(c * P, (c + 1) * P)
                        ins = nc.vector.tensor_scalar(row_a[:, d, dist, cs], row_a[:, d, dist - 1, cs], bl[:, d, at:at + 1], None, ALU.add)
                    link(ins)
            for d in range(2):
                ins = nc.vector.tensor_tensor(rrow[:, d, :], bl[:, d, :], mrow[:, d, :], ALU.subtract)
            ins.then_inc(s["rows_a"], 1)
            dve.wait_ge(s["cols_ps"], 1)
            link(nc.vector.tensor_copy(bias_s[:, :], ps[:, 5, 0:160]))
            dve.wait_ge(s["rscr_out"], 16)
            nc.vector.memset(vtok[:, :, 256:257], 1.0).then_inc(s["gate_end"], 1)

            link = Chain(dve, s["link_ml"])
            ML_LINKS = 4 + 4 * 5 + 2
            with dve.Fori(0, ML_H) as h:
                link.loop(h * ML_LINKS)
                ub = h * 32 + U_ML
                for c in range(2):
                    for k in range(8):
                        lo(ub, 8 * c + k + HL)
                    for b in range(2):
                        blk = h * 2 + (8 * c + b)
                        pb = ps[:, 2 * c + b, :]
                        dve.wait_ge(s["conv_a"], h * 4 + (2 * c + b + 1))
                        link(nc.vector.scalar_tensor_tensor(cv[:, b, 1:S], pb[:, 0:S - 1], par[:, bass.ds(blk + PAR_MLW, 1)],
                                                            cv[:, b, 1:S], ALU.mult, ALU.add))
                        nc.vector.scalar_tensor_tensor(cv[:, b, 0:S - 1], pb[:, 1:S], par[:, bass.ds(blk + (PAR_MLW + 32), 1)],
                                                       cv[:, b, 0:S - 1], ALU.mult, ALU.add).then_inc(s["conv_b"], 1)
                        dve.wait_ge(s["conv_sg"], h * 4 + (2 * c + b + 1))
                        if b == 0:
                            dve.wait_ge(s["qkt_done"], h * 4 + 1)
                        nc.vector.scalar_tensor_tensor((qt, kt)[c][:, b, :], cv[:, b, :], (1.0, 256 ** -0.5)[c], sg[:, b, :],
                                                       ALU.mult, ALU.mult).then_inc(s["qk_done"], 1)
                for c in range(2, 4):
                    for k in range(8):
                        lo(ub, 8 * c + k + HL)
                dve.wait_ge(s["r_in"], (h + 1) * 16)
                for d in range(2):
                    ins = nc.vector.tensor_tensor(rmask[:, d, :].rearrange("p (c t) -> p c t", c=4),
                                                  rbc[:, d, :].rearrange("p (c t) -> p c t", c=4),
                                                  tri[:, d:d + 1, :].to_broadcast([P, 4, P]), ALU.add)
                ins.then_inc(s["rmask_done"], 1)
                for c in range(4):
                    dve.wait_ge(s["e_done"], h * 4 + (c + 1))
                    dve.wait_ge(s["qkt_done"], h * 4 + (c + 1) + 1)
                    pb = ps[:, 6 + c % 2, :]
                    fo = (0, 4, 7, 9)[c] * P
                    bo = (0, 1, 3, 6)[c] * P
                    wf = wmat[:, 0, fo:fo + (4 - c) * P]
                    wb = wmat[:, 1, bo:bo + (c + 1) * P]
                    nc.vector.tensor_tensor(wf, pb[:, c * P:S], wf, ALU.mult)
                    nc.vector.tensor_tensor(wb, pb[:, 0:(c + 1) * P], wb, ALU.mult).then_inc(s["w_done"], 1)
                for tc in range(4):
                    dve.wait_ge(s["pv_done"], h * 4 + (tc + 1) + 1)
                    b0 = 4 + 2 * (tc % 2)
                    den = ps[:, b0:b0 + 2, 256:257].rearrange("p d o -> p (d o)")
                    em = bias_s[:, 128:160].rearrange("p (d t h) -> p d t h", d=2, t=4)[:, :, tc, bass.ds(h, 1)].rearrange("p d o -> p (d o)")
                    link(nc.vector.scalar_tensor_tensor(dn[:, :], den, -1.0, em, ALU.mult, ALU.max))
                    link(nc.vector.tensor_tensor(dn[:, :], dn[:, :], den, ALU.max))
                    link(nc.vector.reciprocal(dn[:, :], dn[:, :]))
                    link(nc.vector.tensor_scalar(htok[:, tc, :], ps[:, b0, 0:256], dn[:, 0:1], None, ALU.mult))
                    nc.vector.scalar_tensor_tensor(htok[:, tc, :], ps[:, b0 + 1, 0:256], dn[:, 1:2], htok[:, tc, :],
                                                   ALU.mult, ALU.add).then_inc(s["pv_free"], 1)
                    dve.wait_ge(s["pv_free"], h * 4 + (tc + 1) + 1)
                    link(nc.vector.bn_stats(st[:, tc, 0, :], htok[:, tc, :]))
                dve.sem_inc(s["dve_mark"], 1)
                for tc in range(4):
                    ins = nc.vector.bn_aggr(mv[:, tc, :], st[:, tc, 0, :])
                link(ins)
                nc.vector.tensor_scalar(veps[:, :], mv[:, :, 1], EPS, None, ALU.add).then_inc(s["var_done"], 1)
                dve.wait_ge(s["std_done"], h + 1)
                link(nc.vector.reciprocal(rstd[:, :], rstd[:, :]))
                for tc in range(4):
                    ins = nc.vector.tensor_scalar(htok[:, tc, :], htok[:, tc, :], mv[:, tc, 0:1], rstd[:, tc:tc + 1],
                                                  ALU.subtract, ALU.mult)
                ins.then_inc(s["hn_done"], 1)
                for b in range(2):
                    dve.wait_ge(s["yps_done"], h * 2 + (b + 1))
                    nc.vector.scalar_tensor_tensor(cv[:, b, :], ps[:, 4 + b, :], par[:, bass.ds(h * 2 + (PAR_NW + b), 1)], ot[:, b, :],
                                                   ALU.mult, ALU.mult).then_inc(s["y_mul"], 1)
                for b in range(2):
                    dve.wait_ge(s["yhi_done"], h * 2 + (b + 1))
                    at = h * 2 + b
                    nc.vector.tensor_tensor(blk_of(yml_lo, at), cv[:, b, :], blk_of(yml_hi, at).bitcast(F32),
                                            ALU.subtract).then_inc(s["ylo_done"], 1)
            assert link.k == ML_LINKS

            link = Chain(dve, s["link_na"])
            NA_LINKS = 2 * 2 * 4
            dve.wait_ge(s["const_in"], 48)
            with dve.Fori(0, 4) as i:
                link.loop(i * NA_LINKS)
                ub = i * 24 + U_NA
                for k in range(8):
                    lo(ub, k + HL)
                for pr in range(2):
                    for k in range(8):
                        lo(ub, 8 + 8 * pr + k + HL)
                    if pr == 0:
                        dve.wait_ge(s["table_in"], (i + 1) * (16 * 2 * ROWS))
                    for hh in range(2):
                        dve.wait_ge(s["s_done"], i * 4 + (2 * pr + hh + 1))
                        for j in range(NJ):
                            shift = KSTART[j] - QCOLS * j + WIN_COLS
                            head = table[:, 2 * pr + hh, shift:shift + 1]
                            bias = bass.AP(head.tensor, head.offset, [list(head.ap[0]), [STRIP, 4], [RPB_C, ROWS], [1, STRIP]])
                            ins = nc.vector.tensor_tensor(strips(sc[:, hh, j, :]),
                                                          strips(ps[:, 4 + 2 * hh + j // 2, (j % 2) * 256:(j % 2) * 256 + 256]),
                                                          bias, ALU.add)
                        link(ins)
                        link(nc.vector.tensor_tensor(sc[:, hh, :, :], sc[:, hh, :, :], namask[:, :, :], ALU.min))
                        link(nc.vector.reduce_max(smax[:, hh, :], sc[:, hh, :, :], AX.X))
                        nc.vector.tensor_scalar(smax[:, hh, :], smax[:, hh, :], -1.0, None, ALU.mult).then_inc(s["smx_done"], 1)
                    for hh in range(2):
                        dve.wait_ge(s["pexp_done"], i * 4 + (2 * pr + hh + 1))
                        link(nc.vector.reciprocal(ssum[:, hh, :], ssum[:, hh, :]))
                        for j in range(NJ):
                            ins = nc.vector.tensor_scalar(sc[:, hh, j, :], sc[:, hh, j, :], ssum[:, hh, j:j + 1], None, ALU.mult)
                        ins.then_inc(s["p_done"], 1)
                    dve.wait_ge(s["yna_h"], i * 2 + (pr + 1))
                    at = i * 2 + pr
                    nc.vector.tensor_tensor(
                        by_strip(blk_of(yna_lo, at)), strips(ps[:, 4, :])[:, :, :, ::-1], by_strip(blk_of(yna_hi, at).bitcast(F32)),
                        ALU.subtract).then_inc(s["yna_l"], 1)
            assert link.k == NA_LINKS

            link = Chain(dve, s["link_mg"])
            with dve.Fori(0, KB // 2) as i:
                link.loop(i * 2)
                ub = i * 24 + U_MG
                for half in range(2):
                    for k in range(12):
                        lo(ub, 12 * half + k + HL)
                    dve.wait_ge(unit_used, ub + 12 * (half + 1) + HL)
                    dve.wait_ge(s["merge_sg"], i * 2 + (half + 1) + 1)
                    nc.vector.tensor_tensor(mt[:, 0, :], ps[:, 2, :], mg[:, 0, :], ALU.mult)
                    link(nc.vector.tensor_tensor(mt[:, 1, :], ps[:, 3, :], mg[:, 1, :], ALU.mult))
                    nc.vector.tensor_tensor(blk_of(mixed, i * 2 + half), mt[:, 0, :], mt[:, 1, :],
                                            ALU.add).then_inc(s["mix_done"], 1)
            for kb in range(KB):
                dve.wait_ge(s["mxhi_done"], kb + 1)
                nc.vector.tensor_tensor(mx_lo[:, kb, :], mixed[:, kb, :], mx_hi[:, kb, :].bitcast(F32),
                                        ALU.subtract).then_inc(s["mxlo_done"], 1)

            dve.wait_ge(s["res_in"], 16)
            link = Chain(dve, s["link_wo"])
            with dve.Fori(0, 2) as i:
                link.loop(i * 2)
                for half in range(2):
                    for k in range(KB):
                        lo(i * 32 + U_WO, 16 * half + k + HL)
                    dve.wait_ge(unit_used, i * 32 + (U_WO + 16 * (half + 1) + HL))
                    for t in range(TT):
                        at = bass.ds(i * 1024 + half * 512, 512)
                        ins = nc.vector.scalar_tensor_tensor(res[:, t, at], res[:, t, at], ALPHA, ps[:, 4 - 4 * half + t, :],
                                                             ALU.mult, ALU.add)
                    ins.then_inc(s["wo_free"], 1)
                    dve.wait_ge(s["wo_free"], i * 2 + (half + 2) + 1)
                    for t in range(TT):
                        ins = nc.vector.bn_stats(st[:, t, :, :].rearrange("p n c -> p (n c)")[:, bass.ds(i * 12 + half * 6, 6)], res[:, t, at])
                    link(ins)
            link = Chain(dve, s["link_ff"])

            def norm_stats(var, std, ready):
                for t in range(TT):
                    ins = nc.vector.bn_aggr(mv[:, t, :], st[:, t, :, :].rearrange("p a b -> p (a b)"))
                link(ins)
                nc.vector.tensor_scalar(veps[:, :], mv[:, :, 1], EPS, None, ALU.add).then_inc(var, 1)
                dve.wait_ge(std, 1)
                link(nc.vector.reciprocal(rstd[:, :], rstd[:, :]))
                nc.vector.scalar_tensor_tensor(nmu[:, :], mv[:, :, 0], -1.0, rstd[:, :], ALU.mult, ALU.mult).then_inc(ready, 1)

            norm_stats(s["ln1_var"], s["ln1_std"], s["ln1_hn"])
            for kb in range(KB):
                dve.wait_ge(s["ht_hi_d"], kb + 1)
                f = ft[:, kb % 2, :]
                link(nc.vector.tensor_scalar(f, ps[:, 4 + kb % 4, :], par[:, PAR_G1 + kb:PAR_G1 + kb + 1],
                                             par[:, PAR_B1 + kb:PAR_B1 + kb + 1], ALU.mult, ALU.add))
                nc.vector.tensor_tensor(ht_lo[:, kb, :], f, ht_hi[:, kb, :].bitcast(F32), ALU.subtract).then_inc(s["ht_lo_d"], 1)

            link = Chain(dve, s["link_u"])

            def ffn_block(n, c, w0, w2, slot):
                f, pg = ft[:, c % 2, :], ps[:, 2 * c, :]
                dve.wait_ge(s["u_conv"], n + 1)
                link(nc.vector.scalar_tensor_tensor(f[:, 1:S], pg[:, 0:S - 1], w0, f[:, 1:S], ALU.mult, ALU.add))
                nc.vector.scalar_tensor_tensor(f[:, 0:S - 1], pg[:, 1:S], w2, f[:, 0:S - 1], ALU.mult, ALU.add).then_inc(s["u_conv2"], 1)
                dve.wait_ge(s["u_gelu"], n + 1)
                nc.vector.tensor_tensor(f, ps[:, 2 * c + 1, :], fg[:, c % 2, :], ALU.mult).then_inc(s["u_mul"], 1)
                dve.wait_ge(s["u_hi"], n + 1)
                nc.vector.tensor_tensor(blk_of(ac_lo, slot), ft[:, c % 2, :], blk_of(ac_hi, slot).bitcast(F32),
                                        ALU.subtract).then_inc(s["act_done"], 1)

            def accumulate(n_cols, b0):
                for t in range(TT):
                    ins = nc.vector.tensor_tensor(res[:, t, n_cols], res[:, t, n_cols], ps[:, b0 + t, :], ALU.add)
                ins.then_inc(s["d_free"], 1)

            with dve.Fori(0, NG) as g:
                with dve.Fori(0, 2) as i:
                    link.loop(g * 8 + i * 4)
                    for c in range(4):
                        for k in range(8):
                            lo(g * 96 + i * 32 + U_FF, 8 * c + k + HL)
                        blk = g * 8 + i * 4 + c
                        ffn_block(blk, c, par[:, bass.ds(blk + PAR_FW, 1)], par[:, bass.ds(blk + (PAR_FW + 2 * FB), 1)],
                                  i * 4 + c)
                dve.wait_ge(s["res_acc"], TT)
                with dve.Fori(0, 2) as i:
                    for half in range(2):
                        for k in range(8):
                            lo(g * 96 + i * 16 + (U_FF + 64), 8 * half + k + HL)
                        dve.wait_ge(unit_used, g * 96 + i * 16 + (U_FF + 64 + 8 * (half + 1) + HL))
                        accumulate(bass.ds(i * 1024 + half * 512, 512), 4 * half)
            link.loop(NG * 8)
            for c in range(TAIL):
                for k in range(8):
                    lo(U_TL, 8 * c + k + HL)
                blk = NG * G + c
                ffn_block(blk, c, par[:, PAR_FW + blk:PAR_FW + blk + 1], par[:, PAR_FW + 2 * FB + blk:PAR_FW + 2 * FB + blk + 1],
                          c)
            for n in range(4):
                for k in range(TAIL):
                    lo(U_TL, 8 * TAIL + n * TAIL + k + HL)
                dve.wait_ge(unit_used, U_TL + 8 * TAIL + TAIL * (n + 1) + HL)
                accumulate(slice(n * 512, (n + 1) * 512), 4 * (n % 2))
                dve.wait_ge(s["d_free"], 4 * NG + n + 2 + 1)
                for t in range(TT):
                    ins = nc.vector.bn_stats(st[:, t, n, :], res[:, t, n * 512:(n + 1) * 512])
                link(ins)
            link = Chain(dve, s["link_y"])
            dve.wait_ge(s["gb_bc"], 64)
            norm_stats(s["ln2_var"], s["ln2_std"], s["ln2_hn"])
            for t in range(TT):
                dve.wait_ge(s["hn_rows"], t + 1)
                link(nc.vector.tensor_tensor(res[:, t, :], res[:, t, :], g2b[:, :], ALU.mult))
                nc.vector.tensor_tensor(res[:, t, :], res[:, t, :], b2b[:, :], ALU.add).then_inc(s["ln2_y"], 1)

        @block.tensor
        def _(pe):
            mm = nc.tensor.matmul

            def transpose(o, i, rows=P):
                return nc.tensor.transpose(o, i, ident[0:rows, 0:rows])

            def unit_ready(ub, k):
                pe.wait_ge(w_lo_ready, ub + k + 1 + RAW)

            def three(o, a_hi, a_lo, b_hi, b_lo, first, last):
                mm(o, a_hi, b_hi, start=first, stop=False)
                mm(o, a_hi, b_lo, start=False, stop=False)
                return mm(o, a_lo, b_hi, start=False, stop=last)

            def two_by_two(ub, k, ko, bank, act_hi, act_lo):
                unit_ready(ub, k)
                for kk in range(2):
                    for o in range(2):
                        cols = slice((2 * kk + o) * P, (2 * kk + o + 1) * P)
                        kb = 2 * ko + kk
                        last = three(ps[:, bank + o, :], whi[:, k % HL, cols], wlo[:, k % HL, cols],
                                     act_hi[:, kb, :], act_lo[:, kb, :], kb == 0, kb == KB - 1)
                last.then_inc(unit_used, 1)

            def four_by_one(ub, k, kq, n_kb, o, act_hi, act_lo):
                unit_ready(ub, k)
                for kk in range(4):
                    kb = 4 * kq + kk
                    cols = slice(kk * P, (kk + 1) * P)
                    last = three(o, whi[:, k % HL, cols], wlo[:, k % HL, cols], act_hi[:, kb, :], act_lo[:, kb, :],
                                 kb == 0, kb == n_kb - 1)
                last.then_inc(unit_used, 1)

            def one_by_four(ub, k, kb, n_kb, bank, act_hi, act_lo):
                unit_ready(ub, k)
                for t in range(TT):
                    ts = slice(t * P, (t + 1) * P)
                    last = three(ps[:, bank + t, :], act_hi[:, kb, ts], act_lo[:, kb, ts],
                                 whi[:, k % HL, :], wlo[:, k % HL, :], kb == 0, kb == n_kb - 1)
                last.then_inc(unit_used, 1)

            pe.wait_ge(s["const_in"], 32)
            for kb in range(KB):
                if kb % 4 == 0:
                    pe.wait_ge(x_in[kb // 4], 16)
                if kb >= 8:
                    pe.wait_ge(s["xt_lo_done"], kb - 7)
                for t in range(TT):
                    last = transpose(ps[:, kb % 8, t * P:(t + 1) * P], x_tok[:, t, kb * P:(kb + 1) * P])
                last.then_inc(s["xt_ps"], 1)
            pe.wait_ge(s["par_in"], 16 * 11)
            pe.wait_ge(s["xt_lo_done"], KB)
            for i, w in enumerate((PAR_B1 + 16, 2 * FB, 2 * FB)):
                last = transpose(ps[:, 7, i * P:i * P + w], prow[0:w, i, :], w)
            last.then_inc(s["par_ps"], 1)
            pe.wait_ge(s["wg_lo_done"], 1)
            for t in range(TT):
                ts = slice(t * P, (t + 1) * P)
                for kb in range(KB):
                    last = three(ps[:, 0, t * 16:(t + 1) * 16], xt_hi[:, kb, ts], xt_lo[:, kb, ts],
                                 wg_hi[:, kb, :], wg_lo[:, kb, :], kb == 0, kb == KB - 1)
            last.then_inc(s["gate_ps"], 1)
            pe.wait_ge(s["gate_tok"], 1)
            for g in range(4):
                for t in range(TT):
                    last = transpose(ps[0:ML_H, 1 + g, t * P:(t + 1) * P], gtok[:, t, 4 * g:4 * g + 4])
            last.then_inc(s["gate_rows"], 1)
            pe.wait_ge(s["rows_a"], 1)
            pe.wait_ge(s["em_row"], 1)
            for d in range(2):
                for c in range(4):
                    cs = slice(c * P, (c + 1) * P)
                    for dist in range(4):
                        at = ((d * 4 + c) * 4 + dist) * 4
                        transpose(ps[:, 5, at:at + 4], row_a[:, d, dist, cs], ML_H)
                    at = 128 + (d * 4 + c) * 4
                    last = transpose(ps[:, 5, at:at + 4], ex[:, d, cs], ML_H)
            last.then_inc(s["cols_ps"], 1)
            pe.wait_ge(s["gate_end"], 1)

            with pe.Fori(0, ML_H) as h:
                ub = h * 32 + U_ML
                for c, (free, n) in enumerate((("free_v", 1), ("free_o", 1), ("conv_b", 2), ("conv_b", 4))):
                    pe.wait_ge(s[free], h * (1 if c < 2 else 4) + n)
                    for k in range(8):
                        two_by_two(ub, 8 * c + k, k, 2 * (c % 2), xt_hi, xt_lo)
                pe.wait_ge(s["free_v"], h + 1 + 1)
                pe.wait_ge(s["y_mul"], h * 2 + 1)
                for b in range(2):
                    for c in range(TT):
                        last = transpose(ps[:, 4 + c // 2, (c % 2) * 256 + b * P:(c % 2) * 256 + (b + 1) * P],
                                         vt[:, b, c * P:(c + 1) * P])
                last.then_inc(s["vtr_done"], 1)
                pe.wait_ge(s["qk_done"], h * 4 + 4 + 1)
                pe.wait_ge(s["pv_free"], h * 4 + 1)
                for c in range(4):
                    if c >= 2:
                        pe.wait_ge(s["w_done"], h * 4 + (c - 1) + 1)
                    for b in range(2):
                        last = mm(ps[:, 6 + c % 2, :], kt[:, b, c * P:(c + 1) * P], qt[:, b, :], start=b == 0, stop=b == 1)
                    last.then_inc(s["qkt_done"], 1)
                pe.wait_ge(s["vtok_done"], h + 1)
                pe.wait_ge(s["w_done"], h * 4 + 4 + 1)
                for tc in range(4):
                    b0 = 4 + 2 * (tc % 2)
                    if tc >= 2:
                        pe.wait_ge(s["pv_free"], h * 4 + (tc - 1) + 1)
                    for d in range(2):
                        cs = list(range(tc + 1)) if d == 0 else list(range(tc, 4))
                        for c in cs:
                            slot = (0, 4, 7, 9)[c] + tc - c if d == 0 else (0, 1, 3, 6)[c] + tc
                            last = mm(ps[:, b0 + d, 0:257], wmat[:, d, slot * P:(slot + 1) * P], vtok[:, c, 0:257],
                                      start=c == cs[0], stop=c == cs[-1])
                    last.then_inc(s["pv_done"], 1)
                pe.wait_ge(s["hn_done"], h + 1)
                for b in range(2):
                    for tc in range(4):
                        last = transpose(ps[:, 4 + b, tc * P:(tc + 1) * P], htok[:, tc, b * P:(b + 1) * P])
                    last.then_inc(s["yps_done"], 1)
            pe.wait_ge(s["free_o"], ML_H + 1)
            pe.wait_ge(s["ylo_done"], 8 + 1)

            with pe.Fori(0, 4) as i:
                ub = i * 24 + U_NA
                pe.wait_ge(s["na_qk_done"], i * 2 + 1)
                for k in range(8):
                    two_by_two(ub, k, k, 0, xt_hi, xt_lo)
                pe.wait_ge(s["na_v_done"], i + 1)
                pe.wait_ge(s["yna_l"], i * 2 + 1)
                for t in range(7):
                    first = P * t if t < 4 else ROWS * STRIP + P * (t - 4)
                    for pr in range(2):
                        last = transpose(ps[:, 4 + t // 2, (t % 2) * 256 + pr * P:(t % 2) * 256 + (pr + 1) * P],
                                         nvt[:, pr, first:first + P])
                last.then_inc(s["na_vt_ps"], 1)
                pe.wait_ge(s["na_v7"], i + 1)
                for pr in range(2):
                    for k in range(8):
                        four_by_one(ub, 8 + 8 * pr + k, k % 4, KB, ps[:, (2, 0)[pr] + k // 4, :], xt_hi, xt_lo)
                    pe.wait_ge(s["na_qk_done"], i * 2 + (pr + 1) + 1)
                    pe.wait_ge(s["yna_l"], i * 2 + pr + 1)
                    for hh in range(2):
                        hp = slice(64 * hh, 64 * hh + 64)
                        for j in range(NJ):
                            last = mm(ps[:, 4 + 2 * hh + j // 2, (j % 2) * 256:(j % 2) * 256 + 256],
                                      qk[hp, 0, P * j:P * (j + 1)], qk[hp, 1, ROWS * KSTART[j]:ROWS * KSTART[j] + 256],
                                      start=True, stop=True)
                        last.then_inc(s["s_done"], 1)
                    for hh in range(2):
                        pe.wait_ge(s["p_done"], i * 4 + (2 * pr + hh + 1))
                        for j in range(NJ):
                            for half in range(2):
                                last = transpose(ps[:, 4 + 2 * hh + j // 2, (2 * (j % 2) + half) * P:(2 * (j % 2) + half + 1) * P],
                                                 sc[:, hh, j, half * P:(half + 1) * P])
                        last.then_inc(s["pt_ps"], 1)
                    for hh in range(2):
                        pe.wait_ge(s["pt_done"], i * 4 + (2 * pr + hh + 1))
                        for j in range(NJ):
                            tiles = ((0, 1), (4, 5), (5, 6), (2, 3))[j]
                            for half in range(2):
                                last = mm(ps[64 * hh:64 * hh + 64, 4, j * P:(j + 1) * P],
                                          v7[:, tiles[half], pr * P + 64 * hh:pr * P + 64 * hh + 64],
                                          pt[:, hh, 2 * j + half, :], start=half == 0, stop=half == 1)
                    last.then_inc(s["ypv_done"], 1)
            pe.wait_ge(s["yna_l"], 8 + 1)

            with pe.Fori(0, KB // 2) as i:
                ub = i * 24 + U_MG
                for half in range(2):
                    pe.wait_ge(s["merge_sg"], i * 2 + half + 1)
                    for k in range(8):
                        four_by_one(ub, 12 * half + k, k % 4, KB, ps[:, k // 4, :], xt_hi, xt_lo)
                    pe.wait_ge(s["mix_done"], i * 2 + half + 1)
                    for k in range(8, 12):
                        y_hi, y_lo = ((yna_hi, yna_lo), (yml_hi, yml_lo))[(k - 8) // 2]
                        four_by_one(ub, 12 * half + k, k % 2, 8, ps[:, 2 + (k - 8) // 2, :], y_hi, y_lo)

            with pe.Fori(0, 2) as i:
                for half in range(2):
                    pe.wait_ge(s["wo_free"], i * 2 + half + 1)
                    for k in range(KB):
                        pe.wait_ge(s["mxlo_done"], k + 1)
                        one_by_four(i * 32 + U_WO, 16 * half + k, k, KB, 4 - 4 * half, mx_hi, mx_lo)
            for kb in range(KB):
                pe.wait_ge(s["hn_cols"], kb // 4 + 1)
                if kb >= 4:
                    pe.wait_ge(s["ht_lo_d"], kb - 3)
                for t in range(TT):
                    last = transpose(ps[:, 4 + kb % 4, t * P:(t + 1) * P], res[:, t, kb * P:(kb + 1) * P])
                last.then_inc(s["ht_ps"], 1)

            with pe.Fori(0, NG) as g:
                with pe.Fori(0, 2) as i:
                    for c in range(4):
                        pe.wait_ge(s["d_free"], g * 4 + c // 2 + 1)
                        pe.wait_ge(s["u_mul"], g * 8 + i * 4 + (c + 1))
                        for k in range(8):
                            if c == 0:
                                pe.wait_ge(s["ht_lo_d"], 4 * (k % 4) + 4)
                            four_by_one(g * 96 + i * 32 + U_FF, 8 * c + k, k % 4, KB, ps[:, 2 * c + k // 4, :], ht_hi, ht_lo)
                with pe.Fori(0, 2) as i:
                    for half in range(2):
                        pe.wait_ge(s["u_mul"], g * 8 + (10, 12)[half])
                        pe.wait_ge(s["d_free"], g * 4 + i * 2 + half + 1)
                        for k in range(G):
                            pe.wait_ge(s["act_done"], g * 8 + (k + 3))
                            one_by_four(g * 96 + i * 16 + (U_FF + 64), 8 * half + k, k, G, 4 * half, ac_hi, ac_lo)
            for c in range(TAIL):
                pe.wait_ge(s["d_free"], NG * 4 + c // 2 + 1)
                for k in range(8):
                    four_by_one(U_TL, 8 * c + k, k % 4, KB, ps[:, 2 * c + k // 4, :], ht_hi, ht_lo)
            for n in range(4):
                pe.wait_ge(s["u_mul"], NG * 8 + 4 + (2, 3)[n % 2] if n < 2 else NG * 8 + 7)
                pe.wait_ge(s["d_free"], NG * 4 + n + 1)
                for k in range(TAIL):
                    pe.wait_ge(s["act_done"], NG * 8 + k + 3)
                    one_by_four(U_TL, 8 * TAIL + n * TAIL + k, k, TAIL, 4 * (n % 2), ac_hi, ac_lo)


_INS = ["x", "w_in", "na_rpb", "ml_conv_w", "ml_conv_b", "ml_igate_b", "ml_fgate_b", "ml_norm_w", "w_branch_na",
        "w_branch_ml", "w_out", "ln1_g", "ln1_b", "ffn_w_up", "ffn_conv_w", "ffn_conv_b", "ffn_w_down", "ln2_g", "ln2_b"]


def shape_constants():
    c = np.zeros((P, 3 * P + NJ * 256), np.float32)
    c[:, 0:P] = np.eye(P)
    a, b = np.arange(P)[:, None], np.arange(P)[None, :]
    c[:, P:2 * P] = np.where(a <= b, 0.0, NEG)
    c[:, 2 * P:3 * P] = np.where(a >= b, 0.0, NEG)
    for j in range(NJ):
        p, f = np.arange(P)[:, None], np.arange(256)[None, :]
        q = QCOLS * j + STRIP * (p // (ROWS * STRIP)) + STRIP - 1 - p % STRIP
        k = KSTART[j] + STRIP * (f // (ROWS * STRIP)) + f % STRIP
        w = np.clip(q - WIN_COLS // 2, 0, GRID_W - WIN_COLS)
        c[:, 3 * P + j * 256:3 * P + (j + 1) * 256] = np.where((k >= w) & (k < w + WIN_COLS), 3e38, NEG)
    return c


def kernel(**inputs):
    import concourse.bacc as bacc
    from concourse.bass_utils import run_bass_kernel_spmd

    nc = bacc.Bacc("TRN2", target_bir_lowering=False, num_devices=1)
    arrays, args = {}, []
    for name in _INS:
        a = np.ascontiguousarray(inputs[name])
        arrays["in_" + name] = a
        args.append(nc.dram_tensor("in_" + name, a.shape, mybir.dt.from_np(a.dtype), kind="ExternalInput").ap())
    consts = shape_constants()
    arrays["in_consts"] = consts
    args.append(nc.dram_tensor("in_consts", consts.shape, F32, kind="ExternalInput").ap())
    out = nc.dram_tensor("out_0", (1, S, D), F32, kind="ExternalOutput").ap()
    build(nc, *args, out)
    r = run_bass_kernel_spmd(nc, [arrays], core_ids=[0])
    return r.results[0]["out_0"]
```

```python
import math
import numpy as np
import concourse.bass as bass
from concourse import mybir
from contextlib import ExitStack

F32 = mybir.dt.float32
F32R = mybir.dt.float32r
ACT = mybir.ActivationFunctionType
ALU = mybir.AluOpType
AX = mybir.AxisListType

P = 128
S = 512
D = 2048
KB = D // P
TT = S // P
GRID_W = 64
ROWS = S // GRID_W
QCOLS = 16
KCOLS = 32
WIN_COLS = 16
STRIP = 8
NJ = GRID_W // QCOLS
KSTART = [min(max(QCOLS * j - WIN_COLS // 2, 0), GRID_W - KCOLS) for j in range(NJ)]
NA_W = 1024
NA_H = 16
ML_W = 1024
ML_H = 4
DFF = 5504
FB = DFF // P
G = 8
NG = FB // G
TAIL = FB - NG * G
RPB_R, RPB_C = 15, 31
RPB_HEAD = RPB_R * RPB_C
TABLE = 7 * RPB_C + KCOLS + WIN_COLS
PAD = 16
NEG = -1e30
EPS = 1e-5
ALPHA = 2 ** 0.25
RAW, HL = 8, 4

C_MLQ, C_MLK, C_MLV, C_MLO = 3072, 4096, 5120, 6144
C_GATE, C_MERGE = 7168, 7184

U_ML = 0
U_NA = U_ML + ML_H * 32
U_MG = U_NA + 4 * 24
U_WO = U_MG + 16 * 12
U_FF = U_WO + 4 * KB
U_TL = U_FF + NG * (8 * G + 4 * G)
U_END = U_TL + TAIL * 8 + 4 * TAIL

PAR_MLW, PAR_MLB, PAR_NW, PAR_G1, PAR_B1 = 0, 48, 64, 72, 88
PAR_FW, PAR_FB = 128, 128 + 3 * FB
PAR_OFF = (0, PAR_FW, PAR_FW + 2 * FB)


def build(nc, x, w_in, na_rpb, ml_conv_w, ml_conv_b, ml_igate_b, ml_fgate_b, ml_norm_w, w_bna, w_bml,
          w_out, ln1_g, ln1_b, w_up, ffn_conv_w, ffn_conv_b, w_down, ln2_g, ln2_b, consts, out):
    ctx = ExitStack()
    with ctx:
        K = 1024
        ARENA = 16640

        def sb(name, shape, offset, dt=F32):
            return nc.alloc_sbuf_tensor_at(name, shape, dt, offset=ARENA + int(offset))

        def sem(name):
            return ctx.enter_context(nc.semaphore(name))

        raw = sb("raw", [P, RAW, 512], 0)
        whi = sb("whi", [P, HL, 512], 16 * K, F32R)
        wlo = sb("wlo", [P, HL, 512], 24 * K, F32R)
        xt_hi = sb("xt_hi", [P, KB, S], 32 * K, F32R)
        xt_lo = sb("xt_lo", [P, KB, S], 64 * K, F32R)
        yml_hi = sb("yml_hi", [P, 8, S], 96 * K, F32R)
        yml_lo = sb("yml_lo", [P, 8, S], 112 * K, F32R)
        yna_hi = sb("yna_hi", [P, 8, S], 128 * K, F32R)
        yna_lo = sb("yna_lo", [P, 8, S], 144 * K, F32R)
        x_tok = sb("x_tok", [P, TT, D], 96 * K)
        row_a = sb("row_a", [ML_H, 2, 4, S], 128 * K)
        li = sb("li", [ML_H, 2, S], 144 * K)
        lf = sb("lf", [ML_H, 2, S], 148 * K)
        mrow = sb("mrow", [ML_H, 2, S], 152 * K)
        bl = sb("bl", [ML_H, 2, S], 156 * K)
        fx = sb("fx", [ML_H, 2, S], 96 * K)
        ex = sb("ex", [ML_H, 2, S], 100 * K)
        rrow = sb("rrow", [ML_H, 2, S], 104 * K)
        prow = sb("prow", [P, 3, P], 181 * K)
        ones4 = sb("ones4", [ML_H, P], 184 * K)
        wg = sb("wg", [P, KB, 16], 189 * K)
        wg_hi = sb("wg_hi", [P, KB, P], 112 * K, F32R)
        wg_lo = sb("wg_lo", [P, KB, P], 120 * K, F32R)
        wmat = sb("wmat", [P, 2, 10 * P], 128 * K)
        vtok = sb("vtok", [P, TT, 258], 138 * K)
        htok = sb("htok", [P, TT, 256], 144 * K)
        qt = sb("qt", [P, 2, S], 160 * K)
        kt = sb("kt", [P, 2, S], 164 * K)
        vt = sb("vt", [P, 2, S], 168 * K)
        ot = sb("ot", [P, 2, S], 172 * K)
        rbc = sb("rbc", [P, 2, S], 181 * K)
        rmask = sb("rmask", [P, 2, S], 185 * K)
        yt = rmask
        cv = sb("cv", [P, 2, S], 193 * K)
        sg = sb("sg", [P, 2, S], 197 * K)
        qk = sb("qk", [P, 2, S], 160 * K)
        nvt = sb("nvt", [P, 2, S], 164 * K)
        v7 = sb("v7", [P, 7, 256], 168 * K)
        table = sb("table", [P, 4, TABLE + 1], 176 * K)
        sc = sb("sc", [P, 2, NJ, 256], 181 * K)
        pt = sb("pt", [P, 2, 8, P], 193 * K)
        namask = sb("namask", [P, NJ, 256], 189 * K)
        mixed = sb("mixed", [P, KB, S], 160 * K)
        mg = sb("mg", [P, 2, S], 192 * K)
        mt = sb("mt", [P, 2, S], 196 * K)
        mx_hi = sb("mx_hi", [P, KB, S], 32 * K, F32R)
        mx_lo = sb("mx_lo", [P, KB, S], 64 * K, F32R)
        res = sb("res", [P, TT, D], 96 * K)
        ht_hi = sb("ht_hi", [P, KB, S], 128 * K, F32R)
        ht_lo = sb("ht_lo", [P, KB, S], 160 * K, F32R)
        ac_hi = sb("ac_hi", [P, G, S], 32 * K, F32R)
        ac_lo = sb("ac_lo", [P, G, S], 48 * K, F32R)
        g1b = sb("g1b", [P, D], 64 * K)
        b1b = sb("b1b", [P, D], 72 * K)
        g2b = sb("g2b", [P, D], 80 * K)
        b2b = sb("b2b", [P, D], 88 * K)
        ft = sb("ft", [P, 2, S], 192 * K)
        fg = sb("fg", [P, 2, S], 196 * K)
        ident = sb("ident", [P, P], 201 * K)
        tri = sb("tri", [P, 2, P], 201 * K + 512)
        par = sb("par", [P, 3 * P], 202 * K + 512)
        bias_s = sb("bias_s", [P, 160], 204 * K)
        st = sb("st", [P, TT, 4, 6], 204 * K + 640)
        mv = sb("mv", [P, TT, 2], 204 * K + 1024)
        rstd = sb("rstd", [P, TT], 204 * K + 1056)
        nmu = sb("nmu", [P, TT], 204 * K + 1088)
        dn = sb("dn", [P, 2], 204 * K + 1120)
        smax = sb("smax", [P, 2, NJ], 204 * K + 1152)
        ssum = sb("ssum", [P, 2, NJ], 204 * K + 1184)
        gb = sb("gb", [P, 1], 204 * K + 1216)
        zpad = sb("zpad", [1, PAD], 204 * K + 1248)
        veps = sb("veps", [P, TT], 204 * K + 1312)
        rpb_pad = nc.dram_tensor("rpb_pad", [PAD + NA_H * RPB_HEAD + PAD], F32)
        rdram = nc.dram_tensor("rdram", [ML_H, 2 * S], F32)

        def blk_of(tile, n):
            return tile[:, :, :].rearrange("p k s -> p (k s)")[:, bass.ds(n * S, S)]

        def together(tile):
            return tile[:, :, :].rearrange("p k (g c) -> p k g c", g=4)

        def apart(tile):
            return tile[:, :, :].rearrange("p k (g c) -> p k g c", g=4)[:, :, :, 0:ML_H]

        def by_strip(ap):
            return ap.rearrange("p (r b e) -> p b r e", r=ROWS, e=STRIP)

        def strips(ap):
            return ap.rearrange("p (b r e) -> p b r e", r=ROWS, e=STRIP)

        ps = ctx.enter_context(nc.psum_tensor("ps", [P, 8, 512], F32))

        x_in = [sem(f"x_in{n}") for n in range(4)]
        weights_in = [sem(f"weights_in{i}") for i in range(RAW)]
        w_hi_ready, w_lo_ready, unit_used = sem("w_hi_ready"), sem("w_lo_ready"), sem("unit_used")
        names = """act_done cols_done cols_ps const_in conv_a conv_b conv_sg d_free dve_mark e_done em_row exp_fx
            free_o free_v gate_rows gb_bc gb_in hn_cols hn_done ident_in hn_rows ht_hi_d ht_lo_d
            ht_ps in_consts link_conv link_ff link_mg link_ml link_na link_pool link_u link_wo link_x link_y
            ln1_hn ln1_std ln1_var ln2_hn ln2_std ln2_var ln2_y log_fx mask_in merge_sg mix_done mxhi_done
            mxlo_done na_qk_done na_v7 na_v_done na_vt_ps neg_fx ones_set out_done p_done pad_out pad_zero
            par_done par_in par_ps pexp_done pt_done pt_ps pv_done pv_free qk_done qkt_done r_in res_acc
            res_in rmask_done rows_a rscr_out s_done smx_done sp_mark std_done table_in u_conv u_conv2
            u_gelu u_hi u_mul var_done vtok_done vtr_done w_done wg_hi_done wg_in wg_lo_done wg_zero wo_free
            xt_hi_done xt_lo_done xt_ps y_mul yhi_done ylo_done yna_h yna_l yps_done ypv_done""".split()
        s = {n: sem(n) for n in names}

        STARTS_AT_ONE = """w_done qk_done ylo_done vtr_done y_mul pv_done na_vt_ps mix_done qkt_done pv_free
            free_v free_o na_qk_done yna_l merge_sg wo_free d_free""".split()

        class Chain:
            def __init__(self, eng, semaphore):
                self.eng, self.sem, self.base, self.k = eng, semaphore, 0, 0

            def loop(self, base):
                self.base, self.k = base, 0

            def __call__(self, instruction):
                self.k += 1
                instruction.then_inc(self.sem, 1)
                self.eng.wait_ge(self.sem, self.base + self.k)

        block = ctx.enter_context(nc.Block())
        win = w_in[0]

        @block.sync
        def _(sp):
            def unit(src, shape, u, n, **dims):
                sp.wait_ge(w_lo_ready, u + n + 1)
                sp.sem_inc(s["sp_mark"], 1)
                dst = raw[:, n % RAW, :]
                if shape:
                    dst = dst.rearrange(shape, **dims)
                sp.dma_start(dst, src).then_inc(weights_in[n % RAW], 16)

            wk = win.rearrange("(k p) c -> p k c", p=P)
            with sp.Fori(0, ML_H) as h:
                for c, col in enumerate((C_MLQ, C_MLK, C_MLV, C_MLO)):
                    for k in range(8):
                        unit(wk[:, 2 * k:2 * k + 2, bass.ds(h * 256 + col, 256)], "p (k c) -> p k c",
                             U_ML + h * 32, 8 * c + k, k=2)
            with sp.Fori(0, 4) as i:
                for k in range(8):
                    unit(wk[:, 4 * (k % 4):4 * (k % 4) + 4, bass.ds(i * 256 + (2 * NA_W + P * (k // 4)), P)], "p (k c) -> p k c",
                         U_NA + i * 24, k, k=4)
                for pr in range(2):
                    for k in range(8):
                        unit(wk[:, 4 * (k % 4):4 * (k % 4) + 4, bass.ds(i * 256 + (pr * P + NA_W * (k // 4)), P)], "p (k c) -> p k c",
                             U_NA + i * 24, 8 + 8 * pr + k, k=4)
            wbn = w_bna[0].rearrange("(k p) c -> p k c", p=P)
            wbm = w_bml[0].rearrange("(k p) c -> p k c", p=P)
            with sp.Fori(0, KB // 2) as i:
                for half in range(2):
                    for k in range(8):
                        unit(wk[:, 4 * (k % 4):4 * (k % 4) + 4, bass.ds(i * 256 + (half * P + C_MERGE + D * (k // 4)), P)],
                             "p (k c) -> p k c", U_MG + i * 24, 12 * half + k, k=4)
                    for k in range(4):
                        w = (wbm, wbn)[k // 2]
                        unit(w[:, 4 * (k % 2):4 * (k % 2) + 4, bass.ds(i * 256 + half * P, P)], "p (k c) -> p k c",
                             U_MG + i * 24, 12 * half + 8 + k, k=4)
            with sp.Fori(0, 2) as i:
                for half in range(2):
                    for k in range(KB):
                        unit(w_out[0][k * P:(k + 1) * P, bass.ds(i * 1024 + half * 512, 512)], None,
                             U_WO + i * 32, 16 * half + k)
            wup = w_up[0].rearrange("(k p) c -> p k c", p=P)
            with sp.Fori(0, NG) as g:
                with sp.Fori(0, 2) as i:
                    for c in range(4):
                        for k in range(8):
                            unit(wup[:, 4 * (k % 4):4 * (k % 4) + 4, bass.ds(g * (G * P) + i * 512 + (c * P + DFF * (k // 4)), P)],
                                 "p (k c) -> p k c", U_FF + g * 96 + i * 32, 8 * c + k, k=4)
                with sp.Fori(0, 2) as i:
                    for half in range(2):
                        for k in range(G):
                            unit(w_down[0][bass.ds(g * (G * P) + k * P, P), bass.ds(i * 1024 + half * 512, 512)],
                                 None, U_FF + g * 96 + 64 + i * 16, 8 * half + k)
            for c in range(TAIL):
                for k in range(8):
                    j = NG * G + c
                    first = j * P + DFF * (k // 4)
                    unit(wup[:, 4 * (k % 4):4 * (k % 4) + 4, first:first + P], "p (k c) -> p k c", U_TL, 8 * c + k, k=4)
            for n in range(4):
                for k in range(TAIL):
                    j = NG * G + k
                    unit(w_down[0][j * P:(j + 1) * P, n * 512:(n + 1) * 512], None, U_TL, 8 * TAIL + n * TAIL + k)
            for t in range(TT):
                sp.wait_ge(s["ln2_y"], t + 1)
                sp.dma_start(out[0, t * P:(t + 1) * P, :], res[:, t, :]).then_inc(s["out_done"], 16)
            sp.wait_ge(s["out_done"], 16 * TT)

        @block.gpsimd
        def _(pool):
            pool.sem_inc(w_lo_ready, RAW)
            pool.sem_inc(unit_used, HL)
            for n in STARTS_AT_ONE + ["wo_free", "d_free"]:
                pool.sem_inc(s[n], 1)
            pool.sem_inc(s["u_mul"], 4)
            pool.sem_inc(s["act_done"], 2)
            pool.dma_start(tri[:, :, :], consts[:, P:3 * P].rearrange("p (d c) -> p d c", d=2)).then_inc(s["const_in"], 16)
            pool.dma_start(wg[:, :, :], win[:, C_GATE:C_GATE + 16].rearrange("(k p) c -> p k c", p=P)).then_inc(s["wg_in"], 16)
            loads = [(0, PAR_MLW, ml_conv_w[0].rearrange("w (b p) -> w b p", p=P), 3, 16),
                     (0, PAR_MLB, ml_conv_b[0].rearrange("(b p) -> b p", p=P), 0, 16),
                     (0, PAR_NW, ml_norm_w[0].rearrange("(b p) -> b p", p=P), 0, 8),
                     (0, PAR_G1, ln1_g[0].rearrange("(b p) -> b p", p=P), 0, 16),
                     (0, PAR_B1, ln1_b[0].rearrange("(b p) -> b p", p=P), 0, 16),
                     (1, 0, ffn_conv_w[0].rearrange("w (b p) -> w b p", p=P)[0:2], 2, FB),
                     (2, 0, ffn_conv_w[0].rearrange("w (b p) -> w b p", p=P)[2:3], 1, FB),
                     (2, FB, ffn_conv_b[0].rearrange("(b p) -> b p", p=P), 0, FB)]
            for tile, r0, src, w, nb in loads:
                for i in range(max(w, 1)):
                    pool.dma_start(prow[r0 + i * nb:r0 + (i + 1) * nb, tile, :], src[i] if w else src).then_inc(s["par_in"], 16)
            for n, b in enumerate((ml_igate_b, ml_fgate_b)):
                for d in range(2):
                    p0 = 32 * (2 * n + d)
                    pool.dma_start(gb[p0:p0 + ML_H, :],
                                   b[0, 4 * d:4 * d + 4].rearrange("(h o) -> h o", o=1)).then_inc(s["gb_in"], 16)
            pool.memset(zpad[:, :], 0.0).then_inc(s["pad_zero"], 1)
            pool.wait_ge(s["pad_zero"], 1)
            rp = rpb_pad.ap()
            end = PAD + NA_H * RPB_HEAD
            pool.dma_start(rp[0:PAD].rearrange("(o n) -> o n", o=1), zpad[:, :]).then_inc(s["pad_out"], 16)
            pool.dma_start(rp[end:end + PAD].rearrange("(o n) -> o n", o=1), zpad[:, :]).then_inc(s["pad_out"], 16)
            pool.dma_start(rp[PAD:end].rearrange("(h n) -> h n", h=NA_H),
                           na_rpb[0].rearrange("h r c -> h (r c)")).then_inc(s["pad_out"], 16)
            def load_table(i):
                for b in range(2):
                    for qr in range(ROWS):
                        p0 = (b * ROWS + qr) * STRIP
                        first = PAD + 4 * i * RPB_HEAD + (7 - qr) * RPB_C - STRIP * b - STRIP
                        pool.dma_start(table[p0:p0 + STRIP, :, 0:TABLE],
                                       bass.AP(rpb_pad, first, [[1, STRIP], [RPB_HEAD, 4], [1, TABLE]])).then_inc(s["table_in"], 16)

            pool.memset(ones4[:, :], 1.0).then_inc(s["ones_set"], 1)
            pool.memset(row_a[:, :, :, :], 0.0).then_inc(s["ones_set"], 1)
            pool.wait_ge(s["xt_ps"], KB)
            pool.memset(wg_hi[:, :, :].bitcast(F32), 0.0).then_inc(s["wg_zero"], 1)
            pool.memset(wg_lo[:, :, :].bitcast(F32), 0.0).then_inc(s["wg_zero"], 1)
            pool.wait_ge(s["pad_out"], 48)
            load_table(0)
            pool.wait_ge(s["rows_a"], 1)
            pool.dma_start(rdram.ap().rearrange("h (d s) -> h d s", d=2), rrow[:, :, :]).then_inc(s["rscr_out"], 16)
            pool.wait_ge(s["rscr_out"], 16)
            pool.wait_ge(s["cols_done"], 1)
            pool.dma_start(namask[:, :, :], consts[:, 3 * P:3 * P + NJ * 256].rearrange("p (j c) -> p j c", j=NJ)).then_inc(s["mask_in"], 16)
            with pool.Fori(0, ML_H) as h:
                pool.wait_ge(s["w_done"], h * 4 + 1)
                src = bass.AP(rdram, h * (2 * S), [[0, P], [1, 2 * S]])
                pool.dma_start(rbc[:, :, :].rearrange("p d s -> p (d s)"), src).then_inc(s["r_in"], 16)
            for i in range(1, 4):
                pool.wait_ge(s["smx_done"], 4 * i)
                load_table(i)
            pool.wait_ge(unit_used, U_WO + HL)
            pool.dma_start(res[:, :, :], x[0].rearrange("(t p) c -> p t c", p=P)).then_inc(s["res_in"], 16)
            pool.wait_ge(unit_used, U_FF + HL)
            for tile, src in ((g1b, ln1_g), (b1b, ln1_b), (g2b, ln2_g), (b2b, ln2_b)):
                pool.dma_start(tile[:, :], bass.AP(src.tensor, 0, [[0, P], [1, D]])).then_inc(s["gb_bc"], 16)
            pool.wait_ge(s["gb_bc"], 64)
            link = Chain(pool, s["link_pool"])
            link(nc.gpsimd.tensor_scalar(g1b[:, :], g1b[:, :], ALPHA, None, ALU.mult))
            link(nc.gpsimd.tensor_scalar(b1b[:, :], b1b[:, :], ALPHA, None, ALU.mult))
            pool.wait_ge(s["ht_ps"], KB)
            for t in range(TT):
                link(nc.gpsimd.tensor_tensor(res[:, t, :], res[:, t, :], g1b[:, :], ALU.mult))
                nc.gpsimd.tensor_tensor(res[:, t, :], res[:, t, :], b1b[:, :], ALU.add).then_inc(s["res_acc"], 1)

        @block.scalar
        def _(act):
            def hi(ub, u8, k):
                if isinstance(ub, int) and ub + k >= U_END:
                    return
                act.wait_ge(weights_in[k % RAW], (u8 + k // RAW + 1) * 16)
                act.wait_ge(unit_used, ub + k + 1)
                nc.scalar.activation(whi[:, k % HL, :], raw[:, k % RAW, :], ACT.Copy).then_inc(w_hi_ready, 1)

            act.dma_start(ident[:, :], consts[:, 0:P]).then_inc(s["ident_in"], 16)
            for n in range(4):
                act.dma_start(x_tok[:, :, n * 512:(n + 1) * 512],
                              x[0].rearrange("(t p) c -> p t c", p=P)[:, :, n * 512:(n + 1) * 512]).then_inc(x_in[n], 16)
            for n in range(4):
                for kb in range(4 * n, 4 * n + 4):
                    act.wait_ge(s["xt_ps"], kb + 1)
                    nc.scalar.activation(xt_hi[:, kb, :], ps[:, 4 + kb % 4, :], ACT.Copy).then_inc(s["xt_hi_done"], 1)
                hi(U_ML, U_ML // 8, 2 * n)
                hi(U_ML, U_ML // 8, 2 * n + 1)

            def do(hooks, u):
                for step in hooks.get(u, ()):
                    step()

            def gate_weights():
                act.wait_ge(s["wg_in"], 16)
                act.wait_ge(s["wg_zero"], 2)
                nc.scalar.activation(apart(wg_hi), together(wg), ACT.Copy).then_inc(s["wg_hi_done"], 1)

            def log1p_exp():
                act.wait_ge(s["neg_fx"], 1)
                nc.scalar.activation(ex[:, :, :], ex[:, :, :], ACT.Exp).then_inc(s["exp_fx"], 1)
                act.wait_ge(s["exp_fx"], 1)
                nc.scalar.activation(ex[:, :, :], ex[:, :, :], ACT.Ln, bias=1.0).then_inc(s["log_fx"], 1)

            def exp_minus_m():
                act.wait_ge(s["rows_a"], 1)
                nc.scalar.activation(ex[:, :, :], mrow[:, :, :], ACT.Exp, scale=-1.0).then_inc(s["em_row"], 1)

            def ml_projections(h, hooks, first=0):
                ub, u8 = h * 32 + U_ML, h * 4 + U_ML // 8
                for u in range(32):
                    if u >= first:
                        hi(ub, u8, u + HL)
                    if u % 8 == 7:
                        c = u // 8
                        act.wait_ge(unit_used, ub + (8 * (c + 1) + HL))
                        if c < 2:
                            for b in range(2):
                                blk = h * 2 + (8 * c + b)
                                act.wait_ge(s["qk_done"], h * 4 + ((1 + b if c else 0) + 1))
                                nc.scalar.activation(cv[:, b, :], ps[:, 2 * c + b, :], ACT.Identity,
                                                     scale=par[:, bass.ds(blk + (PAR_MLW + 16), 1)],
                                                     bias=par[:, bass.ds(blk + PAR_MLB, 1)]).then_inc(s["conv_a"], 1)
                            for b in range(2):
                                act.wait_ge(s["conv_b"], h * 4 + (2 * c + b + 1))
                                nc.scalar.activation(sg[:, b, :], cv[:, b, :], ACT.Sigmoid).then_inc(s["conv_sg"], 1)
                        elif c == 2:
                            act.wait_ge(s["vtr_done"], h + 1)
                            nc.scalar.activation(vt[:, :, :], ps[:, 0:2, :], ACT.Copy).then_inc(s["free_v"], 1)
                        else:
                            act.wait_ge(s["y_mul"], h * 2 + 1)
                            nc.scalar.activation(ot[:, :, :], ps[:, 2:4, :], ACT.Sigmoid).then_inc(s["free_o"], 1)
                    do(hooks, u)

            def mlstm(h):
                def v_token_major():
                    act.wait_ge(s["vtr_done"], h + 2)
                    act.wait_ge(s["pv_done"], h * 4 + 1)
                    nc.scalar.activation(vtok[:, :, 0:256], ps[:, 4:6, :].rearrange("p b (t c) -> p (b t) c", t=2),
                                         ACT.Copy).then_inc(s["vtok_done"], 1)

                def decay(c):
                    if c == 0:
                        act.wait_ge(s["rmask_done"], h + 1)
                    fo, bo = (0, 4, 7, 9)[c], (0, 1, 3, 6)[c]
                    work = [(0, c, 0, fo)] + [(0, tc, tc - c, fo + tc - c) for tc in range(c + 1, 4)] \
                        + [(1, tc, c - tc, bo + tc) for tc in range(c)] + [(1, c, 0, bo + c)]
                    for n, (d, tc, dist, slot) in enumerate(work):
                        src = rmask if dist == 0 else rbc
                        e = nc.scalar.activation(wmat[:, d, slot * P:(slot + 1) * P], src[:, d, tc * P:(tc + 1) * P], ACT.Exp,
                                                 bias=bias_s[:, bass.ds(h + ((d * 4 + c) * 4 + dist) * 4, 1)])
                    e.then_inc(s["e_done"], 1)

                def std():
                    act.wait_ge(s["var_done"], h + 1)
                    nc.scalar.activation(rstd[:, :], veps[:, :], ACT.Sqrt).then_inc(s["std_done"], 1)

                def y_hi():
                    for b in range(2):
                        act.wait_ge(s["y_mul"], h * 2 + (b + 2))
                        nc.scalar.activation(blk_of(yml_hi, h * 2 + b), yt[:, b, :], ACT.Copy).then_inc(s["yhi_done"], 1)

                return {1: [v_token_major, lambda: decay(0)], 2: [lambda: decay(1)], 4: [lambda: decay(2)],
                        5: [lambda: decay(3)], 12: [std], 15: [y_hi]}

            ml_projections(0, {4: [gate_weights], 6: [lambda: act.wait_ge(s["par_done"], 1)], 10: [log1p_exp], 18: [exp_minus_m]}, first=4)
            with act.Fori(0, ML_H - 1) as h:
                ml_projections(h + 1, mlstm(h))

            def na_v(i, hooks, first_out=3):
                ub, u8 = i * 24 + U_NA, i * 3 + U_NA // 8
                for u in range(8):
                    hi(ub, u8, u + HL)
                    for b, after in enumerate((first_out, 7)):
                        if u == after:
                            act.wait_ge(s["qkt_done"], 4 * ML_H + 1)
                            act.wait_ge(s["na_vt_ps"], i + 1)
                            nc.scalar.activation(strips(nvt[:, b, :]), by_strip(ps[:, b, :]), ACT.Copy).then_inc(s["na_v_done"], 1)
                    do(hooks, u)

            def na_qk(i, pr, hooks):
                ub, u8 = i * 24 + U_NA, i * 3 + U_NA // 8
                b0 = (2, 0)[pr]
                for u in range(8):
                    hi(ub, u8, 8 + 8 * pr + u + HL)
                    if u in (3, 7):
                        if not isinstance(i, int) or pr:
                            act.wait_ge(s["s_done"], i * 4 + 2 * pr)
                    if u == 3:
                        nc.scalar.activation(strips(qk[:, 0, :]), by_strip(ps[:, b0, :])[:, :, :, ::-1], ACT.Copy,
                                             scale=0.125).then_inc(s["na_qk_done"], 1)
                    if u == 7:
                        nc.scalar.activation(strips(qk[:, 1, :]), by_strip(ps[:, b0 + 1, :]), ACT.Copy).then_inc(s["na_qk_done"], 1)
                    do(hooks, u)

            def v7_copy(i):
                act.wait_ge(s["na_vt_ps"], i + 2)
                nc.scalar.activation(v7[:, :, :].rearrange("p i c -> p (i c)"),
                                     ps[:, 4:8, :].rearrange("p b c -> p (b c)")[:, 0:7 * 256], ACT.Copy).then_inc(s["na_v7"], 1)

            def softmax(i, pr, at):
                def exps(hh):
                    act.wait_ge(s["smx_done"], i * 4 + (2 * pr + hh + 1))
                    for j in range(NJ):
                        e = nc.scalar.activation(sc[:, hh, j, :], sc[:, hh, j, :], ACT.Exp, bias=smax[:, hh, j:j + 1],
                                                 accum_out=ssum[:, hh, j:j + 1])
                    e.then_inc(s["pexp_done"], 1)

                def pt_copy(hh):
                    act.wait_ge(s["pt_ps"], i * 4 + (2 * pr + hh + 1))
                    nc.scalar.activation(pt[:, hh, :, :].rearrange("p a b -> p (a b)"),
                                         ps[:, 4 + 2 * hh:6 + 2 * hh, :].rearrange("p a b -> p (a b)"), ACT.Copy).then_inc(s["pt_done"], 1)

                return {at + 1: [lambda: exps(0)], at + 2: [lambda: exps(1)], at + 5: [lambda: pt_copy(0)],
                        min(at + 6, 7): [lambda: pt_copy(1)]} if at < 2 else \
                    {at + 1: [lambda: exps(0)], at + 2: [lambda: exps(1)], 7: [lambda: pt_copy(0), lambda: pt_copy(1)]}

            def y_out(i, pr):
                act.wait_ge(s["ypv_done"], i * 2 + (pr + 1))
                nc.scalar.activation(by_strip(blk_of(yna_hi, i * 2 + pr)), strips(ps[:, 4, :])[:, :, :, ::-1],
                                     ACT.Copy).then_inc(s["yna_h"], 1)

            def plus(*all_hooks):
                out = {}
                for hooks in all_hooks:
                    for u, steps in hooks.items():
                        out.setdefault(u, []).extend(steps)
                return out

            last_head = mlstm(ML_H - 1)
            na_v(0, {u: f for u, f in last_head.items() if u < 8}, first_out=7)
            na_qk(0, 0, {u - 8: f for u, f in last_head.items() if u >= 8})
            na_qk(0, 1, plus({1: [lambda: v7_copy(0)]}, softmax(0, 0, 2)))
            with act.Fori(1, 4) as i:
                na_v(i, plus({0: [lambda: y_out(i - 1, 0)]}, softmax(i - 1, 1, 1)))
                na_qk(i, 0, {1: [lambda: y_out(i - 1, 1)], 4: [lambda: v7_copy(i)]})
                na_qk(i, 1, softmax(i, 0, 0))

            def merge(i, hooks):
                ub, u8 = i * 24 + U_MG, i * 3 + U_MG // 8
                for half in range(2):
                    for k in range(12):
                        hi(ub, u8, 12 * half + k + HL)
                        do(hooks, 12 * half + k)
                        if k == (9 if hooks and half == 0 else 7):
                            act.wait_ge(unit_used, ub + (12 * half + 8 + HL))
                            act.wait_ge(s["mix_done"], i * 2 + (half + 1))
                            nc.scalar.activation(mg[:, :, :], ps[:, 0:2, :], ACT.Sigmoid).then_inc(s["merge_sg"], 1)

            merge(0, plus({0: [lambda: y_out(3, 0)]}, softmax(3, 1, 1), {9: [lambda: y_out(3, 1)]}))
            with act.Fori(1, KB // 2) as i:
                merge(i, {})
            for kb in range(KB):
                act.wait_ge(s["mix_done"], KB + 1)
                act.wait_ge(unit_used, U_WO + HL)
                nc.scalar.activation(mx_hi[:, kb, :], mixed[:, kb, :], ACT.Copy).then_inc(s["mxhi_done"], 1)
            with act.Fori(0, 2) as i:
                for k in range(32):
                    hi(i * 32 + U_WO, i * 4 + U_WO // 8, k + HL)
            act.wait_ge(s["ln1_var"], 1)
            nc.scalar.activation(rstd[:, :], veps[:, :], ACT.Sqrt).then_inc(s["ln1_std"], 1)
            for n in range(4):
                act.wait_ge(s["ln1_hn"], 1)
                for t in range(TT):
                    e = nc.scalar.activation(res[:, t, n * 512:(n + 1) * 512], res[:, t, n * 512:(n + 1) * 512], ACT.Identity,
                                             scale=rstd[:, t:t + 1], bias=nmu[:, t:t + 1])
                e.then_inc(s["hn_cols"], 1)
            for kb in range(KB):
                act.wait_ge(s["ht_ps"], kb + 1)
                nc.scalar.activation(ht_hi[:, kb, :], ps[:, 4 + kb % 4, :], ACT.Identity,
                                     scale=par[:, PAR_G1 + kb:PAR_G1 + kb + 1],
                                     bias=par[:, PAR_B1 + kb:PAR_B1 + kb + 1]).then_inc(s["ht_hi_d"], 1)

            def ffn_block(n, c, par_w, par_b, slot):
                act.wait_ge(s["act_done"], n + 1)
                nc.scalar.activation(ft[:, c % 2, :], ps[:, 2 * c, :], ACT.Identity, scale=par_w, bias=par_b).then_inc(s["u_conv"], 1)
                act.wait_ge(s["u_conv2"], n + 1)
                nc.scalar.activation(fg[:, c % 2, :], ft[:, c % 2, :], ACT.Gelu).then_inc(s["u_gelu"], 1)
                act.wait_ge(s["u_mul"], n + 5)
                nc.scalar.activation(blk_of(ac_hi, slot), ft[:, c % 2, :], ACT.Copy).then_inc(s["u_hi"], 1)

            with act.Fori(0, NG) as g:
                with act.Fori(0, 2) as i:
                    for c in range(4):
                        for k in range(8):
                            hi(g * 96 + i * 32 + U_FF, g * 12 + i * 4 + U_FF // 8, 8 * c + k + HL)
                        blk = g * 8 + i * 4 + c
                        act.wait_ge(unit_used, g * 96 + i * 32 + (U_FF + 8 * (c + 1) + HL))
                        ffn_block(blk, c, par[:, bass.ds(blk + (PAR_FW + FB), 1)], par[:, bass.ds(blk + PAR_FB, 1)],
                                  i * 4 + c)
                with act.Fori(0, 2) as i:
                    for k in range(16):
                        hi(g * 96 + i * 16 + (U_FF + 64), g * 12 + i * 2 + (U_FF + 64) // 8, k + HL)
            for c in range(TAIL):
                for k in range(8):
                    hi(U_TL, U_TL // 8, 8 * c + k + HL)
                blk = NG * G + c
                act.wait_ge(unit_used, U_TL + 8 * (c + 1) + HL)
                ffn_block(blk, c, par[:, PAR_FW + FB + blk:PAR_FW + FB + blk + 1], par[:, PAR_FB + blk:PAR_FB + blk + 1],
                          c)
            for k in range(4 * TAIL):
                hi(U_TL, U_TL // 8, 8 * TAIL + k + HL)
            act.wait_ge(s["ln2_var"], 1)
            nc.scalar.activation(rstd[:, :], veps[:, :], ACT.Sqrt).then_inc(s["ln2_std"], 1)
            act.wait_ge(s["ln2_hn"], 1)
            for t in range(TT):
                nc.scalar.activation(res[:, t, :], res[:, t, :], ACT.Identity, scale=rstd[:, t:t + 1],
                                     bias=nmu[:, t:t + 1]).then_inc(s["hn_rows"], 1)

        @block.vector
        def _(dve):
            def lo(ub, k):
                if isinstance(ub, int) and ub + k >= U_END:
                    return
                dve.wait_ge(w_hi_ready, ub + k + 1)
                nc.vector.tensor_tensor(wlo[:, k % HL, :], raw[:, k % RAW, :], whi[:, k % HL, :].bitcast(F32),
                                        ALU.subtract).then_inc(w_lo_ready, 1)

            def do(hooks, u):
                for step in hooks.get(u, ()):
                    step()

            for n in range(4):
                for kb in range(4 * n, 4 * n + 4):
                    dve.wait_ge(s["xt_hi_done"], kb + 1)
                    nc.vector.tensor_tensor(xt_lo[:, kb, :], ps[:, 4 + kb % 4, :], xt_hi[:, kb, :].bitcast(F32),
                                            ALU.subtract).then_inc(s["xt_lo_done"], 1)
                lo(U_ML, 2 * n)
                lo(U_ML, 2 * n + 1)

            glink = Chain(dve, s["link_x"])

            def columns():
                dve.wait_ge(s["par_ps"], 1)
                for i, w in enumerate((PAR_B1 + 16, 2 * FB, 2 * FB)):
                    ins = nc.vector.tensor_copy(par[:, PAR_OFF[i]:PAR_OFF[i] + w], ps[:, 7, i * P:i * P + w])
                ins.then_inc(s["par_done"], 1)

            def gate_weights():
                dve.wait_ge(s["wg_hi_done"], 1)
                nc.vector.tensor_tensor(apart(wg_lo), together(wg), apart(wg_hi).bitcast(F32), ALU.subtract).then_inc(s["wg_lo_done"], 1)

            def gate_inputs():
                dve.wait_ge(s["gb_in"], 64)
                dve.wait_ge(s["ones_set"], 2)
                dve.wait_ge(s["gate_rows"], 1)
                for d in range(2):
                    i_rows, f_rows = slice(32 * d, 32 * d + ML_H), slice(64 + 32 * d, 64 + 32 * d + ML_H)
                    nc.vector.tensor_scalar(li[:, d, :], ps[i_rows, 4, :], gb[i_rows, :], None, ALU.add)
                    ins = nc.vector.tensor_scalar(fx[:, d, :], ps[f_rows, 4, :], gb[f_rows, :], None, ALU.add)
                glink(ins)
                nc.vector.scalar_tensor_tensor(ex[:, :, :], fx[:, :, :], -1.0, fx[:, :, :], ALU.mult, ALU.min).then_inc(s["neg_fx"], 1)

            def log_sigmoid():
                dve.wait_ge(s["log_fx"], 1)
                glink(nc.vector.scalar_tensor_tensor(lf[:, :, :], fx[:, :, :], 0.0, ex[:, :, :], ALU.min, ALU.subtract))

            def way(ap, d):
                return ap if d == 0 else ap[:, ::-1]

            def running_max(d):
                nc.vector.tensor_tensor_scan(way(mrow[:, d, :], d), way(lf[:, d, :], d), way(li[:, d, :], d), NEG, ALU.add, ALU.max)

            def chunk_sums(d):
                for c in range(4):
                    cs = slice(c * P, (c + 1) * P)
                    ins = nc.vector.tensor_tensor_scan(way(bl[:, d, cs], d), ones4[:, :], way(lf[:, d, cs], d), 0.0, ALU.mult, ALU.add)
                glink(ins)
                glink(nc.vector.tensor_tensor(row_a[:, d, 0, :], li[:, d, :], bl[:, d, :], ALU.subtract))

            def exponents(d, dist):
                for c in range(4):
                    tc = c + dist if d == 0 else c - dist
                    if 0 <= tc < 4:
                        mid = tc - 1 if d == 0 else tc + 1
                        at = mid * P + P - 1 if d == 0 else mid * P
                        cs = slice(c * P, (c + 1) * P)
                        ins = nc.vector.tensor_scalar(row_a[:, d, dist, cs], row_a[:, d, dist - 1, cs], bl[:, d, at:at + 1], None, ALU.add)
                glink(ins)

            def decay_rows():
                for d in range(2):
                    ins = nc.vector.tensor_tensor(rrow[:, d, :], bl[:, d, :], mrow[:, d, :], ALU.subtract)
                ins.then_inc(s["rows_a"], 1)

            def exponent_columns():
                dve.wait_ge(s["cols_ps"], 1)
                nc.vector.tensor_copy(bias_s[:, :], ps[:, 4, 0:160])
                nc.vector.memset(vtok[:, :, 256:257], 1.0).then_inc(s["cols_done"], 1)

            gate_hooks = {4: [columns], 5: [gate_weights], 9: [gate_inputs], 11: [log_sigmoid, lambda: running_max(0)],
                          12: [lambda: chunk_sums(0), lambda: exponents(0, 1)],
                          13: [lambda: exponents(0, 2), lambda: exponents(0, 3), lambda: running_max(1)],
                          14: [lambda: chunk_sums(1), lambda: exponents(1, 1)],
                          15: [lambda: exponents(1, 2), lambda: exponents(1, 3)],
                          16: [decay_rows], 21: [exponent_columns]}

            clink = Chain(dve, s["link_conv"])
            mlink = Chain(dve, s["link_ml"])
            ML_LINKS = 4 * 5 + 2

            def ml_projections(h, hooks, first=0):
                ub = h * 32 + U_ML
                clink.loop(h * 4)
                for u in range(32):
                    if u >= first:
                        lo(ub, u + HL)
                    if u in (7, 15):
                        c = u // 8
                        for b in range(2):
                            blk = h * 2 + (8 * c + b)
                            pb = ps[:, 2 * c + b, :]
                            dve.wait_ge(s["conv_a"], h * 4 + (2 * c + b + 1))
                            clink(nc.vector.scalar_tensor_tensor(cv[:, b, 1:S], pb[:, 0:S - 1], par[:, bass.ds(blk + PAR_MLW, 1)],
                                                                 cv[:, b, 1:S], ALU.mult, ALU.add))
                            nc.vector.scalar_tensor_tensor(cv[:, b, 0:S - 1], pb[:, 1:S], par[:, bass.ds(blk + (PAR_MLW + 32), 1)],
                                                           cv[:, b, 0:S - 1], ALU.mult, ALU.add).then_inc(s["conv_b"], 1)
                        for b in range(2):
                            dve.wait_ge(s["conv_sg"], h * 4 + (2 * c + b + 1))
                            if b == 0:
                                dve.wait_ge(s["qkt_done"], h * 4 + 1)
                            nc.vector.scalar_tensor_tensor((qt, kt)[c][:, b, :], cv[:, b, :], (1.0, 256 ** -0.5)[c], sg[:, b, :],
                                                           ALU.mult, ALU.mult).then_inc(s["qk_done"], 1)
                    do(hooks, u)

            def mlstm(h):
                mlink.loop(h * ML_LINKS)

                def mask_rows():
                    dve.wait_ge(s["r_in"], (h + 1) * 16)
                    for d in range(2):
                        ins = nc.vector.tensor_tensor(rmask[:, d, :].rearrange("p (c t) -> p c t", c=4),
                                                      rbc[:, d, :].rearrange("p (c t) -> p c t", c=4),
                                                      tri[:, d:d + 1, :].to_broadcast([P, 4, P]), ALU.add)
                    ins.then_inc(s["rmask_done"], 1)

                def weigh(c):
                    dve.wait_ge(s["e_done"], h * 4 + (c + 1))
                    dve.wait_ge(s["qkt_done"], h * 4 + (c + 2))
                    pb = ps[:, 6 + c % 2, :]
                    fo = (0, 4, 7, 9)[c] * P
                    bo = (0, 1, 3, 6)[c] * P
                    wf = wmat[:, 0, fo:fo + (4 - c) * P]
                    wb = wmat[:, 1, bo:bo + (c + 1) * P]
                    nc.vector.tensor_tensor(wf, pb[:, c * P:S], wf, ALU.mult)
                    nc.vector.tensor_tensor(wb, pb[:, 0:(c + 1) * P], wb, ALU.mult).then_inc(s["w_done"], 1)

                def normalise(tc):
                    dve.wait_ge(s["pv_done"], h * 4 + (tc + 2))
                    b0 = 4 + 2 * (tc % 2)
                    den = ps[:, b0:b0 + 2, 256:257].rearrange("p d o -> p (d o)")
                    em = bias_s[:, 128:160].rearrange("p (d t h) -> p d t h", d=2, t=4)[:, :, tc, bass.ds(h, 1)].rearrange("p d o -> p (d o)")
                    mlink(nc.vector.scalar_tensor_tensor(dn[:, :], den, -1.0, em, ALU.mult, ALU.max))
                    mlink(nc.vector.tensor_tensor(dn[:, :], dn[:, :], den, ALU.max))
                    mlink(nc.vector.reciprocal(dn[:, :], dn[:, :]))
                    mlink(nc.vector.tensor_scalar(htok[:, tc, :], ps[:, b0, 0:256], dn[:, 0:1], None, ALU.mult))
                    nc.vector.scalar_tensor_tensor(htok[:, tc, :], ps[:, b0 + 1, 0:256], dn[:, 1:2], htok[:, tc, :],
                                                   ALU.mult, ALU.add).then_inc(s["pv_free"], 1)
                    dve.wait_ge(s["pv_free"], h * 4 + (tc + 2))
                    mlink(nc.vector.bn_stats(st[:, tc, 0, :], htok[:, tc, :]))

                def variance():
                    dve.sem_inc(s["dve_mark"], 1)
                    for tc in range(4):
                        ins = nc.vector.bn_aggr(mv[:, tc, :], st[:, tc, 0, :])
                    mlink(ins)
                    nc.vector.tensor_scalar(veps[:, :], mv[:, :, 1], EPS, None, ALU.add).then_inc(s["var_done"], 1)

                def standardise():
                    dve.wait_ge(s["std_done"], h + 1)
                    mlink(nc.vector.reciprocal(rstd[:, :], rstd[:, :]))
                    for tc in range(4):
                        ins = nc.vector.tensor_scalar(htok[:, tc, :], htok[:, tc, :], mv[:, tc, 0:1], rstd[:, tc:tc + 1],
                                                      ALU.subtract, ALU.mult)
                    ins.then_inc(s["hn_done"], 1)

                def y_gate():
                    for b in range(2):
                        dve.wait_ge(s["yps_done"], h * 2 + (b + 1))
                        nc.vector.scalar_tensor_tensor(yt[:, b, :], ps[:, 4 + b, :], par[:, bass.ds(h * 2 + (PAR_NW + b), 1)], ot[:, b, :],
                                                       ALU.mult, ALU.mult).then_inc(s["y_mul"], 1)

                def y_low():
                    for b in range(2):
                        dve.wait_ge(s["yhi_done"], h * 2 + (b + 1))
                        at = h * 2 + b
                        nc.vector.tensor_tensor(blk_of(yml_lo, at), yt[:, b, :], blk_of(yml_hi, at).bitcast(F32),
                                                ALU.subtract).then_inc(s["ylo_done"], 1)
                    assert mlink.k == ML_LINKS

                return {0: [mask_rows], 2: [lambda: weigh(0)], 3: [lambda: weigh(1)], 5: [lambda: weigh(2)], 6: [lambda: weigh(3)],
                        8: [lambda: normalise(0)], 9: [lambda: normalise(1)], 10: [lambda: normalise(2)],
                        11: [lambda: normalise(3), variance], 12: [standardise], 14: [y_gate], 15: [y_low]}

            ml_projections(0, gate_hooks, first=4)
            dve.wait_ge(s["const_in"], 16)
            with dve.Fori(0, ML_H - 1) as h:
                ml_projections(h + 1, mlstm(h))

            nlink = Chain(dve, s["link_na"])
            NA_LINKS = 8

            def na_units(ub, n, hooks):
                for u in range(8):
                    lo(ub, 8 * n + u + HL)
                    do(hooks, u)

            def softmax(i, pr, at):
                def shifted(hh):
                    nlink.loop(i * (2 * NA_LINKS) + (NA_LINKS * pr + 3 * hh))
                    if pr == 0 and hh == 0:
                        dve.wait_ge(s["table_in"], (i + 1) * (16 * 2 * ROWS))
                    dve.wait_ge(s["s_done"], i * 4 + (2 * pr + hh + 1))
                    for j in range(NJ):
                        shift = KSTART[j] - QCOLS * j + WIN_COLS
                        head = table[:, 2 * pr + hh, shift:shift + 1]
                        bias = bass.AP(head.tensor, head.offset, [list(head.ap[0]), [STRIP, 4], [RPB_C, ROWS], [1, STRIP]])
                        ins = nc.vector.tensor_tensor(strips(sc[:, hh, j, :]),
                                                      strips(ps[:, 4 + 2 * hh + j // 2, (j % 2) * 256:(j % 2) * 256 + 256]),
                                                      bias, ALU.add)
                    nlink(ins)
                    nlink(nc.vector.tensor_tensor(sc[:, hh, :, :], sc[:, hh, :, :], namask[:, :, :], ALU.min))
                    nlink(nc.vector.reduce_max(smax[:, hh, :], sc[:, hh, :, :], AX.X))
                    nc.vector.tensor_scalar(smax[:, hh, :], smax[:, hh, :], -1.0, None, ALU.mult).then_inc(s["smx_done"], 1)

                def divided(hh):
                    nlink.loop(i * (2 * NA_LINKS) + (NA_LINKS * pr + 6 + hh))
                    dve.wait_ge(s["pexp_done"], i * 4 + (2 * pr + hh + 1))
                    nlink(nc.vector.reciprocal(ssum[:, hh, :], ssum[:, hh, :]))
                    for j in range(NJ):
                        ins = nc.vector.tensor_scalar(sc[:, hh, j, :], sc[:, hh, j, :], ssum[:, hh, j:j + 1], None, ALU.mult)
                    ins.then_inc(s["p_done"], 1)

                return {at: [lambda: shifted(0)], at + 1: [lambda: shifted(1)], at + 2: [lambda: divided(0)],
                        at + 3: [lambda: divided(1)]}

            def y_out(i, pr):
                dve.wait_ge(s["yna_h"], i * 2 + (pr + 1))
                at = i * 2 + pr
                nc.vector.tensor_tensor(by_strip(blk_of(yna_lo, at)), strips(ps[:, 4, :])[:, :, :, ::-1],
                                        by_strip(blk_of(yna_hi, at).bitcast(F32)), ALU.subtract).then_inc(s["yna_l"], 1)

            def plus(*all_hooks):
                out = {}
                for hooks in all_hooks:
                    for u, steps in hooks.items():
                        out.setdefault(u, []).extend(steps)
                return out

            last_head = mlstm(ML_H - 1)
            na_units(U_NA, 0, {u: f for u, f in last_head.items() if u < 8})
            na_units(U_NA, 1, {u - 8: f for u, f in last_head.items() if u >= 8})
            dve.wait_ge(s["mask_in"], 16)
            na_units(U_NA, 2, softmax(0, 0, 2))
            with dve.Fori(1, 4) as i:
                ub = i * 24 + U_NA
                na_units(ub, 0, plus({0: [lambda: y_out(i - 1, 0)]}, softmax(i - 1, 1, 1)))
                na_units(ub, 1, {1: [lambda: y_out(i - 1, 1)]})
                na_units(ub, 2, softmax(i, 0, 0))

            link = Chain(dve, s["link_mg"])
            def merge(i, hooks):
                link.loop(i * 2)
                ub = i * 24 + U_MG
                for half in range(2):
                    for k in range(12):
                        lo(ub, 12 * half + k + HL)
                        do(hooks, 12 * half + k)
                    dve.wait_ge(unit_used, ub + (12 * (half + 1) + HL))
                    dve.wait_ge(s["merge_sg"], i * 2 + (half + 2))
                    nc.vector.tensor_tensor(mt[:, 0, :], ps[:, 3, :], mg[:, 0, :], ALU.mult)
                    link(nc.vector.tensor_tensor(mt[:, 1, :], ps[:, 2, :], mg[:, 1, :], ALU.mult))
                    nc.vector.tensor_tensor(blk_of(mixed, i * 2 + half), mt[:, 0, :], mt[:, 1, :],
                                            ALU.add).then_inc(s["mix_done"], 1)

            merge(0, plus({0: [lambda: y_out(3, 0)]}, softmax(3, 1, 1), {9: [lambda: y_out(3, 1)]}))
            with dve.Fori(1, KB // 2) as i:
                merge(i, {})
            for kb in range(KB):
                dve.wait_ge(s["mxhi_done"], kb + 1)
                nc.vector.tensor_tensor(mx_lo[:, kb, :], mixed[:, kb, :], mx_hi[:, kb, :].bitcast(F32),
                                        ALU.subtract).then_inc(s["mxlo_done"], 1)

            dve.wait_ge(s["res_in"], 16)
            link = Chain(dve, s["link_wo"])
            with dve.Fori(0, 2) as i:
                link.loop(i * 2)
                for half in range(2):
                    for k in range(KB):
                        lo(i * 32 + U_WO, 16 * half + k + HL)
                    dve.wait_ge(unit_used, i * 32 + (U_WO + 16 * (half + 1) + HL))
                    for t in range(TT):
                        at = bass.ds(i * 1024 + half * 512, 512)
                        ins = nc.vector.scalar_tensor_tensor(res[:, t, at], res[:, t, at], ALPHA, ps[:, 4 - 4 * half + t, :],
                                                             ALU.mult, ALU.add)
                    ins.then_inc(s["wo_free"], 1)
                    dve.wait_ge(s["wo_free"], i * 2 + (half + 2) + 1)
                    for t in range(TT):
                        ins = nc.vector.bn_stats(st[:, t, :, :].rearrange("p n c -> p (n c)")[:, bass.ds(i * 12 + half * 6, 6)], res[:, t, at])
                    link(ins)
            link = Chain(dve, s["link_ff"])

            def norm_stats(var, std, ready):
                for t in range(TT):
                    ins = nc.vector.bn_aggr(mv[:, t, :], st[:, t, :, :].rearrange("p a b -> p (a b)"))
                link(ins)
                nc.vector.tensor_scalar(veps[:, :], mv[:, :, 1], EPS, None, ALU.add).then_inc(var, 1)
                dve.wait_ge(std, 1)
                link(nc.vector.reciprocal(rstd[:, :], rstd[:, :]))
                nc.vector.scalar_tensor_tensor(nmu[:, :], mv[:, :, 0], -1.0, rstd[:, :], ALU.mult, ALU.mult).then_inc(ready, 1)

            norm_stats(s["ln1_var"], s["ln1_std"], s["ln1_hn"])
            for kb in range(KB):
                dve.wait_ge(s["ht_hi_d"], kb + 1)
                f = ft[:, kb % 2, :]
                link(nc.vector.tensor_scalar(f, ps[:, 4 + kb % 4, :], par[:, PAR_G1 + kb:PAR_G1 + kb + 1],
                                             par[:, PAR_B1 + kb:PAR_B1 + kb + 1], ALU.mult, ALU.add))
                nc.vector.tensor_tensor(ht_lo[:, kb, :], f, ht_hi[:, kb, :].bitcast(F32), ALU.subtract).then_inc(s["ht_lo_d"], 1)

            link = Chain(dve, s["link_u"])

            def ffn_block(n, c, w0, w2, slot):
                f, pg = ft[:, c % 2, :], ps[:, 2 * c, :]
                dve.wait_ge(s["u_conv"], n + 1)
                link(nc.vector.scalar_tensor_tensor(f[:, 1:S], pg[:, 0:S - 1], w0, f[:, 1:S], ALU.mult, ALU.add))
                nc.vector.scalar_tensor_tensor(f[:, 0:S - 1], pg[:, 1:S], w2, f[:, 0:S - 1], ALU.mult, ALU.add).then_inc(s["u_conv2"], 1)
                dve.wait_ge(s["u_gelu"], n + 1)
                nc.vector.tensor_tensor(f, ps[:, 2 * c + 1, :], fg[:, c % 2, :], ALU.mult).then_inc(s["u_mul"], 1)
                dve.wait_ge(s["u_hi"], n + 1)
                nc.vector.tensor_tensor(blk_of(ac_lo, slot), ft[:, c % 2, :], blk_of(ac_hi, slot).bitcast(F32),
                                        ALU.subtract).then_inc(s["act_done"], 1)

            def accumulate(n_cols, b0):
                for t in range(TT):
                    ins = nc.vector.tensor_tensor(res[:, t, n_cols], res[:, t, n_cols], ps[:, b0 + t, :], ALU.add)
                ins.then_inc(s["d_free"], 1)

            with dve.Fori(0, NG) as g:
                with dve.Fori(0, 2) as i:
                    link.loop(g * 8 + i * 4)
                    for c in range(4):
                        for k in range(8):
                            lo(g * 96 + i * 32 + U_FF, 8 * c + k + HL)
                        blk = g * 8 + i * 4 + c
                        ffn_block(blk, c, par[:, bass.ds(blk + PAR_FW, 1)], par[:, bass.ds(blk + (PAR_FW + 2 * FB), 1)],
                                  i * 4 + c)
                dve.wait_ge(s["res_acc"], TT)
                with dve.Fori(0, 2) as i:
                    for half in range(2):
                        for k in range(8):
                            lo(g * 96 + i * 16 + (U_FF + 64), 8 * half + k + HL)
                        dve.wait_ge(unit_used, g * 96 + i * 16 + (U_FF + 64 + 8 * (half + 1) + HL))
                        accumulate(bass.ds(i * 1024 + half * 512, 512), 4 * half)
            link.loop(NG * 8)
            for c in range(TAIL):
                for k in range(8):
                    lo(U_TL, 8 * c + k + HL)
                blk = NG * G + c
                ffn_block(blk, c, par[:, PAR_FW + blk:PAR_FW + blk + 1], par[:, PAR_FW + 2 * FB + blk:PAR_FW + 2 * FB + blk + 1],
                          c)
            for n in range(4):
                for k in range(TAIL):
                    lo(U_TL, 8 * TAIL + n * TAIL + k + HL)
                dve.wait_ge(unit_used, U_TL + 8 * TAIL + TAIL * (n + 1) + HL)
                accumulate(slice(n * 512, (n + 1) * 512), 4 * (n % 2))
                dve.wait_ge(s["d_free"], 4 * NG + n + 2 + 1)
                for t in range(TT):
                    ins = nc.vector.bn_stats(st[:, t, n, :], res[:, t, n * 512:(n + 1) * 512])
                link(ins)
            link = Chain(dve, s["link_y"])
            dve.wait_ge(s["gb_bc"], 64)
            norm_stats(s["ln2_var"], s["ln2_std"], s["ln2_hn"])
            for t in range(TT):
                dve.wait_ge(s["hn_rows"], t + 1)
                link(nc.vector.tensor_tensor(res[:, t, :], res[:, t, :], g2b[:, :], ALU.mult))
                nc.vector.tensor_tensor(res[:, t, :], res[:, t, :], b2b[:, :], ALU.add).then_inc(s["ln2_y"], 1)

        @block.tensor
        def _(pe):
            mm = nc.tensor.matmul

            def transpose(o, i, rows=P):
                return nc.tensor.transpose(o, i, ident[0:rows, 0:rows])

            def unit_ready(ub, k):
                pe.wait_ge(w_lo_ready, ub + k + 1 + RAW)

            def three(o, a_hi, a_lo, b_hi, b_lo, first, last):
                mm(o, a_hi, b_hi, start=first, stop=False)
                mm(o, a_hi, b_lo, start=False, stop=False)
                return mm(o, a_lo, b_hi, start=False, stop=last)

            def two_by_two(ub, k, ko, bank, act_hi, act_lo):
                unit_ready(ub, k)
                for kk in range(2):
                    for o in range(2):
                        cols = slice((2 * kk + o) * P, (2 * kk + o + 1) * P)
                        kb = 2 * ko + kk
                        last = three(ps[:, bank + o, :], whi[:, k % HL, cols], wlo[:, k % HL, cols],
                                     act_hi[:, kb, :], act_lo[:, kb, :], kb == 0, kb == KB - 1)
                last.then_inc(unit_used, 1)

            def four_by_one(ub, k, kq, n_kb, o, act_hi, act_lo):
                unit_ready(ub, k)
                for kk in range(4):
                    kb = 4 * kq + kk
                    cols = slice(kk * P, (kk + 1) * P)
                    last = three(o, whi[:, k % HL, cols], wlo[:, k % HL, cols], act_hi[:, kb, :], act_lo[:, kb, :],
                                 kb == 0, kb == n_kb - 1)
                last.then_inc(unit_used, 1)

            def one_by_four(ub, k, kb, n_kb, bank, act_hi, act_lo):
                unit_ready(ub, k)
                for t in range(TT):
                    ts = slice(t * P, (t + 1) * P)
                    last = three(ps[:, bank + t, :], act_hi[:, kb, ts], act_lo[:, kb, ts],
                                 whi[:, k % HL, :], wlo[:, k % HL, :], kb == 0, kb == n_kb - 1)
                last.then_inc(unit_used, 1)

            def do(hooks, u):
                for step in hooks.get(u, ()):
                    step()

            def x_columns(n):
                pe.wait_ge(x_in[n], 16)
                for kb in range(4 * n, 4 * n + 4):
                    if kb >= 4:
                        pe.wait_ge(s["xt_lo_done"], kb - 3)
                    for t in range(TT):
                        last = transpose(ps[:, 4 + kb % 4, t * P:(t + 1) * P], x_tok[:, t, kb * P:(kb + 1) * P])
                    last.then_inc(s["xt_ps"], 1)

            def columns():
                pe.wait_ge(s["par_in"], 16 * 11)
                pe.wait_ge(s["xt_lo_done"], KB)
                for i, w in enumerate((PAR_B1 + 16, 2 * FB, 2 * FB)):
                    last = transpose(ps[:, 7, i * P:i * P + w], prow[0:w, i, :], w)
                last.then_inc(s["par_ps"], 1)

            def gates():
                pe.wait_ge(s["wg_lo_done"], 1)
                pe.wait_ge(s["par_done"], 1)
                for kb in range(KB):
                    last = three(ps[:, 4, :], wg_hi[:, kb, :], wg_lo[:, kb, :], xt_hi[:, kb, :], xt_lo[:, kb, :],
                                 kb == 0, kb == KB - 1)
                last.then_inc(s["gate_rows"], 1)

            def exponent_columns():
                pe.wait_ge(s["rows_a"], 1)
                pe.wait_ge(s["em_row"], 1)
                for d in range(2):
                    for c in range(4):
                        cs = slice(c * P, (c + 1) * P)
                        for dist in range(4):
                            at = ((d * 4 + c) * 4 + dist) * 4
                            transpose(ps[:, 4, at:at + 4], row_a[:, d, dist, cs], ML_H)
                        at = 128 + (d * 4 + c) * 4
                        last = transpose(ps[:, 4, at:at + 4], ex[:, d, cs], ML_H)
                last.then_inc(s["cols_ps"], 1)

            def ml_projections(h, hooks, ahead={}):
                ub = h * 32 + U_ML
                for c, (free, n) in enumerate((("free_v", 1), ("free_o", 1), ("conv_b", 2), ("conv_b", 4))):
                    pe.wait_ge(s[free], h * (1 if c < 2 else 4) + n)
                    for k in range(8):
                        do(ahead, 8 * c + k)
                        two_by_two(ub, 8 * c + k, k, 2 * (c % 2), xt_hi, xt_lo)
                        do(hooks, 8 * c + k)

            def mlstm(h):
                def v_token_major():
                    pe.wait_ge(s["free_v"], h + 2)
                    pe.wait_ge(s["y_mul"], h * 2 + 1)
                    for b in range(2):
                        for c in range(TT):
                            last = transpose(ps[:, 4 + c // 2, (c % 2) * 256 + b * P:(c % 2) * 256 + (b + 1) * P],
                                             vt[:, b, c * P:(c + 1) * P])
                    last.then_inc(s["vtr_done"], 1)

                def scores(c):
                    if c == 0:
                        pe.wait_ge(s["qk_done"], h * 4 + 5)
                        pe.wait_ge(s["pv_free"], h * 4 + 1)
                    if c >= 2:
                        pe.wait_ge(s["w_done"], h * 4 + c)
                    for b in range(2):
                        last = mm(ps[:, 6 + c % 2, :], kt[:, b, c * P:(c + 1) * P], qt[:, b, :], start=b == 0, stop=b == 1)
                    last.then_inc(s["qkt_done"], 1)

                def values(tc):
                    if tc == 0:
                        pe.wait_ge(s["vtok_done"], h + 1)
                        pe.wait_ge(s["w_done"], h * 4 + 5)
                    b0 = 4 + 2 * (tc % 2)
                    if tc >= 2:
                        pe.wait_ge(s["pv_free"], h * 4 + tc)
                    for d in range(2):
                        cs = list(range(tc + 1)) if d == 0 else list(range(tc, 4))
                        for c in cs:
                            slot = (0, 4, 7, 9)[c] + tc - c if d == 0 else (0, 1, 3, 6)[c] + tc
                            last = mm(ps[:, b0 + d, 0:257], wmat[:, d, slot * P:(slot + 1) * P], vtok[:, c, 0:257],
                                      start=c == cs[0], stop=c == cs[-1])
                    last.then_inc(s["pv_done"], 1)

                def y_feature_major():
                    pe.wait_ge(s["hn_done"], h + 1)
                    for b in range(2):
                        for tc in range(4):
                            last = transpose(ps[:, 4 + b, tc * P:(tc + 1) * P], htok[:, tc, b * P:(b + 1) * P])
                        last.then_inc(s["yps_done"], 1)

                return {0: [v_token_major, lambda: scores(0)], 1: [lambda: scores(1)], 3: [lambda: scores(2)], 5: [lambda: scores(3)],
                        7: [lambda: values(0)], 8: [lambda: values(1)], 9: [lambda: values(2)], 10: [lambda: values(3)],
                        13: [y_feature_major]}

            pe.wait_ge(s["ident_in"], 16)
            ml_projections(0, {8: [gates], 20: [exponent_columns]},
                           {0: [lambda: x_columns(0)], 1: [lambda: x_columns(1)], 3: [lambda: x_columns(2)],
                            5: [lambda: x_columns(3)], 6: [columns]})
            pe.wait_ge(s["cols_done"], 1)
            with pe.Fori(0, ML_H - 1) as h:
                ml_projections(h + 1, mlstm(h))

            def na_v(i, hooks):
                for k in range(8):
                    if k % 4 == 0:
                        if isinstance(i, int):
                            pe.wait_ge(s["free_v"], ML_H + 1)
                        else:
                            pe.wait_ge(s["na_qk_done"], i * 4 + k // 4)
                    four_by_one(i * 24 + U_NA, k, k % 4, KB, ps[:, k // 4, :], xt_hi, xt_lo)
                    do(hooks, k)

            def na_qk(i, pr, hooks):
                for k in range(8):
                    if pr and k % 4 == 0:
                        pe.wait_ge(s["na_v_done"], i * 2 + (k // 4 + 1))
                    four_by_one(i * 24 + U_NA, 8 + 8 * pr + k, k % 4, KB, ps[:, (2, 0)[pr] + k // 4, :], xt_hi, xt_lo)
                    do(hooks, k)

            def v_tiles(i):
                pe.wait_ge(s["na_v_done"], i * 2 + 2)
                pe.wait_ge(s["yna_l"], i * 2 + 1)
                pe.wait_ge(s["y_mul"], 2 * ML_H + 1)
                for t in range(7):
                    first = P * t if t < 4 else ROWS * STRIP + P * (t - 4)
                    for pr in range(2):
                        last = transpose(ps[:, 4 + t // 2, (t % 2) * 256 + pr * P:(t % 2) * 256 + (pr + 1) * P],
                                         nvt[:, pr, first:first + P])
                last.then_inc(s["na_vt_ps"], 1)

            def attend(i, pr, at):
                def na_scores():
                    pe.wait_ge(s["na_v7"], i + 1)
                    pe.wait_ge(s["na_qk_done"], i * 4 + (2 * pr + 3))
                    pe.wait_ge(s["yna_l"], i * 2 + (pr + 1))
                    for hh in range(2):
                        hp = slice(64 * hh, 64 * hh + 64)
                        for j in range(NJ):
                            last = mm(ps[:, 4 + 2 * hh + j // 2, (j % 2) * 256:(j % 2) * 256 + 256],
                                      qk[hp, 0, P * j:P * (j + 1)], qk[hp, 1, ROWS * KSTART[j]:ROWS * KSTART[j] + 256],
                                      start=True, stop=True)
                        last.then_inc(s["s_done"], 1)

                def probabilities(hh):
                    pe.wait_ge(s["p_done"], i * 4 + (2 * pr + hh + 1))
                    for j in range(NJ):
                        for half in range(2):
                            last = transpose(ps[:, 4 + 2 * hh + j // 2, (2 * (j % 2) + half) * P:(2 * (j % 2) + half + 1) * P],
                                             sc[:, hh, j, half * P:(half + 1) * P])
                    last.then_inc(s["pt_ps"], 1)

                return {at: [na_scores], at + 4: [lambda: probabilities(0)], at + 5: [lambda: probabilities(1)]}

            def na_values(i, pr):
                for hh in range(2):
                    pe.wait_ge(s["pt_done"], i * 4 + (2 * pr + hh + 1))
                    for j in range(NJ):
                        tiles = ((0, 1), (4, 5), (5, 6), (2, 3))[j]
                        for half in range(2):
                            last = mm(ps[64 * hh:64 * hh + 64, 4, j * P:(j + 1) * P],
                                      v7[:, tiles[half], pr * P + 64 * hh:pr * P + 64 * hh + 64],
                                      pt[:, hh, 2 * j + half, :], start=half == 0, stop=half == 1)
                last.then_inc(s["ypv_done"], 1)

            def plus(*all_hooks):
                out = {}
                for hooks in all_hooks:
                    for u, steps in hooks.items():
                        out.setdefault(u, []).extend(steps)
                return out

            last_head = mlstm(ML_H - 1)
            na_v(0, {u: f for u, f in last_head.items() if u < 8})
            pe.wait_ge(s["free_o"], ML_H + 1)
            na_qk(0, 0, {u - 8: f for u, f in last_head.items() if u >= 8})
            na_qk(0, 1, plus({0: [lambda: v_tiles(0)]}, attend(0, 0, 2)))
            with pe.Fori(1, 4) as i:
                na_v(i, plus({0: [lambda: na_values(i - 1, 0)]}, attend(i - 1, 1, 1)))
                na_qk(i, 0, {1: [lambda: na_values(i - 1, 1)], 3: [lambda: v_tiles(i)]})
                na_qk(i, 1, attend(i, 0, 0))
            pe.wait_ge(s["na_qk_done"], 4 * 4 + 1)

            def merge(i, hooks):
                ub = i * 24 + U_MG
                for half in range(2):
                    pe.wait_ge(s["merge_sg"], i * 2 + (half + 1))
                    for k in range(8):
                        four_by_one(ub, 12 * half + k, k % 4, KB, ps[:, k // 4, :], xt_hi, xt_lo)
                        do(hooks, 12 * half + k)
                    pe.wait_ge(s["mix_done"], i * 2 + (half + 1))
                    for k in range(8, 12):
                        if hooks and half == 0:
                            pe.wait_ge(s["ylo_done"], 2 * ML_H + 1)
                            if k == 10:
                                pe.wait_ge(s["yna_l"], 9)
                        y_hi, y_lo = ((yml_hi, yml_lo), (yna_hi, yna_lo))[(k - 8) // 2]
                        four_by_one(ub, 12 * half + k, k % 2, 8, ps[:, 2 + (k - 8) // 2, :], y_hi, y_lo)
                        do(hooks, 12 * half + k)

            merge(0, plus({0: [lambda: na_values(3, 0)]}, attend(3, 1, 1), {8: [lambda: na_values(3, 1)]}))
            with pe.Fori(1, KB // 2) as i:
                merge(i, {})

            with pe.Fori(0, 2) as i:
                for half in range(2):
                    pe.wait_ge(s["wo_free"], i * 2 + half + 1)
                    for k in range(KB):
                        pe.wait_ge(s["mxlo_done"], k + 1)
                        one_by_four(i * 32 + U_WO, 16 * half + k, k, KB, 4 - 4 * half, mx_hi, mx_lo)
            for kb in range(KB):
                pe.wait_ge(s["hn_cols"], kb // 4 + 1)
                if kb >= 4:
                    pe.wait_ge(s["ht_lo_d"], kb - 3)
                for t in range(TT):
                    last = transpose(ps[:, 4 + kb % 4, t * P:(t + 1) * P], res[:, t, kb * P:(kb + 1) * P])
                last.then_inc(s["ht_ps"], 1)

            with pe.Fori(0, NG) as g:
                with pe.Fori(0, 2) as i:
                    for c in range(4):
                        pe.wait_ge(s["d_free"], g * 4 + c // 2 + 1)
                        pe.wait_ge(s["u_mul"], g * 8 + i * 4 + (c + 1))
                        for k in range(8):
                            if c == 0:
                                pe.wait_ge(s["ht_lo_d"], 4 * (k % 4) + 4)
                            four_by_one(g * 96 + i * 32 + U_FF, 8 * c + k, k % 4, KB, ps[:, 2 * c + k // 4, :], ht_hi, ht_lo)
                with pe.Fori(0, 2) as i:
                    for half in range(2):
                        pe.wait_ge(s["u_mul"], g * 8 + (10, 12)[half])
                        pe.wait_ge(s["d_free"], g * 4 + i * 2 + half + 1)
                        for k in range(G):
                            pe.wait_ge(s["act_done"], g * 8 + (k + 3))
                            one_by_four(g * 96 + i * 16 + (U_FF + 64), 8 * half + k, k, G, 4 * half, ac_hi, ac_lo)
            for c in range(TAIL):
                pe.wait_ge(s["d_free"], NG * 4 + c // 2 + 1)
                for k in range(8):
                    four_by_one(U_TL, 8 * c + k, k % 4, KB, ps[:, 2 * c + k // 4, :], ht_hi, ht_lo)
            for n in range(4):
                pe.wait_ge(s["u_mul"], NG * 8 + 4 + (2, 3)[n % 2] if n < 2 else NG * 8 + 7)
                pe.wait_ge(s["d_free"], NG * 4 + n + 1)
                for k in range(TAIL):
                    pe.wait_ge(s["act_done"], NG * 8 + k + 3)
                    one_by_four(U_TL, 8 * TAIL + n * TAIL + k, k, TAIL, 4 * (n % 2), ac_hi, ac_lo)


_INS = ["x", "w_in", "na_rpb", "ml_conv_w", "ml_conv_b", "ml_igate_b", "ml_fgate_b", "ml_norm_w", "w_branch_na",
        "w_branch_ml", "w_out", "ln1_g", "ln1_b", "ffn_w_up", "ffn_conv_w", "ffn_conv_b", "ffn_w_down", "ln2_g", "ln2_b"]


def shape_constants():
    c = np.zeros((P, 3 * P + NJ * 256), np.float32)
    c[:, 0:P] = np.eye(P)
    a, b = np.arange(P)[:, None], np.arange(P)[None, :]
    c[:, P:2 * P] = np.where(a <= b, 0.0, NEG)
    c[:, 2 * P:3 * P] = np.where(a >= b, 0.0, NEG)
    for j in range(NJ):
        p, f = np.arange(P)[:, None], np.arange(256)[None, :]
        q = QCOLS * j + STRIP * (p // (ROWS * STRIP)) + STRIP - 1 - p % STRIP
        k = KSTART[j] + STRIP * (f // (ROWS * STRIP)) + f % STRIP
        w = np.clip(q - WIN_COLS // 2, 0, GRID_W - WIN_COLS)
        c[:, 3 * P + j * 256:3 * P + (j + 1) * 256] = np.where((k >= w) & (k < w + WIN_COLS), 3e38, NEG)
    return c


def kernel(**inputs):
    import concourse.bacc as bacc
    from concourse.bass_utils import run_bass_kernel_spmd

    nc = bacc.Bacc("TRN2", target_bir_lowering=False, num_devices=1)
    arrays, args = {}, []
    for name in _INS:
        a = np.ascontiguousarray(inputs[name])
        arrays["in_" + name] = a
        args.append(nc.dram_tensor("in_" + name, a.shape, mybir.dt.from_np(a.dtype), kind="ExternalInput").ap())
    consts = shape_constants()
    arrays["in_consts"] = consts
    args.append(nc.dram_tensor("in_consts", consts.shape, F32, kind="ExternalInput").ap())
    out = nc.dram_tensor("out_0", (1, S, D), F32, kind="ExternalOutput").ap()
    build(nc, *args, out)
    r = run_bass_kernel_spmd(nc, [arrays], core_ids=[0])
    return r.results[0]["out_0"]
```

```python
import math
import numpy as np
import concourse.bass as bass
from concourse import mybir
from contextlib import ExitStack

F32 = mybir.dt.float32
F32R = mybir.dt.float32r
ACT = mybir.ActivationFunctionType
ALU = mybir.AluOpType
AX = mybir.AxisListType

P = 128
S = 512
D = 2048
KB = D // P
TT = S // P
GRID_W = 64
ROWS = S // GRID_W
QCOLS = 16
KCOLS = 32
WIN_COLS = 16
STRIP = 8
NJ = GRID_W // QCOLS
KSTART = [min(max(QCOLS * j - WIN_COLS // 2, 0), GRID_W - KCOLS) for j in range(NJ)]
NA_W = 1024
NA_H = 16
ML_W = 1024
ML_H = 4
DFF = 5504
FB = DFF // P
G = 8
NG = FB // G
TAIL = FB - NG * G
RPB_R, RPB_C = 15, 31
RPB_HEAD = RPB_R * RPB_C
TABLE = 7 * RPB_C + KCOLS + WIN_COLS
PAD = 16
NEG = -1e30
EPS = 1e-5
ALPHA = 2 ** 0.25
RAW, HL = 8, 4

POOL_HALVES = ((0, 0), (0, 1), (1, 1))
DVE_HALVES = ((1, 0), (2, 0), (2, 1), (3, 0), (3, 1))

X_PIECES = ((0, 2), (2, 2), (4, 4), (8, 4), (12, 4))

C_MLQ, C_MLK, C_MLV, C_MLO = (3 * NA_W + n * ML_W for n in range(4))
C_GATE = 3 * NA_W + 4 * ML_W
C_MERGE = C_GATE + 4 * ML_H

U_ML = 0
U_NA = U_ML + ML_H * 32
U_MG = U_NA + 4 * 24
U_WO = U_MG + 16 * 12
U_FF = U_WO + 4 * KB
U_TL = U_FF + NG * (8 * G + 4 * G)
U_END = U_TL + TAIL * 8 + 4 * TAIL

PAR_MLW, PAR_MLB, PAR_NW, PAR_G1, PAR_B1 = 0, 48, 64, 72, 88
PAR_FW, PAR_FB = 128, 128 + 3 * FB
PAR_OFF = (0, PAR_FW, PAR_FW + 2 * FB)


FWD_AT = (0, 4, 7, 9)
BWD_AT = (0, 1, 3, 6)


def do(hooks, u):
    for step in hooks.get(u, ()):
        step()


def plus(*all_hooks):
    out = {}
    for hooks in all_hooks:
        for u, steps in hooks.items():
            out.setdefault(u, []).extend(steps)
    return out


def build(nc, x, w_in, na_rpb, ml_conv_w, ml_conv_b, ml_igate_b, ml_fgate_b, ml_norm_w, w_bna, w_bml,
          w_out, ln1_g, ln1_b, w_up, ffn_conv_w, ffn_conv_b, w_down, ln2_g, ln2_b, consts, out):
    ctx = ExitStack()
    with ctx:
        K = 1024
        ARENA = 16640

        def sb(name, shape, offset, dt=F32):
            return nc.alloc_sbuf_tensor_at(name, shape, dt, offset=ARENA + int(offset))

        def sem(name):
            return ctx.enter_context(nc.semaphore(name))

        raw = sb("raw", [P, RAW, 512], 0)
        whi = sb("whi", [P, HL, 512], 16 * K, F32R)
        wlo = sb("wlo", [P, HL, 512], 24 * K, F32R)
        xt_hi = sb("xt_hi", [P, KB, S], 32 * K, F32R)
        xt_lo = sb("xt_lo", [P, KB, S], 64 * K, F32R)
        yml_hi = sb("yml_hi", [P, 8, S], 96 * K, F32R)
        yml_lo = sb("yml_lo", [P, 8, S], 112 * K, F32R)
        yna_hi = sb("yna_hi", [P, 8, S], 128 * K, F32R)
        yna_lo = sb("yna_lo", [P, 8, S], 144 * K, F32R)
        x_tok = sb("x_tok", [P, TT, D], 96 * K)
        row_a = sb("row_a", [ML_H, 2, 4, S], 128 * K)
        li = sb("li", [ML_H, 2, S], 144 * K)
        lf = sb("lf", [ML_H, 2, S], 148 * K)
        mrow = sb("mrow", [ML_H, 2, S], 152 * K)
        bl = sb("bl", [ML_H, 2, S], 156 * K)
        fx = sb("fx", [ML_H, 2, S], 96 * K)
        ex = sb("ex", [ML_H, 2, S], 100 * K)
        rrow = sb("rrow", [ML_H, 2, S], 104 * K)
        prow = sb("prow", [P, 3, P], 181 * K)
        ones4 = sb("ones4", [ML_H, P], 184 * K)
        wg = sb("wg", [P, KB, 16], 189 * K)
        wg_hi = sb("wg_hi", [P, KB, P], 112 * K, F32R)
        wg_lo = sb("wg_lo", [P, KB, P], 120 * K, F32R)
        wmat = sb("wmat", [P, 2, 10 * P], 128 * K)
        wmat_lo = sb("wmat_lo", [P, 2, 10 * P], 128 * K, F32R)
        wmat_hi = sb("wmat_hi", [P, 2, 10 * P], 148 * K, F32R)
        vtok_lo = sb("vtok_lo", [P, TT, 258], 138 * K, F32R)
        vtok_hi = sb("vtok_hi", [P, TT, 258], 176 * K, F32R)
        htok = sb("htok", [P, TT, 256], 144 * K)
        qt = sb("qt", [P, 2, S], 160 * K)
        kt = sb("kt", [P, 2, S], 164 * K)
        qt_lo = sb("qt_lo", [P, 2, S], 160 * K, F32R)
        kt_lo = sb("kt_lo", [P, 2, S], 164 * K, F32R)
        qt_hi = sb("qt_hi", [P, 2, S], 189 * K, F32R)
        kt_hi = sb("kt_hi", [P, 2, S], 197 * K, F32R)
        vt = sb("vt", [P, 2, S], 168 * K)
        ot = sb("ot", [P, 2, S], 172 * K)
        rbc = sb("rbc", [P, 2, S], 181 * K)
        rmask = sb("rmask", [P, 2, S], 185 * K)
        yt = rmask
        cv = sb("cv", [P, 2, S], 193 * K)
        sg = sb("sg", [P, 2, S], 197 * K)
        qk_hi = sb("qk_hi", [P, 2, S], 160 * K, F32R)
        qk_lo = sb("qk_lo", [P, 2, S], 164 * K, F32R)
        nvt = sb("nvt", [P, 2, S], 164 * K)
        v7 = sb("v7", [P, 7, 256], 168 * K)
        table = sb("table", [P, 4, TABLE + 1], 176 * K)
        sc = sb("sc", [P, 2, NJ, 256], 181 * K)
        pt = sb("pt", [P, 2, 8, P], 193 * K)
        namask = sb("namask", [P, NJ, 256], 189 * K)
        mixed = sb("mixed", [P, KB, S], 160 * K)
        mg = sb("mg", [P, 2, S], 192 * K)
        mt = sb("mt", [P, 2, S], 196 * K)
        mx_hi = sb("mx_hi", [P, KB, S], 32 * K, F32R)
        mx_lo = sb("mx_lo", [P, KB, S], 64 * K, F32R)
        res = sb("res", [P, TT, D], 96 * K)
        ht_hi = sb("ht_hi", [P, KB, S], 128 * K, F32R)
        ht_lo = sb("ht_lo", [P, KB, S], 160 * K, F32R)
        ac_hi = sb("ac_hi", [P, G, S], 32 * K, F32R)
        ac_lo = sb("ac_lo", [P, G, S], 48 * K, F32R)
        g1b = sb("g1b", [P, D], 64 * K)
        b1b = sb("b1b", [P, D], 72 * K)
        g2b = sb("g2b", [P, D], 80 * K)
        b2b = sb("b2b", [P, D], 88 * K)
        ft = sb("ft", [P, 2, S], 192 * K)
        fg = sb("fg", [P, 2, S], 196 * K)
        ident = sb("ident", [P, P], 201 * K)
        tri = sb("tri", [P, 2, P], 201 * K + 512)
        par = sb("par", [P, 3 * P], 202 * K + 512)
        bias_s = sb("bias_s", [P, 160], 204 * K)
        st = sb("st", [P, TT, 4, 6], 204 * K + 640)
        mv = sb("mv", [P, TT, 2], 204 * K + 1024)
        rstd = sb("rstd", [P, TT], 204 * K + 1056)
        nmu = sb("nmu", [P, TT], 204 * K + 1088)
        dn = sb("dn", [P, 2], 204 * K + 1120)
        smax = sb("smax", [P, 2, NJ], 204 * K + 1152)
        ssum = sb("ssum", [P, 2, NJ], 204 * K + 1184)
        gb = sb("gb", [P, 1], 204 * K + 1216)
        zpad = sb("zpad", [1, PAD], 204 * K + 1248)
        veps = sb("veps", [P, TT], 204 * K + 1312)
        rpb_pad = nc.dram_tensor("rpb_pad", [PAD + NA_H * RPB_HEAD + PAD], F32)
        rdram = nc.dram_tensor("rdram", [ML_H, 2 * S], F32)

        def blk_of(tile, n):
            return tile[:, :, :].rearrange("p k s -> p (k s)")[:, bass.ds(n * S, S)]

        def together(tile):
            return tile[:, :, :].rearrange("p k (g c) -> p k g c", g=4)

        def apart(tile):
            return tile[:, :, :].rearrange("p k (g c) -> p k g c", g=4)[:, :, :, 0:ML_H]

        def by_strip(ap):
            return ap.rearrange("p (r b e) -> p b r e", r=ROWS, e=STRIP)

        def strips(ap):
            return ap.rearrange("p (b r e) -> p b r e", r=ROWS, e=STRIP)

        ps = ctx.enter_context(nc.psum_tensor("ps", [P, 8, 512], F32))

        x_in = [sem(f"x_in{n}") for n in range(len(X_PIECES))]
        weights_in = [sem(f"weights_in{i}") for i in range(RAW)]
        w_hi_ready, w_lo_ready, unit_used = sem("w_hi_ready"), sem("w_lo_ready"), sem("unit_used")
        names = """act_done cols_done cols_ps const_in conv_a conv_b conv_sg d_free dve_mark e_done em_row
            exp_fx free_o free_v gate_rows gb_bc gb_in h_own hn_cols_a hn_cols_v hn_done hn_rows ht_hi_d
            ht_lo_d ht_ps ident_in link_conv link_norm1 link_hcols link_mg link_ml link_na link_pool link_ffn
            link_wo link_gates link_norm2 ln1_hn ln1_std ln1_var ln2_hn ln2_std ln2_var ln2_y ln2_y_pool log_fx
            mask_in merge_sg mix_done mxhi_done mxlo_done na_qk_done na_qk_hi na_v7 na_v_done na_vt_ps
            neg_fx ones_set out_done out_done_pool p_done pad_out pad_zero par_done par_in par_ps
            pexp_done pt_done pt_ps pv_done pv_free qk_done qk_hi_done qk_lo_done qkt_done r_in res_acc
            res_in rmask_done rows_a rscr_out s_done smx_done sp_mark std_done sw_hi_done sw_lo_done
            table_in tile_sums u_conv u_conv2 u_gelu u_hi u_mul v_lo_done var_done vtok_done vtr_done
            w_done wg_hi_done wg_in wg_lo_done wg_zero wo_free wo_tiles xt_hi_done xt_lo_done xt_ps
            y_mul yhi_done ylo_done yna_h yna_l yps_done ypv_done""".split()
        s = {n: sem(n) for n in names}

        STARTS_AT_ONE = """w_done qk_done ylo_done vtr_done y_mul pv_done na_vt_ps mix_done qkt_done pv_free
            free_v free_o na_qk_done yna_l merge_sg wo_free d_free""".split()

        def split_hooks(split):
            return {u: [lambda kb=kb: split(kb) for kb in range(KB - 1) if min(19 + kb // 3, 23) == u] for u in range(19, 24)}

        class Chain:
            def __init__(self, eng, semaphore):
                self.eng, self.sem, self.base, self.k = eng, semaphore, 0, 0

            def loop(self, base):
                self.base, self.k = base, 0

            def __call__(self, instruction):
                self.k += 1
                instruction.then_inc(self.sem, 1)
                self.eng.wait_ge(self.sem, self.base + self.k)

        block = ctx.enter_context(nc.Block())
        win = w_in[0]

        @block.sync
        def _(sp):
            def unit(src, shape, u, n, **dims):
                sp.wait_ge(w_lo_ready, u + n + 1)
                sp.sem_inc(s["sp_mark"], 1)
                dst = raw[:, n % RAW, :]
                if shape:
                    dst = dst.rearrange(shape, **dims)
                sp.dma_start(dst, src).then_inc(weights_in[n % RAW], 16)

            wk = win.rearrange("(k p) c -> p k c", p=P)
            with sp.Fori(0, ML_H) as h:
                for c, col in enumerate((C_MLQ, C_MLK, C_MLV, C_MLO)):
                    for k in range(8):
                        unit(wk[:, 2 * k:2 * k + 2, bass.ds(h * 256 + col, 256)], "p (k c) -> p k c",
                             U_ML + h * 32, 8 * c + k, k=2)
            with sp.Fori(0, 4) as i:
                for k in range(8):
                    unit(wk[:, 4 * (k % 4):4 * (k % 4) + 4, bass.ds(i * 256 + (2 * NA_W + P * (k // 4)), P)], "p (k c) -> p k c",
                         U_NA + i * 24, k, k=4)
                for pr in range(2):
                    for k in range(8):
                        unit(wk[:, 4 * (k % 4):4 * (k % 4) + 4, bass.ds(i * 256 + (pr * P + NA_W * (k // 4)), P)], "p (k c) -> p k c",
                             U_NA + i * 24, 8 + 8 * pr + k, k=4)
            wbn = w_bna[0].rearrange("(k p) c -> p k c", p=P)
            wbm = w_bml[0].rearrange("(k p) c -> p k c", p=P)
            with sp.Fori(0, KB // 2) as i:
                for half in range(2):
                    for k in range(8):
                        unit(wk[:, 4 * (k % 4):4 * (k % 4) + 4, bass.ds(i * 256 + (half * P + C_MERGE + D * (k // 4)), P)],
                             "p (k c) -> p k c", U_MG + i * 24, 12 * half + k, k=4)
                    for k in range(4):
                        w = (wbm, wbn)[k // 2]
                        unit(w[:, 4 * (k % 2):4 * (k % 2) + 4, bass.ds(i * 256 + half * P, P)], "p (k c) -> p k c",
                             U_MG + i * 24, 12 * half + 8 + k, k=4)
            with sp.Fori(0, 2) as i:
                for half in range(2):
                    for k in range(KB):
                        unit(w_out[0][k * P:(k + 1) * P, bass.ds(i * 1024 + half * 512, 512)], None,
                             U_WO + i * 32, 16 * half + k)
            wup = w_up[0].rearrange("(k p) c -> p k c", p=P)
            with sp.Fori(0, NG) as g:
                with sp.Fori(0, 2) as i:
                    for c in range(4):
                        for k in range(8):
                            unit(wup[:, 4 * (k % 4):4 * (k % 4) + 4, bass.ds(g * (G * P) + i * 512 + (c * P + DFF * (k // 4)), P)],
                                 "p (k c) -> p k c", U_FF + g * 96 + i * 32, 8 * c + k, k=4)
                with sp.Fori(0, 2) as i:
                    for half in range(2):
                        for k in range(G):
                            unit(w_down[0][bass.ds(g * (G * P) + k * P, P), bass.ds(i * 1024 + half * 512, 512)],
                                 None, U_FF + g * 96 + 64 + i * 16, 8 * half + k)
            for c in range(TAIL):
                for k in range(8):
                    j = NG * G + c
                    first = j * P + DFF * (k // 4)
                    unit(wup[:, 4 * (k % 4):4 * (k % 4) + 4, first:first + P], "p (k c) -> p k c", U_TL, 8 * c + k, k=4)
            for n in range(4):
                for k in range(TAIL):
                    j = NG * G + k
                    unit(w_down[0][j * P:(j + 1) * P, n * 512:(n + 1) * 512], None, U_TL, 8 * TAIL + n * TAIL + k)
            for n, (t, half) in enumerate(DVE_HALVES):
                cs = slice(half * 1024, (half + 1) * 1024)
                sp.wait_ge(s["ln2_y"], n + 1)
                sp.dma_start(out[0, t * P:(t + 1) * P, cs], res[:, t, cs]).then_inc(s["out_done"], 16)
            sp.wait_ge(s["out_done"], 16 * len(DVE_HALVES))

        @block.gpsimd
        def _(pool):
            pool.sem_inc(w_lo_ready, RAW)
            pool.sem_inc(unit_used, HL)
            for n in STARTS_AT_ONE + ["wo_free", "d_free"]:
                pool.sem_inc(s[n], 1)
            pool.sem_inc(s["u_mul"], 4)
            pool.sem_inc(s["act_done"], 2)
            pool.dma_start(tri[:, :, :], consts[:, P:3 * P].rearrange("p (d c) -> p d c", d=2)).then_inc(s["const_in"], 16)
            pool.dma_start(wg[:, :, :], win[:, C_GATE:C_GATE + 16].rearrange("(k p) c -> p k c", p=P)).then_inc(s["wg_in"], 16)
            loads = [(0, PAR_MLW, ml_conv_w[0].rearrange("w (b p) -> w b p", p=P), 3, 16),
                     (0, PAR_MLB, ml_conv_b[0].rearrange("(b p) -> b p", p=P), 0, 16),
                     (0, PAR_NW, ml_norm_w[0].rearrange("(b p) -> b p", p=P), 0, 8),
                     (0, PAR_G1, ln1_g[0].rearrange("(b p) -> b p", p=P), 0, 16),
                     (0, PAR_B1, ln1_b[0].rearrange("(b p) -> b p", p=P), 0, 16),
                     (1, 0, ffn_conv_w[0].rearrange("w (b p) -> w b p", p=P)[0:2], 2, FB),
                     (2, 0, ffn_conv_w[0].rearrange("w (b p) -> w b p", p=P)[2:3], 1, FB),
                     (2, FB, ffn_conv_b[0].rearrange("(b p) -> b p", p=P), 0, FB)]
            for tile, r0, src, w, nb in loads:
                for i in range(max(w, 1)):
                    pool.dma_start(prow[r0 + i * nb:r0 + (i + 1) * nb, tile, :], src[i] if w else src).then_inc(s["par_in"], 16)
            for n, b in enumerate((ml_igate_b, ml_fgate_b)):
                for d in range(2):
                    p0 = 32 * (2 * n + d)
                    pool.dma_start(gb[p0:p0 + ML_H, :],
                                   b[0, 4 * d:4 * d + 4].rearrange("(h o) -> h o", o=1)).then_inc(s["gb_in"], 16)
            pool.memset(zpad[:, :], 0.0).then_inc(s["pad_zero"], 1)
            pool.wait_ge(s["pad_zero"], 1)
            rp = rpb_pad.ap()
            end = PAD + NA_H * RPB_HEAD
            pool.dma_start(rp[0:PAD].rearrange("(o n) -> o n", o=1), zpad[:, :]).then_inc(s["pad_out"], 16)
            pool.dma_start(rp[end:end + PAD].rearrange("(o n) -> o n", o=1), zpad[:, :]).then_inc(s["pad_out"], 16)
            pool.dma_start(rp[PAD:end].rearrange("(h n) -> h n", h=NA_H),
                           na_rpb[0].rearrange("h r c -> h (r c)")).then_inc(s["pad_out"], 16)
            def load_table(i):
                for b in range(2):
                    for qr in range(ROWS):
                        p0 = (b * ROWS + qr) * STRIP
                        first = PAD + 4 * i * RPB_HEAD + (7 - qr) * RPB_C - STRIP * b - STRIP
                        pool.dma_start(table[p0:p0 + STRIP, :, 0:TABLE],
                                       bass.AP(rpb_pad, first, [[1, STRIP], [RPB_HEAD, 4], [1, TABLE]])).then_inc(s["table_in"], 16)

            pool.memset(ones4[:, :], 1.0).then_inc(s["ones_set"], 1)
            pool.memset(row_a[:, :, :, :], 0.0).then_inc(s["ones_set"], 1)
            pool.wait_ge(s["xt_ps"], KB)
            pool.memset(wg_hi[:, :, :].bitcast(F32), 0.0).then_inc(s["wg_zero"], 1)
            pool.memset(wg_lo[:, :, :].bitcast(F32), 0.0).then_inc(s["wg_zero"], 1)
            pool.wait_ge(s["rows_a"], 1)
            pool.dma_start(rdram.ap().rearrange("h (d s) -> h d s", d=2), rrow[:, :, :]).then_inc(s["rscr_out"], 16)
            pool.wait_ge(s["rscr_out"], 16)
            pool.wait_ge(s["cols_done"], 1)
            with pool.Fori(0, ML_H) as h:
                pool.wait_ge(s["w_done"], h * 4 + 1)
                src = bass.AP(rdram, h * (2 * S), [[0, P], [1, 2 * S]])
                pool.dma_start(rbc[:, :, :].rearrange("p d s -> p (d s)"), src).then_inc(s["r_in"], 16)
            pool.wait_ge(s["qkt_done"], 4 * ML_H + 1)
            pool.dma_start(namask[:, :, :], consts[:, 3 * P:3 * P + NJ * 256].rearrange("p (j c) -> p j c", j=NJ)).then_inc(s["mask_in"], 16)
            pool.wait_ge(s["pv_done"], 4 * ML_H + 1)
            pool.wait_ge(s["pad_out"], 48)
            load_table(0)
            for i in range(1, 4):
                pool.wait_ge(s["smx_done"], 4 * i)
                load_table(i)
            for n in range(4):
                pool.wait_ge(unit_used, U_WO + 10 * n + HL)
                if n:
                    pool.wait_ge(s["res_in"], 16 * n)
                pool.dma_start(res[:, :, n * 512:(n + 1) * 512],
                               x[0].rearrange("(t p) c -> p t c", p=P)[:, :, n * 512:(n + 1) * 512]).then_inc(s["res_in"], 16)
            pool.wait_ge(unit_used, U_FF + HL)
            for tile, src in ((g1b, ln1_g), (b1b, ln1_b)):
                pool.dma_start(tile[:, :], bass.AP(src.tensor, 0, [[0, P], [1, D]])).then_inc(s["gb_bc"], 16)
            pool.wait_ge(s["gb_bc"], 32)
            link = Chain(pool, s["link_pool"])
            link(nc.gpsimd.tensor_scalar(g1b[:, :], g1b[:, :], ALPHA, None, ALU.mult))
            link(nc.gpsimd.tensor_scalar(b1b[:, :], b1b[:, :], ALPHA, None, ALU.mult))
            pool.wait_ge(s["ht_ps"], KB)
            for t in range(TT):
                link(nc.gpsimd.tensor_tensor(res[:, t, :], res[:, t, :], g1b[:, :], ALU.mult))
                nc.gpsimd.tensor_tensor(res[:, t, :], res[:, t, :], b1b[:, :], ALU.add).then_inc(s["res_acc"], 1)
            for tile, src in ((g2b, ln2_g), (b2b, ln2_b)):
                pool.dma_start(tile[:, :], bass.AP(src.tensor, 0, [[0, P], [1, D]])).then_inc(s["gb_bc"], 16)
            pool.wait_ge(s["gb_bc"], 64)
            for n, (t, half) in enumerate(POOL_HALVES):
                pool.wait_ge(s["hn_rows"], n + 1)
                cs = slice(half * 1024, (half + 1) * 1024)
                link(nc.gpsimd.tensor_tensor(res[:, t, cs], res[:, t, cs], g2b[:, cs], ALU.mult))
                nc.gpsimd.tensor_tensor(res[:, t, cs], res[:, t, cs], b2b[:, cs], ALU.add).then_inc(s["ln2_y_pool"], 1)

        @block.scalar
        def _(act):
            def hi(ub, u8, k):
                if isinstance(ub, int) and ub + k >= U_END:
                    return
                act.wait_ge(weights_in[k % RAW], (u8 + k // RAW + 1) * 16)
                act.wait_ge(unit_used, ub + k + 1)
                nc.scalar.activation(whi[:, k % HL, :], raw[:, k % RAW, :], ACT.Copy).then_inc(w_hi_ready, 1)

            act.dma_start(ident[:, :], consts[:, 0:P]).then_inc(s["ident_in"], 16)
            for n, (kb, blocks) in enumerate(X_PIECES):
                cs = slice(kb * P, (kb + blocks) * P)
                act.dma_start(x_tok[:, :, cs], x[0].rearrange("(t p) c -> p t c", p=P)[:, :, cs]).then_inc(x_in[n], 16)
            for n in range(4):
                for kb in range(4 * n, 4 * n + 4):
                    act.wait_ge(s["xt_ps"], kb + 1)
                    nc.scalar.activation(xt_hi[:, kb, :], ps[:, 4 + kb % 4, :], ACT.Copy).then_inc(s["xt_hi_done"], 1)
                hi(U_ML, U_ML // 8, 2 * n)
                hi(U_ML, U_ML // 8, 2 * n + 1)

            def gate_weights():
                act.wait_ge(s["wg_in"], 16)
                act.wait_ge(s["wg_zero"], 2)
                nc.scalar.activation(apart(wg_hi), together(wg), ACT.Copy).then_inc(s["wg_hi_done"], 1)

            def log1p_exp():
                act.wait_ge(s["neg_fx"], 1)
                nc.scalar.activation(ex[:, :, :], ex[:, :, :], ACT.Exp).then_inc(s["exp_fx"], 1)
                act.wait_ge(s["exp_fx"], 1)
                nc.scalar.activation(ex[:, :, :], ex[:, :, :], ACT.Ln, bias=1.0).then_inc(s["log_fx"], 1)

            def exp_minus_m():
                act.wait_ge(s["rows_a"], 1)
                nc.scalar.activation(ex[:, :, :], mrow[:, :, :], ACT.Exp, scale=-1.0).then_inc(s["em_row"], 1)

            def ml_projections(h, hooks, first=0):
                ub, u8 = h * 32 + U_ML, h * 4 + U_ML // 8
                for u in range(32):
                    if u >= first:
                        hi(ub, u8, u + HL)
                    if u in (8, 16):
                        c = u // 8 - 1
                        for b in range(2):
                            act.wait_ge(s["qk_done"], h * 4 + (2 * c + b + 2))
                            nc.scalar.activation((qt_hi, kt_hi)[c][:, b, :], (qt, kt)[c][:, b, :], ACT.Copy).then_inc(s["qk_hi_done"], 1)
                    if u % 8 == 7:
                        c = u // 8
                        act.wait_ge(unit_used, ub + (8 * (c + 1) + HL))
                        if c < 2:
                            for b in range(2):
                                blk = h * 2 + (8 * c + b)
                                act.wait_ge(s["qk_done"], h * 4 + ((1 + b if c else 0) + 1))
                                act.wait_ge(s["qkt_done"], h * 4 + 1)
                                nc.scalar.activation(cv[:, b, :], ps[:, 2 * c + b, :], ACT.Identity,
                                                     scale=par[:, bass.ds(blk + (PAR_MLW + 16), 1)],
                                                     bias=par[:, bass.ds(blk + PAR_MLB, 1)]).then_inc(s["conv_a"], 1)
                            for b in range(2):
                                act.wait_ge(s["conv_b"], h * 4 + (2 * c + b + 1))
                                nc.scalar.activation(sg[:, b, :], cv[:, b, :], ACT.Sigmoid).then_inc(s["conv_sg"], 1)
                        elif c == 2:
                            act.wait_ge(s["vtr_done"], h + 1)
                            nc.scalar.activation(vt[:, :, :], ps[:, 0:2, :], ACT.Copy).then_inc(s["free_v"], 1)
                        else:
                            act.wait_ge(s["y_mul"], h * 2 + 1)
                            nc.scalar.activation(ot[:, :, :], ps[:, 2:4, :], ACT.Sigmoid).then_inc(s["free_o"], 1)
                    do(hooks, u)

            def mlstm(h):
                def v_token_major():
                    act.wait_ge(s["vtr_done"], h + 2)
                    act.wait_ge(s["pv_done"], h * 4 + 1)
                    nc.scalar.activation(vtok_hi[:, :, 0:256], ps[:, 4:6, :].rearrange("p b (t c) -> p (b t) c", t=2),
                                         ACT.Copy).then_inc(s["vtok_done"], 1)

                def decay(c):
                    if c == 0:
                        act.wait_ge(s["rmask_done"], h + 1)
                    fo, bo = FWD_AT[c], BWD_AT[c]
                    work = [(0, c, 0, fo)] + [(0, tc, tc - c, fo + tc - c) for tc in range(c + 1, 4)] \
                        + [(1, tc, c - tc, bo + tc) for tc in range(c)] + [(1, c, 0, bo + c)]
                    for n, (d, tc, dist, slot) in enumerate(work):
                        src = rmask if dist == 0 else rbc
                        e = nc.scalar.activation(wmat[:, d, slot * P:(slot + 1) * P], src[:, d, tc * P:(tc + 1) * P], ACT.Exp,
                                                 bias=bias_s[:, bass.ds(h + ((d * 4 + c) * 4 + dist) * 4, 1)])
                    e.then_inc(s["e_done"], 1)

                def weights_hi(c):
                    act.wait_ge(s["w_done"], h * 4 + (c + 2))
                    fo, bo = FWD_AT[c] * P, BWD_AT[c] * P
                    nc.scalar.activation(wmat_hi[:, 0, fo:fo + (4 - c) * P], wmat[:, 0, fo:fo + (4 - c) * P], ACT.Copy)
                    nc.scalar.activation(wmat_hi[:, 1, bo:bo + (c + 1) * P], wmat[:, 1, bo:bo + (c + 1) * P],
                                         ACT.Copy).then_inc(s["sw_hi_done"], 1)

                def std():
                    act.wait_ge(s["var_done"], h + 1)
                    nc.scalar.activation(rstd[:, :], veps[:, :], ACT.Sqrt).then_inc(s["std_done"], 1)

                def y_hi():
                    for b in range(2):
                        act.wait_ge(s["y_mul"], h * 2 + (b + 2))
                        nc.scalar.activation(blk_of(yml_hi, h * 2 + b), yt[:, b, :], ACT.Copy).then_inc(s["yhi_done"], 1)

                return {1: [v_token_major, lambda: decay(0)], 2: [lambda: decay(1)], 3: [lambda: decay(2), lambda: weights_hi(0)],
                        4: [lambda: decay(3), lambda: weights_hi(1)], 5: [lambda: weights_hi(2)], 6: [lambda: weights_hi(3)],
                        11: [std], 15: [y_hi]}

            ml_projections(0, {4: [gate_weights], 6: [lambda: act.wait_ge(s["par_done"], 1)], 10: [log1p_exp], 18: [exp_minus_m]}, first=4)
            with act.Fori(0, ML_H - 1) as h:
                ml_projections(h + 1, mlstm(h))

            def na_v(i, hooks, first_out=3):
                ub, u8 = i * 24 + U_NA, i * 3 + U_NA // 8
                for u in range(8):
                    hi(ub, u8, u + HL)
                    for b, after in enumerate((first_out, 7)):
                        if u == after:
                            act.wait_ge(s["qkt_done"], 4 * ML_H + 1)
                            act.wait_ge(s["na_vt_ps"], i + 1)
                            if not isinstance(i, int):
                                act.wait_ge(s["s_done"], i * 4)
                            nc.scalar.activation(strips(nvt[:, b, :]), by_strip(ps[:, b, :]), ACT.Copy).then_inc(s["na_v_done"], 1)
                    do(hooks, u)

            def na_qk(i, pr, hooks):
                ub, u8 = i * 24 + U_NA, i * 3 + U_NA // 8
                b0 = (2, 0)[pr]
                for u in range(8):
                    hi(ub, u8, 8 + 8 * pr + u + HL)
                    if u in (3, 7):
                        if not isinstance(i, int) or pr:
                            act.wait_ge(s["s_done"], i * 4 + 2 * pr)
                    if u == 3:
                        nc.scalar.activation(strips(qk_hi[:, 0, :]), by_strip(ps[:, b0, :])[:, :, :, ::-1], ACT.Copy,
                                             scale=0.125).then_inc(s["na_qk_hi"], 1)
                    if u == 7:
                        nc.scalar.activation(strips(qk_hi[:, 1, :]), by_strip(ps[:, b0 + 1, :]), ACT.Copy).then_inc(s["na_qk_hi"], 1)
                    do(hooks, u)

            def v7_copy(i):
                act.wait_ge(s["na_vt_ps"], i + 2)
                nc.scalar.activation(v7[:, :, :].rearrange("p i c -> p (i c)"),
                                     ps[:, 4:8, :].rearrange("p b c -> p (b c)")[:, 0:7 * 256], ACT.Copy).then_inc(s["na_v7"], 1)

            def softmax(i, pr, at):
                def exps(hh):
                    act.wait_ge(s["smx_done"], i * 4 + (2 * pr + hh + 1))
                    for j in range(NJ):
                        e = nc.scalar.activation(sc[:, hh, j, :], sc[:, hh, j, :], ACT.Exp, bias=smax[:, hh, j:j + 1],
                                                 accum_out=ssum[:, hh, j:j + 1])
                    e.then_inc(s["pexp_done"], 1)

                def pt_copy(hh):
                    act.wait_ge(s["pt_ps"], i * 4 + (2 * pr + hh + 1))
                    nc.scalar.activation(pt[:, hh, :, :].rearrange("p a b -> p (a b)"),
                                         ps[:, 4 + 2 * hh:6 + 2 * hh, :].rearrange("p a b -> p (a b)"), ACT.Copy).then_inc(s["pt_done"], 1)

                return {at + 1: [lambda: exps(0)], at + 2: [lambda: exps(1)], at + 5: [lambda: pt_copy(0)],
                        min(at + 6, 7): [lambda: pt_copy(1)]} if at < 2 else \
                    {at + 1: [lambda: exps(0)], at + 2: [lambda: exps(1)], 7: [lambda: pt_copy(0), lambda: pt_copy(1)]}

            def y_out(i, pr):
                act.wait_ge(s["ypv_done"], i * 2 + (pr + 1))
                nc.scalar.activation(by_strip(blk_of(yna_hi, i * 2 + pr)), strips(ps[:, 4, :])[:, :, :, ::-1],
                                     ACT.Copy).then_inc(s["yna_h"], 1)

            last_head = mlstm(ML_H - 1)
            na_v(0, {u: f for u, f in last_head.items() if u < 8}, first_out=7)
            na_qk(0, 0, {u - 8: f for u, f in last_head.items() if u >= 8})
            na_qk(0, 1, plus({1: [lambda: v7_copy(0)]}, softmax(0, 0, 2)))
            with act.Fori(1, 4) as i:
                na_v(i, plus({0: [lambda: y_out(i - 1, 0)]}, softmax(i - 1, 1, 1)))
                na_qk(i, 0, {1: [lambda: y_out(i - 1, 1)], 3: [lambda: v7_copy(i)]})
                na_qk(i, 1, softmax(i, 0, 0))

            def merge(i, hooks):
                ub, u8 = i * 24 + U_MG, i * 3 + U_MG // 8
                for half in range(2):
                    for k in range(12):
                        hi(ub, u8, 12 * half + k + HL)
                        do(hooks, 12 * half + k)
                        if k == (9 if 0 in hooks and half == 0 else 7):
                            act.wait_ge(unit_used, ub + (12 * half + 8 + HL))
                            act.wait_ge(s["mix_done"], i * 2 + (half + 1))
                            nc.scalar.activation(mg[:, :, :], ps[:, 0:2, :], ACT.Sigmoid).then_inc(s["merge_sg"], 1)

            merge(0, plus({0: [lambda: y_out(3, 0)]}, softmax(3, 1, 1), {8: [lambda: y_out(3, 1)]}))
            with act.Fori(1, KB // 2 - 1) as i:
                merge(i, {})

            def mixed_hi(kb):
                act.wait_ge(unit_used, U_WO - 4 + HL)
                act.wait_ge(s["mix_done"], kb + 2)
                nc.scalar.activation(mx_hi[:, kb, :], mixed[:, kb, :], ACT.Copy).then_inc(s["mxhi_done"], 1)

            merge(KB // 2 - 1, split_hooks(mixed_hi))
            mixed_hi(KB - 1)
            with act.Fori(0, 2) as i:
                for k in range(32):
                    hi(i * 32 + U_WO, i * 4 + U_WO // 8, k + HL)
            act.wait_ge(s["ln1_var"], 1)
            nc.scalar.activation(rstd[:, :], veps[:, :], ACT.Sqrt).then_inc(s["ln1_std"], 1)
            def rows(n):
                act.wait_ge(s["ln1_hn"], 1)
                for t in range(2):
                    e = nc.scalar.activation(res[:, t, n * 512:(n + 1) * 512], res[:, t, n * 512:(n + 1) * 512], ACT.Identity,
                                             scale=rstd[:, t:t + 1], bias=nmu[:, t:t + 1])
                e.then_inc(s["hn_cols_a"], 1)

            def h_columns(kb):
                act.wait_ge(s["ht_ps"], kb + 1)
                g1, b1 = par[:, PAR_G1 + kb:PAR_G1 + kb + 1], par[:, PAR_B1 + kb:PAR_B1 + kb + 1]
                if kb % 2:
                    if kb > 2:
                        act.wait_ge(s["ht_lo_d"], kb - 1)
                    nc.scalar.activation(ft[:, 1, :], ps[:, 4 + kb % 4, :], ACT.Identity, scale=g1, bias=b1).then_inc(s["h_own"], 1)
                    act.wait_ge(s["h_own"], (kb + 1) // 2)
                    nc.scalar.activation(ht_hi[:, kb, :], ft[:, 1, :], ACT.Copy).then_inc(s["ht_hi_d"], 1)
                else:
                    nc.scalar.activation(ht_hi[:, kb, :], ps[:, 4 + kb % 4, :], ACT.Identity, scale=g1, bias=b1).then_inc(s["ht_hi_d"], 1)

            rows(0)
            rows(1)
            for kb in range(0, 4):
                h_columns(kb)
            rows(2)
            for kb in range(4, 8):
                h_columns(kb)
            rows(3)

            def ffn_block(n, c, par_w, par_b, slot):
                act.wait_ge(s["act_done"], n + 1)
                nc.scalar.activation(ft[:, c % 2, :], ps[:, 2 * c, :], ACT.Identity, scale=par_w, bias=par_b).then_inc(s["u_conv"], 1)
                act.wait_ge(s["u_conv2"], n + 1)
                nc.scalar.activation(fg[:, c % 2, :], ft[:, c % 2, :], ACT.Gelu).then_inc(s["u_gelu"], 1)
                act.wait_ge(s["u_mul"], n + 5)
                nc.scalar.activation(blk_of(ac_hi, slot), ft[:, c % 2, :], ACT.Copy).then_inc(s["u_hi"], 1)

            def ffn_up(g, i, hooks):
                for c in range(4):
                    for k in range(8):
                        do(hooks, 8 * c + k)
                        hi(g * 96 + i * 32 + U_FF, g * 12 + i * 4 + U_FF // 8, 8 * c + k + HL)
                    blk = g * 8 + i * 4 + c
                    act.wait_ge(unit_used, g * 96 + i * 32 + (U_FF + 8 * (c + 1) + HL))
                    ffn_block(blk, c, par[:, bass.ds(blk + (PAR_FW + FB), 1)], par[:, bass.ds(blk + PAR_FB, 1)],
                              i * 4 + c)

            def ffn_down(g):
                with act.Fori(0, 2) as i:
                    for k in range(16):
                        hi(g * 96 + i * 16 + (U_FF + 64), g * 12 + i * 2 + (U_FF + 64) // 8, k + HL)

            ffn_up(0, 0, {0: [lambda kb=kb: h_columns(kb) for kb in range(8, 12)],
                          1: [lambda kb=kb: h_columns(kb) for kb in range(12, 16)]})
            ffn_up(0, 1, {})
            ffn_down(0)
            with act.Fori(1, NG) as g:
                with act.Fori(0, 2) as i:
                    ffn_up(g, i, {})
                ffn_down(g)
            for c in range(TAIL):
                for k in range(8):
                    hi(U_TL, U_TL // 8, 8 * c + k + HL)
                blk = NG * G + c
                act.wait_ge(unit_used, U_TL + 8 * (c + 1) + HL)
                ffn_block(blk, c, par[:, PAR_FW + FB + blk:PAR_FW + FB + blk + 1], par[:, PAR_FB + blk:PAR_FB + blk + 1],
                          c)
            for k in range(4 * TAIL):
                hi(U_TL, U_TL // 8, 8 * TAIL + k + HL)
            def std(t):
                act.wait_ge(s["ln2_var"], t + 1)
                nc.scalar.activation(rstd[:, t:t + 1], veps[:, t:t + 1], ACT.Sqrt).then_inc(s["ln2_std"], 1)

            def rows_out(n):
                t, half = POOL_HALVES[n]
                cs = slice(half * 1024, (half + 1) * 1024)
                act.wait_ge(s["ln2_hn"], t + 1)
                nc.scalar.activation(res[:, t, cs], res[:, t, cs], ACT.Identity, scale=rstd[:, t:t + 1],
                                     bias=nmu[:, t:t + 1]).then_inc(s["hn_rows"], 1)

            std(0)
            rows_out(0)
            std(1)
            rows_out(1)
            std(2)
            rows_out(2)
            std(3)
            for n, (t, half) in enumerate(POOL_HALVES):
                cs = slice(half * 1024, (half + 1) * 1024)
                act.wait_ge(s["ln2_y_pool"], n + 1)
                act.dma_start(out[0, t * P:(t + 1) * P, cs], res[:, t, cs]).then_inc(s["out_done_pool"], 16)
            act.wait_ge(s["out_done_pool"], 16 * len(POOL_HALVES))

        @block.vector
        def _(dve):
            def lo(ub, k):
                if isinstance(ub, int) and ub + k >= U_END:
                    return
                dve.wait_ge(w_hi_ready, ub + k + 1)
                nc.vector.tensor_tensor(wlo[:, k % HL, :], raw[:, k % RAW, :], whi[:, k % HL, :].bitcast(F32),
                                        ALU.subtract).then_inc(w_lo_ready, 1)

            for n in range(4):
                for kb in range(4 * n, 4 * n + 4):
                    dve.wait_ge(s["xt_hi_done"], kb + 1)
                    nc.vector.tensor_tensor(xt_lo[:, kb, :], ps[:, 4 + kb % 4, :], xt_hi[:, kb, :].bitcast(F32),
                                            ALU.subtract).then_inc(s["xt_lo_done"], 1)
                lo(U_ML, 2 * n)
                lo(U_ML, 2 * n + 1)

            glink = Chain(dve, s["link_gates"])

            def columns():
                dve.wait_ge(s["par_ps"], 1)
                for i, w in enumerate((PAR_B1 + 16, 2 * FB, 2 * FB)):
                    ins = nc.vector.tensor_copy(par[:, PAR_OFF[i]:PAR_OFF[i] + w], ps[:, 7, i * P:i * P + w])
                ins.then_inc(s["par_done"], 1)

            def gate_weights():
                dve.wait_ge(s["wg_hi_done"], 1)
                nc.vector.tensor_tensor(apart(wg_lo), together(wg), apart(wg_hi).bitcast(F32), ALU.subtract).then_inc(s["wg_lo_done"], 1)

            def gate_inputs():
                dve.wait_ge(s["gb_in"], 64)
                dve.wait_ge(s["ones_set"], 2)
                dve.wait_ge(s["gate_rows"], 1)
                for d in range(2):
                    i_rows, f_rows = slice(32 * d, 32 * d + ML_H), slice(64 + 32 * d, 64 + 32 * d + ML_H)
                    nc.vector.tensor_scalar(li[:, d, :], ps[i_rows, 4, :], gb[i_rows, :], None, ALU.add)
                    ins = nc.vector.tensor_scalar(fx[:, d, :], ps[f_rows, 4, :], gb[f_rows, :], None, ALU.add)
                glink(ins)
                nc.vector.scalar_tensor_tensor(ex[:, :, :], fx[:, :, :], -1.0, fx[:, :, :], ALU.mult, ALU.min).then_inc(s["neg_fx"], 1)

            def log_sigmoid():
                dve.wait_ge(s["log_fx"], 1)
                glink(nc.vector.scalar_tensor_tensor(lf[:, :, :], fx[:, :, :], 0.0, ex[:, :, :], ALU.min, ALU.subtract))

            def way(ap, d):
                return ap if d == 0 else ap[:, ::-1]

            def running_max(d):
                nc.vector.tensor_tensor_scan(way(mrow[:, d, :], d), way(lf[:, d, :], d), way(li[:, d, :], d), NEG, ALU.add, ALU.max)

            def chunk_sums(d):
                for c in range(4):
                    cs = slice(c * P, (c + 1) * P)
                    ins = nc.vector.tensor_tensor_scan(way(bl[:, d, cs], d), ones4[:, :], way(lf[:, d, cs], d), 0.0, ALU.mult, ALU.add)
                glink(ins)
                glink(nc.vector.tensor_tensor(row_a[:, d, 0, :], li[:, d, :], bl[:, d, :], ALU.subtract))

            def exponents(d, dist):
                for c in range(4):
                    tc = c + dist if d == 0 else c - dist
                    if 0 <= tc < 4:
                        mid = tc - 1 if d == 0 else tc + 1
                        at = mid * P + P - 1 if d == 0 else mid * P
                        cs = slice(c * P, (c + 1) * P)
                        ins = nc.vector.tensor_scalar(row_a[:, d, dist, cs], row_a[:, d, dist - 1, cs], bl[:, d, at:at + 1], None, ALU.add)
                glink(ins)

            def decay_rows():
                for d in range(2):
                    ins = nc.vector.tensor_tensor(rrow[:, d, :], bl[:, d, :], mrow[:, d, :], ALU.subtract)
                ins.then_inc(s["rows_a"], 1)

            def exponent_columns():
                dve.wait_ge(s["cols_ps"], 1)
                nc.vector.tensor_copy(bias_s[:, :], ps[:, 4, 0:160])
                nc.vector.memset(vtok_lo[:, :, 256:258].bitcast(F32), 0.0)
                nc.vector.memset(vtok_hi[:, :, 256:258].bitcast(F32), 1.0).then_inc(s["cols_done"], 1)

            gate_hooks = {4: [columns], 5: [gate_weights], 9: [gate_inputs], 11: [log_sigmoid, lambda: running_max(0)],
                          12: [lambda: chunk_sums(0), lambda: exponents(0, 1)],
                          13: [lambda: exponents(0, 2), lambda: exponents(0, 3), lambda: running_max(1)],
                          14: [lambda: chunk_sums(1), lambda: exponents(1, 1)],
                          15: [lambda: exponents(1, 2), lambda: exponents(1, 3)],
                          16: [decay_rows], 21: [exponent_columns]}

            clink = Chain(dve, s["link_conv"])
            mlink = Chain(dve, s["link_ml"])
            ML_LINKS = 4 * 5 + 2

            def ml_projections(h, hooks, first=0):
                ub = h * 32 + U_ML
                clink.loop(h * 4)
                for u in range(32):
                    if u >= first:
                        lo(ub, u + HL)
                    if u in (8, 16):
                        c = u // 8 - 1
                        for b in range(2):
                            dve.wait_ge(s["qk_hi_done"], h * 4 + (2 * c + b + 1))
                            nc.vector.tensor_tensor((qt_lo, kt_lo)[c][:, b, :], (qt, kt)[c][:, b, :],
                                                    (qt_hi, kt_hi)[c][:, b, :].bitcast(F32), ALU.subtract).then_inc(s["qk_lo_done"], 1)
                    if u in (7, 15):
                        c = u // 8
                        for b in range(2):
                            blk = h * 2 + (8 * c + b)
                            pb = ps[:, 2 * c + b, :]
                            dve.wait_ge(s["conv_a"], h * 4 + (2 * c + b + 1))
                            clink(nc.vector.scalar_tensor_tensor(cv[:, b, 1:S], pb[:, 0:S - 1], par[:, bass.ds(blk + PAR_MLW, 1)],
                                                                 cv[:, b, 1:S], ALU.mult, ALU.add))
                            nc.vector.scalar_tensor_tensor(cv[:, b, 0:S - 1], pb[:, 1:S], par[:, bass.ds(blk + (PAR_MLW + 32), 1)],
                                                           cv[:, b, 0:S - 1], ALU.mult, ALU.add).then_inc(s["conv_b"], 1)
                        for b in range(2):
                            dve.wait_ge(s["conv_sg"], h * 4 + (2 * c + b + 1))
                            if b == 0:
                                dve.wait_ge(s["qkt_done"], h * 4 + 1)
                            nc.vector.scalar_tensor_tensor((qt, kt)[c][:, b, :], cv[:, b, :], (1.0, 256 ** -0.5)[c], sg[:, b, :],
                                                           ALU.mult, ALU.mult).then_inc(s["qk_done"], 1)
                    do(hooks, u)

            def mlstm(h):
                mlink.loop(h * ML_LINKS)

                def mask_rows():
                    dve.wait_ge(s["r_in"], (h + 1) * 16)
                    for d in range(2):
                        ins = nc.vector.tensor_tensor(rmask[:, d, :].rearrange("p (c t) -> p c t", c=4),
                                                      rbc[:, d, :].rearrange("p (c t) -> p c t", c=4),
                                                      tri[:, d:d + 1, :].to_broadcast([P, 4, P]), ALU.add)
                    ins.then_inc(s["rmask_done"], 1)

                def weigh(c):
                    dve.wait_ge(s["e_done"], h * 4 + (c + 1))
                    dve.wait_ge(s["qkt_done"], h * 4 + (c + 2))
                    pb = ps[:, 6 + c % 2, :]
                    fo = FWD_AT[c] * P
                    bo = BWD_AT[c] * P
                    wf = wmat[:, 0, fo:fo + (4 - c) * P]
                    wb = wmat[:, 1, bo:bo + (c + 1) * P]
                    nc.vector.tensor_tensor(wf, pb[:, c * P:S], wf, ALU.mult)
                    nc.vector.tensor_tensor(wb, pb[:, 0:(c + 1) * P], wb, ALU.mult).then_inc(s["w_done"], 1)

                def v_low():
                    dve.wait_ge(s["vtok_done"], h + 1)
                    nc.vector.tensor_tensor(vtok_lo[:, :, 0:256], ps[:, 4:6, :].rearrange("p b (t c) -> p (b t) c", t=2),
                                            vtok_hi[:, :, 0:256].bitcast(F32), ALU.subtract).then_inc(s["v_lo_done"], 1)

                def weights_lo(c):
                    dve.wait_ge(s["sw_hi_done"], h * 4 + (c + 1))
                    fo, bo = FWD_AT[c] * P, BWD_AT[c] * P
                    nc.vector.tensor_tensor(wmat_lo[:, 0, fo:fo + (4 - c) * P], wmat[:, 0, fo:fo + (4 - c) * P],
                                            wmat_hi[:, 0, fo:fo + (4 - c) * P].bitcast(F32), ALU.subtract)
                    nc.vector.tensor_tensor(wmat_lo[:, 1, bo:bo + (c + 1) * P], wmat[:, 1, bo:bo + (c + 1) * P],
                                            wmat_hi[:, 1, bo:bo + (c + 1) * P].bitcast(F32), ALU.subtract).then_inc(s["sw_lo_done"], 1)

                def normalise(tc):
                    dve.wait_ge(s["pv_done"], h * 4 + (tc + 2))
                    b0 = 4 + 2 * (tc % 2)
                    den = ps[:, b0:b0 + 2, 256:257].rearrange("p d o -> p (d o)")
                    em = bias_s[:, 128:160].rearrange("p (d t h) -> p d t h", d=2, t=4)[:, :, tc, bass.ds(h, 1)].rearrange("p d o -> p (d o)")
                    mlink(nc.vector.scalar_tensor_tensor(dn[:, :], den, -1.0, em, ALU.mult, ALU.max))
                    mlink(nc.vector.tensor_tensor(dn[:, :], dn[:, :], den, ALU.max))
                    mlink(nc.vector.reciprocal(dn[:, :], dn[:, :]))
                    mlink(nc.vector.tensor_scalar(htok[:, tc, :], ps[:, b0, 0:256], dn[:, 0:1], None, ALU.mult))
                    nc.vector.scalar_tensor_tensor(htok[:, tc, :], ps[:, b0 + 1, 0:256], dn[:, 1:2], htok[:, tc, :],
                                                   ALU.mult, ALU.add).then_inc(s["pv_free"], 1)
                    dve.wait_ge(s["pv_free"], h * 4 + (tc + 2))
                    mlink(nc.vector.bn_stats(st[:, tc, 0, :], htok[:, tc, :]))

                def variance():
                    dve.sem_inc(s["dve_mark"], 1)
                    for tc in range(4):
                        ins = nc.vector.bn_aggr(mv[:, tc, :], st[:, tc, 0, :])
                    mlink(ins)
                    nc.vector.tensor_scalar(veps[:, :], mv[:, :, 1], EPS, None, ALU.add).then_inc(s["var_done"], 1)

                def standardise():
                    dve.wait_ge(s["std_done"], h + 1)
                    mlink(nc.vector.reciprocal(rstd[:, :], rstd[:, :]))
                    for tc in range(4):
                        ins = nc.vector.tensor_scalar(htok[:, tc, :], htok[:, tc, :], mv[:, tc, 0:1], rstd[:, tc:tc + 1],
                                                      ALU.subtract, ALU.mult)
                    ins.then_inc(s["hn_done"], 1)

                def y_gate():
                    for b in range(2):
                        dve.wait_ge(s["yps_done"], h * 2 + (b + 1))
                        nc.vector.scalar_tensor_tensor(yt[:, b, :], ps[:, 4 + b, :], par[:, bass.ds(h * 2 + (PAR_NW + b), 1)], ot[:, b, :],
                                                       ALU.mult, ALU.mult).then_inc(s["y_mul"], 1)

                def y_low():
                    for b in range(2):
                        dve.wait_ge(s["yhi_done"], h * 2 + (b + 1))
                        at = h * 2 + b
                        nc.vector.tensor_tensor(blk_of(yml_lo, at), yt[:, b, :], blk_of(yml_hi, at).bitcast(F32),
                                                ALU.subtract).then_inc(s["ylo_done"], 1)
                    assert mlink.k == ML_LINKS

                return {0: [mask_rows], 1: [v_low], 2: [lambda: weigh(0)], 3: [lambda: weigh(1), lambda: weights_lo(0)],
                        4: [lambda: weigh(2), lambda: weights_lo(1)], 5: [lambda: weigh(3), lambda: weights_lo(2)],
                        6: [lambda: weights_lo(3)],
                        7: [lambda: normalise(0)], 8: [lambda: normalise(1)], 9: [lambda: normalise(2)],
                        10: [lambda: normalise(3), variance], 12: [standardise], 15: [y_gate, y_low]}

            ml_projections(0, gate_hooks, first=4)
            dve.wait_ge(s["const_in"], 16)
            with dve.Fori(0, ML_H - 1) as h:
                ml_projections(h + 1, mlstm(h))

            nlink = Chain(dve, s["link_na"])
            NA_LINKS = 8

            def na_units(ub, n, hooks):
                for u in range(8):
                    lo(ub, 8 * n + u + HL)
                    do(hooks, u)

            def softmax(i, pr, at):
                def shifted(hh):
                    nlink.loop(i * (2 * NA_LINKS) + (NA_LINKS * pr + 3 * hh))
                    if pr == 0 and hh == 0:
                        dve.wait_ge(s["table_in"], (i + 1) * (16 * 2 * ROWS))
                    dve.wait_ge(s["s_done"], i * 4 + (2 * pr + hh + 1))
                    for j in range(NJ):
                        shift = KSTART[j] - QCOLS * j + WIN_COLS
                        head = table[:, 2 * pr + hh, shift:shift + 1]
                        bias = bass.AP(head.tensor, head.offset, [list(head.ap[0]), [STRIP, 4], [RPB_C, ROWS], [1, STRIP]])
                        ins = nc.vector.tensor_tensor(strips(sc[:, hh, j, :]),
                                                      strips(ps[:, 4 + 2 * hh + j // 2, (j % 2) * 256:(j % 2) * 256 + 256]),
                                                      bias, ALU.add)
                    nlink(ins)
                    nlink(nc.vector.tensor_tensor(sc[:, hh, :, :], sc[:, hh, :, :], namask[:, :, :], ALU.min))
                    nlink(nc.vector.reduce_max(smax[:, hh, :], sc[:, hh, :, :], AX.X))
                    nc.vector.tensor_scalar(smax[:, hh, :], smax[:, hh, :], -1.0, None, ALU.mult).then_inc(s["smx_done"], 1)

                def divided(hh):
                    nlink.loop(i * (2 * NA_LINKS) + (NA_LINKS * pr + 6 + hh))
                    dve.wait_ge(s["pexp_done"], i * 4 + (2 * pr + hh + 1))
                    nlink(nc.vector.reciprocal(ssum[:, hh, :], ssum[:, hh, :]))
                    for j in range(NJ):
                        ins = nc.vector.tensor_scalar(sc[:, hh, j, :], sc[:, hh, j, :], ssum[:, hh, j:j + 1], None, ALU.mult)
                    ins.then_inc(s["p_done"], 1)

                return {at: [lambda: shifted(0)], at + 1: [lambda: shifted(1)], at + 2: [lambda: divided(0)],
                        at + 3: [lambda: divided(1)]}

            def qk_low(i, pr, which):
                dve.wait_ge(s["na_qk_hi"], i * 4 + (2 * pr + which + 1))
                dve.wait_ge(s["na_vt_ps"], i + 2)
                pb = by_strip(ps[:, (2, 0)[pr] + which, :])
                high, low = strips(qk_hi[:, which, :].bitcast(F32)), strips(qk_lo[:, which, :])
                if which:
                    ins = nc.vector.tensor_tensor(low, pb, high, ALU.subtract)
                else:
                    for b in range(GRID_W // STRIP):
                        ins = nc.vector.scalar_tensor_tensor(low[:, b, :, :], pb[:, b, :, ::-1], 0.125, high[:, b, :, :],
                                                             ALU.mult, ALU.subtract)
                ins.then_inc(s["na_qk_done"], 1)

            def both(i, pr):
                return {3: [lambda: qk_low(i, pr, 0)], 7: [lambda: qk_low(i, pr, 1)]}

            def y_out(i, pr):
                dve.wait_ge(s["yna_h"], i * 2 + (pr + 1))
                at = i * 2 + pr
                nc.vector.tensor_tensor(by_strip(blk_of(yna_lo, at)), strips(ps[:, 4, :])[:, :, :, ::-1],
                                        by_strip(blk_of(yna_hi, at).bitcast(F32)), ALU.subtract).then_inc(s["yna_l"], 1)

            last_head = mlstm(ML_H - 1)
            na_units(U_NA, 0, {u: f for u, f in last_head.items() if u < 8})
            na_units(U_NA, 1, {u - 8: f for u, f in last_head.items() if u >= 8})
            dve.wait_ge(s["mask_in"], 16)
            na_units(U_NA, 2, plus({0: [lambda: qk_low(0, 0, 0), lambda: qk_low(0, 0, 1)]}, softmax(0, 0, 2), both(0, 1)))
            with dve.Fori(1, 4) as i:
                ub = i * 24 + U_NA
                na_units(ub, 0, plus({0: [lambda: y_out(i - 1, 0)]}, softmax(i - 1, 1, 1)))
                na_units(ub, 1, plus({1: [lambda: y_out(i - 1, 1)]}, both(i, 0)))
                na_units(ub, 2, plus(softmax(i, 0, 0), both(i, 1)))

            link = Chain(dve, s["link_mg"])
            def merge(i, hooks):
                link.loop(i * 2)
                ub = i * 24 + U_MG
                for half in range(2):
                    for k in range(12):
                        lo(ub, 12 * half + k + HL)
                        do(hooks, 12 * half + k)
                    dve.wait_ge(unit_used, ub + (12 * (half + 1) + HL))
                    dve.wait_ge(s["merge_sg"], i * 2 + (half + 2))
                    nc.vector.tensor_tensor(mt[:, 0, :], ps[:, 3, :], mg[:, 0, :], ALU.mult)
                    link(nc.vector.tensor_tensor(mt[:, 1, :], ps[:, 2, :], mg[:, 1, :], ALU.mult))
                    nc.vector.tensor_tensor(blk_of(mixed, i * 2 + half), mt[:, 0, :], mt[:, 1, :],
                                            ALU.add).then_inc(s["mix_done"], 1)

            merge(0, plus({0: [lambda: y_out(3, 0)]}, softmax(3, 1, 1), {8: [lambda: y_out(3, 1)]}))
            with dve.Fori(1, KB // 2 - 1) as i:
                merge(i, {})

            def mixed_lo(kb):
                dve.wait_ge(s["mxhi_done"], kb + 1)
                nc.vector.tensor_tensor(mx_lo[:, kb, :], mixed[:, kb, :], mx_hi[:, kb, :].bitcast(F32),
                                        ALU.subtract).then_inc(s["mxlo_done"], 1)

            merge(KB // 2 - 1, split_hooks(mixed_lo))
            mixed_lo(KB - 1)

            link = Chain(dve, s["link_wo"])
            with dve.Fori(0, 2) as i:
                link.loop(i * 5)
                for half in range(2):
                    for k in range(KB - half):
                        lo(i * 32 + U_WO, 16 * half + k + HL)
                    dve.wait_ge(s["res_in"], i * 32 + 16 * (half + 1))
                    at = bass.ds(i * 1024 + half * 512, 512)

                    def add(t):
                        return nc.vector.scalar_tensor_tensor(res[:, t, at], res[:, t, at], ALPHA, ps[:, 4 - 4 * half + t, :],
                                                              ALU.mult, ALU.add)

                    def stats(t):
                        return nc.vector.bn_stats(st[:, t, :, :].rearrange("p n c -> p (n c)")[:, bass.ds(i * 12 + half * 6, 6)],
                                                  res[:, t, at])

                    for t in range(TT - 1):
                        if half:
                            dve.wait_ge(s["wo_tiles"], i * (TT - 1) + (t + 1))
                            link(add(t))
                            stats(t)
                        else:
                            if t == 0:
                                dve.wait_ge(unit_used, i * 32 + (U_WO + 16 + HL))
                            add(t)
                    if half:
                        dve.wait_ge(unit_used, i * 32 + (U_WO + 32 + HL))
                    add(TT - 1).then_inc(s["wo_free"], 1)
                    dve.wait_ge(s["wo_free"], i * 2 + (half + 2) + 1)
                    for t in range(TT) if half == 0 else (TT - 1,):
                        ins = stats(t)
                    link(ins)
                    if half:
                        lo(i * 32 + U_WO, 31 + HL)
            link = Chain(dve, s["link_norm1"])

            def norm_stats(var, std, ready):
                for t in range(TT):
                    ins = nc.vector.bn_aggr(mv[:, t, :], st[:, t, :, :].rearrange("p a b -> p (a b)"))
                link(ins)
                nc.vector.tensor_scalar(veps[:, :], mv[:, :, 1], EPS, None, ALU.add).then_inc(var, 1)
                dve.wait_ge(std, 1)
                link(nc.vector.reciprocal(rstd[:, :], rstd[:, :]))
                nc.vector.scalar_tensor_tensor(nmu[:, :], mv[:, :, 0], -1.0, rstd[:, :], ALU.mult, ALU.mult).then_inc(ready, 1)

            norm_stats(s["ln1_var"], s["ln1_std"], s["ln1_hn"])
            dve.wait_ge(s["ln1_hn"], 1)

            def rows(n):
                for t in range(2, TT):
                    ins = nc.vector.tensor_scalar(res[:, t, n * 512:(n + 1) * 512], res[:, t, n * 512:(n + 1) * 512],
                                                  rstd[:, t:t + 1], nmu[:, t:t + 1], ALU.mult, ALU.add)
                ins.then_inc(s["hn_cols_v"], 1)

            hlink = Chain(dve, s["link_hcols"])

            def h_columns(kb):
                dve.wait_ge(s["ht_hi_d"], kb + 1)
                if kb % 2 == 0:
                    if kb:
                        dve.wait_ge(s["ht_lo_d"], kb - 1)
                    hlink(nc.vector.tensor_scalar(ft[:, 0, :], ps[:, 4 + kb % 4, :], par[:, PAR_G1 + kb:PAR_G1 + kb + 1],
                                                  par[:, PAR_B1 + kb:PAR_B1 + kb + 1], ALU.mult, ALU.add))
                nc.vector.tensor_tensor(ht_lo[:, kb, :], ft[:, kb % 2, :], ht_hi[:, kb, :].bitcast(F32), ALU.subtract).then_inc(s["ht_lo_d"], 1)

            for n in range(4):
                rows(n)
            for kb in range(8):
                h_columns(kb)

            link = Chain(dve, s["link_ffn"])

            def ffn_block(n, c, w0, w2, slot):
                f, pg = ft[:, c % 2, :], ps[:, 2 * c, :]
                dve.wait_ge(s["u_conv"], n + 1)
                link(nc.vector.scalar_tensor_tensor(f[:, 1:S], pg[:, 0:S - 1], w0, f[:, 1:S], ALU.mult, ALU.add))
                nc.vector.scalar_tensor_tensor(f[:, 0:S - 1], pg[:, 1:S], w2, f[:, 0:S - 1], ALU.mult, ALU.add).then_inc(s["u_conv2"], 1)
                dve.wait_ge(s["u_gelu"], n + 1)
                nc.vector.tensor_tensor(f, ps[:, 2 * c + 1, :], fg[:, c % 2, :], ALU.mult).then_inc(s["u_mul"], 1)
                dve.wait_ge(s["u_hi"], n + 1)
                nc.vector.tensor_tensor(blk_of(ac_lo, slot), ft[:, c % 2, :], blk_of(ac_hi, slot).bitcast(F32),
                                        ALU.subtract).then_inc(s["act_done"], 1)

            def accumulate(n_cols, b0):
                for t in range(TT):
                    ins = nc.vector.tensor_tensor(res[:, t, n_cols], res[:, t, n_cols], ps[:, b0 + t, :], ALU.add)
                ins.then_inc(s["d_free"], 1)

            def ffn_up(g, i, hooks):
                link.loop(g * 8 + i * 4)
                for c in range(4):
                    for k in range(8):
                        do(hooks, 8 * c + k)
                        lo(g * 96 + i * 32 + U_FF, 8 * c + k + HL)
                    blk = g * 8 + i * 4 + c
                    ffn_block(blk, c, par[:, bass.ds(blk + PAR_FW, 1)], par[:, bass.ds(blk + (PAR_FW + 2 * FB), 1)],
                              i * 4 + c)

            def ffn_down(g):
                with dve.Fori(0, 2) as i:
                    for half in range(2):
                        for k in range(8):
                            lo(g * 96 + i * 16 + (U_FF + 64), 8 * half + k + HL)
                        dve.wait_ge(unit_used, g * 96 + i * 16 + (U_FF + 64 + 8 * (half + 1) + HL))
                        accumulate(bass.ds(i * 1024 + half * 512, 512), 4 * half)

            ffn_up(0, 0, {0: [lambda kb=kb: h_columns(kb) for kb in range(8, 12)],
                          1: [lambda kb=kb: h_columns(kb) for kb in range(12, 16)]})
            ffn_up(0, 1, {})
            dve.wait_ge(s["res_acc"], TT)
            ffn_down(0)
            with dve.Fori(1, NG) as g:
                with dve.Fori(0, 2) as i:
                    ffn_up(g, i, {})
                ffn_down(g)
            link.loop(NG * 8)
            for c in range(TAIL):
                for k in range(8):
                    lo(U_TL, 8 * c + k + HL)
                blk = NG * G + c
                ffn_block(blk, c, par[:, PAR_FW + blk:PAR_FW + blk + 1], par[:, PAR_FW + 2 * FB + blk:PAR_FW + 2 * FB + blk + 1],
                          c)
            for n in range(3):
                for k in range(TAIL):
                    lo(U_TL, 8 * TAIL + n * TAIL + k + HL)
                dve.wait_ge(unit_used, U_TL + 8 * TAIL + TAIL * (n + 1) + HL)
                accumulate(slice(n * 512, (n + 1) * 512), 4 * (n % 2))
                dve.wait_ge(s["d_free"], 4 * NG + n + 2 + 1)
                for t in range(TT):
                    ins = nc.vector.bn_stats(st[:, t, n, :], res[:, t, n * 512:(n + 1) * 512])
                link(ins)
            link = Chain(dve, s["link_norm2"])
            dve.wait_ge(s["gb_bc"], 64)

            def stats(t):
                last = res[:, t, 3 * 512:4 * 512]
                dve.wait_ge(s["tile_sums"], t + 1)
                link(nc.vector.tensor_tensor(last, last, ps[:, 4 + t, :], ALU.add))
                link(nc.vector.bn_stats(st[:, t, 3, :], last))
                link(nc.vector.bn_aggr(mv[:, t, :], st[:, t, :, :].rearrange("p a b -> p (a b)")))
                nc.vector.tensor_scalar(veps[:, t:t + 1], mv[:, t, 1:2], EPS, None, ALU.add).then_inc(s["ln2_var"], 1)

            def inverse(t):
                dve.wait_ge(s["ln2_std"], t + 1)
                link(nc.vector.reciprocal(rstd[:, t:t + 1], rstd[:, t:t + 1]))
                if t in [tile for tile, _ in POOL_HALVES]:
                    nc.vector.scalar_tensor_tensor(nmu[:, t:t + 1], mv[:, t, 0:1], -1.0, rstd[:, t:t + 1],
                                                   ALU.mult, ALU.mult).then_inc(s["ln2_hn"], 1)

            def rows_out(n):
                t, half = DVE_HALVES[n]
                cs = slice(half * 1024, (half + 1) * 1024)
                link(nc.vector.scalar_tensor_tensor(res[:, t, cs], res[:, t, cs], mv[:, t, 0:1], g2b[:, cs], ALU.subtract, ALU.mult))
                nc.vector.scalar_tensor_tensor(res[:, t, cs], res[:, t, cs], rstd[:, t:t + 1], b2b[:, cs],
                                               ALU.mult, ALU.add).then_inc(s["ln2_y"], 1)

            stats(0)
            inverse(0)
            stats(1)
            inverse(1)
            stats(2)
            rows_out(0)
            inverse(2)
            stats(3)
            rows_out(1)
            inverse(3)
            for n in range(2, 5):
                rows_out(n)

        @block.tensor
        def _(pe):
            mm = nc.tensor.matmul

            def transpose(o, i, rows=P):
                return nc.tensor.transpose(o, i, ident[0:rows, 0:rows])

            def unit_ready(ub, k):
                pe.wait_ge(w_lo_ready, ub + k + 1 + RAW)

            def three(o, a_hi, a_lo, b_hi, b_lo, first, last):
                mm(o, a_hi, b_hi, start=first, stop=False)
                mm(o, a_hi, b_lo, start=False, stop=False)
                return mm(o, a_lo, b_hi, start=False, stop=last)

            def two_by_two(ub, k, ko, bank, act_hi, act_lo):
                unit_ready(ub, k)
                for kk in range(2):
                    for o in range(2):
                        cols = slice((2 * kk + o) * P, (2 * kk + o + 1) * P)
                        kb = 2 * ko + kk
                        last = three(ps[:, bank + o, :], whi[:, k % HL, cols], wlo[:, k % HL, cols],
                                     act_hi[:, kb, :], act_lo[:, kb, :], kb == 0, kb == KB - 1)
                last.then_inc(unit_used, 1)

            def four_by_one(ub, k, kq, n_kb, o, act_hi, act_lo):
                unit_ready(ub, k)
                for kk in range(4):
                    kb = 4 * kq + kk
                    cols = slice(kk * P, (kk + 1) * P)
                    last = three(o, whi[:, k % HL, cols], wlo[:, k % HL, cols], act_hi[:, kb, :], act_lo[:, kb, :],
                                 kb == 0, kb == n_kb - 1)
                last.then_inc(unit_used, 1)

            def one_by_four(ub, k, kb, n_kb, bank, act_hi, act_lo, tile_done=None):
                unit_ready(ub, k)
                for t in range(TT):
                    ts = slice(t * P, (t + 1) * P)
                    last = three(ps[:, bank + t, :], act_hi[:, kb, ts], act_lo[:, kb, ts],
                                 whi[:, k % HL, :], wlo[:, k % HL, :], kb == 0, kb == n_kb - 1)
                    if tile_done and t < TT - 1:
                        last.then_inc(tile_done, 1)
                last.then_inc(unit_used, 1)

            def x_columns(n):
                for kb in range(4 * n, 4 * n + 4):
                    for piece, (first, _) in enumerate(X_PIECES):
                        if kb == first:
                            pe.wait_ge(x_in[piece], 16)
                    if kb >= 4:
                        pe.wait_ge(s["xt_lo_done"], kb - 3)
                    for t in range(TT):
                        last = transpose(ps[:, 4 + kb % 4, t * P:(t + 1) * P], x_tok[:, t, kb * P:(kb + 1) * P])
                    last.then_inc(s["xt_ps"], 1)

            def columns():
                pe.wait_ge(s["par_in"], 16 * 11)
                pe.wait_ge(s["xt_lo_done"], KB)
                for i, w in enumerate((PAR_B1 + 16, 2 * FB, 2 * FB)):
                    last = transpose(ps[:, 7, i * P:i * P + w], prow[0:w, i, :], w)
                last.then_inc(s["par_ps"], 1)

            def gates():
                pe.wait_ge(s["wg_lo_done"], 1)
                pe.wait_ge(s["par_done"], 1)
                for kb in range(KB):
                    last = three(ps[:, 4, :], wg_hi[:, kb, :], wg_lo[:, kb, :], xt_hi[:, kb, :], xt_lo[:, kb, :],
                                 kb == 0, kb == KB - 1)
                last.then_inc(s["gate_rows"], 1)

            def exponent_columns():
                pe.wait_ge(s["rows_a"], 1)
                pe.wait_ge(s["em_row"], 1)
                for d in range(2):
                    for c in range(4):
                        cs = slice(c * P, (c + 1) * P)
                        for dist in range(4):
                            at = ((d * 4 + c) * 4 + dist) * 4
                            transpose(ps[:, 4, at:at + 4], row_a[:, d, dist, cs], ML_H)
                        at = 128 + (d * 4 + c) * 4
                        last = transpose(ps[:, 4, at:at + 4], ex[:, d, cs], ML_H)
                last.then_inc(s["cols_ps"], 1)

            def ml_projections(h, hooks, ahead={}):
                ub = h * 32 + U_ML
                for c, (free, n) in enumerate((("free_v", 1), ("free_o", 1), ("conv_b", 2), ("conv_b", 4))):
                    pe.wait_ge(s[free], h * (1 if c < 2 else 4) + n)
                    for k in range(8):
                        do(ahead, 8 * c + k)
                        two_by_two(ub, 8 * c + k, k, 2 * (c % 2), xt_hi, xt_lo)
                        do(hooks, 8 * c + k)

            def mlstm(h):
                def v_token_major():
                    pe.wait_ge(s["free_v"], h + 2)
                    pe.wait_ge(s["y_mul"], h * 2 + 1)
                    for b in range(2):
                        for c in range(TT):
                            last = transpose(ps[:, 4 + c // 2, (c % 2) * 256 + b * P:(c % 2) * 256 + (b + 1) * P],
                                             vt[:, b, c * P:(c + 1) * P])
                    last.then_inc(s["vtr_done"], 1)

                def scores(c):
                    if c == 0:
                        pe.wait_ge(s["qk_lo_done"], h * 4 + 4)
                        pe.wait_ge(s["pv_free"], h * 4 + 1)
                    if c >= 2:
                        pe.wait_ge(s["w_done"], h * 4 + c)
                    for b in range(2):
                        cs = slice(c * P, (c + 1) * P)
                        last = three(ps[:, 6 + c % 2, :], kt_hi[:, b, cs], kt_lo[:, b, cs], qt_hi[:, b, :], qt_lo[:, b, :],
                                     b == 0, b == 1)
                    last.then_inc(s["qkt_done"], 1)

                def values(tc):
                    if tc == 0:
                        pe.wait_ge(s["v_lo_done"], h + 1)
                        pe.wait_ge(s["sw_lo_done"], h * 4 + 4)
                    b0 = 4 + 2 * (tc % 2)
                    if tc >= 2:
                        pe.wait_ge(s["pv_free"], h * 4 + tc)
                    for d in range(2):
                        cs = list(range(tc + 1)) if d == 0 else list(range(tc, 4))
                        for c in cs:
                            slot = FWD_AT[c] + tc - c if d == 0 else BWD_AT[c] + tc
                            block = slice(slot * P, (slot + 1) * P)
                            last = three(ps[:, b0 + d, 0:258], wmat_hi[:, d, block], wmat_lo[:, d, block],
                                         vtok_hi[:, c, :], vtok_lo[:, c, :], c == cs[0], c == cs[-1])
                    last.then_inc(s["pv_done"], 1)

                def y_feature_major():
                    pe.wait_ge(s["hn_done"], h + 1)
                    for b in range(2):
                        for tc in range(4):
                            last = transpose(ps[:, 4 + b, tc * P:(tc + 1) * P], htok[:, tc, b * P:(b + 1) * P])
                        last.then_inc(s["yps_done"], 1)

                return {0: [v_token_major, lambda: scores(0)], 1: [lambda: scores(1)], 3: [lambda: scores(2)], 4: [lambda: scores(3)],
                        7: [lambda: values(0)], 8: [lambda: values(1)], 9: [lambda: values(2)], 10: [lambda: values(3)],
                        14: [y_feature_major]}

            pe.wait_ge(s["ident_in"], 16)
            ml_projections(0, {8: [gates], 20: [exponent_columns]},
                           {0: [lambda: x_columns(0), lambda: x_columns(1)], 2: [lambda: x_columns(2)],
                            4: [lambda: x_columns(3)], 6: [columns]})
            pe.wait_ge(s["cols_done"], 1)
            with pe.Fori(0, ML_H - 1) as h:
                ml_projections(h + 1, mlstm(h))

            def na_v(i, hooks):
                for k in range(8):
                    if k % 4 == 0:
                        if isinstance(i, int):
                            pe.wait_ge(s["free_v"], ML_H + 1)
                        else:
                            pe.wait_ge(s["na_qk_done"], i * 4 + k // 4)
                    four_by_one(i * 24 + U_NA, k, k % 4, KB, ps[:, k // 4, :], xt_hi, xt_lo)
                    do(hooks, k)

            def na_qk(i, pr, hooks):
                for k in range(8):
                    if pr and k % 4 == 0:
                        pe.wait_ge(s["na_v_done"], i * 2 + (k // 4 + 1))
                    four_by_one(i * 24 + U_NA, 8 + 8 * pr + k, k % 4, KB, ps[:, (2, 0)[pr] + k // 4, :], xt_hi, xt_lo)
                    do(hooks, k)

            def v_tiles(i):
                pe.wait_ge(s["na_v_done"], i * 2 + 2)
                pe.wait_ge(s["yna_l"], i * 2 + 1)
                pe.wait_ge(s["y_mul"], 2 * ML_H + 1)
                for t in range(7):
                    first = P * t if t < 4 else ROWS * STRIP + P * (t - 4)
                    for pr in range(2):
                        last = transpose(ps[:, 4 + t // 2, (t % 2) * 256 + pr * P:(t % 2) * 256 + (pr + 1) * P],
                                         nvt[:, pr, first:first + P])
                last.then_inc(s["na_vt_ps"], 1)

            def attend(i, pr, at):
                def na_scores():
                    pe.wait_ge(s["na_v7"], i + 1)
                    pe.wait_ge(s["na_qk_done"], i * 4 + (2 * pr + 3))
                    pe.wait_ge(s["yna_l"], i * 2 + (pr + 1))
                    for hh in range(2):
                        hp = slice(64 * hh, 64 * hh + 64)
                        for j in range(NJ):
                            queries = slice(P * j, P * (j + 1))
                            keys = slice(ROWS * KSTART[j], ROWS * KSTART[j] + 256)
                            last = three(ps[:, 4 + 2 * hh + j // 2, (j % 2) * 256:(j % 2) * 256 + 256],
                                         qk_hi[hp, 0, queries], qk_lo[hp, 0, queries], qk_hi[hp, 1, keys], qk_lo[hp, 1, keys],
                                         True, True)
                        last.then_inc(s["s_done"], 1)

                def probabilities(hh):
                    pe.wait_ge(s["p_done"], i * 4 + (2 * pr + hh + 1))
                    for j in range(NJ):
                        for half in range(2):
                            last = transpose(ps[:, 4 + 2 * hh + j // 2, (2 * (j % 2) + half) * P:(2 * (j % 2) + half + 1) * P],
                                             sc[:, hh, j, half * P:(half + 1) * P])
                    last.then_inc(s["pt_ps"], 1)

                return {at: [na_scores], at + 4: [lambda: probabilities(0)], at + 5: [lambda: probabilities(1)]}

            def na_values(i, pr):
                for hh in range(2):
                    pe.wait_ge(s["pt_done"], i * 4 + (2 * pr + hh + 1))
                    for j in range(NJ):
                        tiles = ((0, 1), (4, 5), (5, 6), (2, 3))[j]
                        for half in range(2):
                            last = mm(ps[64 * hh:64 * hh + 64, 4, j * P:(j + 1) * P],
                                      v7[:, tiles[half], pr * P + 64 * hh:pr * P + 64 * hh + 64],
                                      pt[:, hh, 2 * j + half, :], start=half == 0, stop=half == 1)
                last.then_inc(s["ypv_done"], 1)

            last_head = mlstm(ML_H - 1)
            na_v(0, {u: f for u, f in last_head.items() if u < 8})
            pe.wait_ge(s["free_o"], ML_H + 1)
            na_qk(0, 0, {u - 8: f for u, f in last_head.items() if u >= 8})
            na_qk(0, 1, plus({0: [lambda: v_tiles(0)]}, attend(0, 0, 2)))
            with pe.Fori(1, 4) as i:
                na_v(i, plus({0: [lambda: na_values(i - 1, 0)]}, attend(i - 1, 1, 1)))
                na_qk(i, 0, {1: [lambda: na_values(i - 1, 1)], 2: [lambda: v_tiles(i)]})
                na_qk(i, 1, attend(i, 0, 0))
            def merge(i, hooks):
                ub = i * 24 + U_MG
                for half in range(2):
                    pe.wait_ge(s["merge_sg"], i * 2 + (half + 1))
                    for k in range(8):
                        if 0 in hooks and half == 0 and k % 4 == 0:
                            pe.wait_ge(s["na_qk_done"], 4 * 4 + k // 4)
                        four_by_one(ub, 12 * half + k, k % 4, KB, ps[:, k // 4, :], xt_hi, xt_lo)
                        do(hooks, 12 * half + k)
                    pe.wait_ge(s["mix_done"], i * 2 + (half + 1))
                    for k in range(8, 12):
                        if 0 in hooks and half == 0:
                            pe.wait_ge(s["ylo_done"], 2 * ML_H + 1)
                            if k == 10:
                                pe.wait_ge(s["yna_l"], 9)
                        y_hi, y_lo = ((yml_hi, yml_lo), (yna_hi, yna_lo))[(k - 8) // 2]
                        four_by_one(ub, 12 * half + k, k % 2, 8, ps[:, 2 + (k - 8) // 2, :], y_hi, y_lo)
                        do(hooks, 12 * half + k)

            merge(0, plus({0: [lambda: na_values(3, 0)]}, attend(3, 1, 1), {8: [lambda: na_values(3, 1)]}))
            with pe.Fori(1, KB // 2) as i:
                merge(i, {})

            with pe.Fori(0, 2) as i:
                for half in range(2):
                    pe.wait_ge(s["wo_free"], i * 2 + half + 1)
                    for k in range(KB):
                        pe.wait_ge(s["mxlo_done"], k + 1)
                        one_by_four(i * 32 + U_WO, 16 * half + k, k, KB, 4 - 4 * half, mx_hi, mx_lo,
                                    s["wo_tiles"] if half and k == KB - 1 else None)
            def h_columns(kb):
                pe.wait_ge(s["hn_cols_a"], kb // 4 + 1)
                pe.wait_ge(s["hn_cols_v"], kb // 4 + 1)
                if kb >= 4:
                    pe.wait_ge(s["ht_lo_d"], kb - 3)
                for t in range(TT):
                    last = transpose(ps[:, 4 + kb % 4, t * P:(t + 1) * P], res[:, t, kb * P:(kb + 1) * P])
                last.then_inc(s["ht_ps"], 1)

            def ffn_up(g, i, hooks):
                for c in range(4):
                    pe.wait_ge(s["d_free"], g * 4 + c // 2 + 1)
                    pe.wait_ge(s["u_mul"], g * 8 + i * 4 + (c + 1))
                    for k in range(8):
                        if hooks and c == 0:
                            pe.wait_ge(s["ht_lo_d"], 4 * (k % 4) + 4)
                        four_by_one(g * 96 + i * 32 + U_FF, 8 * c + k, k % 4, KB, ps[:, 2 * c + k // 4, :], ht_hi, ht_lo)
                        do(hooks, 8 * c + k)

            def ffn_down(g):
                with pe.Fori(0, 2) as i:
                    for half in range(2):
                        pe.wait_ge(s["u_mul"], g * 8 + (10, 12)[half])
                        pe.wait_ge(s["d_free"], g * 4 + i * 2 + half + 1)
                        for k in range(G):
                            pe.wait_ge(s["act_done"], g * 8 + (k + 3))
                            one_by_four(g * 96 + i * 16 + (U_FF + 64), 8 * half + k, k, G, 4 * half, ac_hi, ac_lo)

            for kb in range(8):
                h_columns(kb)
            ffn_up(0, 0, {0: [lambda kb=kb: h_columns(kb) for kb in range(8, 12)],
                          1: [lambda kb=kb: h_columns(kb) for kb in range(12, 16)]})
            ffn_up(0, 1, {})
            ffn_down(0)
            with pe.Fori(1, NG) as g:
                with pe.Fori(0, 2) as i:
                    ffn_up(g, i, {})
                ffn_down(g)
            for c in range(TAIL):
                pe.wait_ge(s["d_free"], NG * 4 + c // 2 + 1)
                for k in range(8):
                    four_by_one(U_TL, 8 * c + k, k % 4, KB, ps[:, 2 * c + k // 4, :], ht_hi, ht_lo)
            for n in range(3):
                pe.wait_ge(s["u_mul"], NG * 8 + (6, 7, 7)[n])
                pe.wait_ge(s["d_free"], NG * 4 + n + 1)
                for k in range(TAIL):
                    pe.wait_ge(s["act_done"], NG * 8 + k + 3)
                    one_by_four(U_TL, 8 * TAIL + n * TAIL + k, k, TAIL, 4 * (n % 2), ac_hi, ac_lo)
            pe.wait_ge(s["d_free"], NG * 4 + 4)
            unit_ready(U_END - 1, 0)
            for t in range(TT):
                ts = slice(t * P, (t + 1) * P)
                for k in range(TAIL):
                    slot = (8 * TAIL + 3 * TAIL + k) % HL
                    last = three(ps[:, 4 + t, :], ac_hi[:, k, ts], ac_lo[:, k, ts], whi[:, slot, :], wlo[:, slot, :],
                                 k == 0, k == TAIL - 1)
                last.then_inc(s["tile_sums"], 1)


_INS = ["x", "w_in", "na_rpb", "ml_conv_w", "ml_conv_b", "ml_igate_b", "ml_fgate_b", "ml_norm_w", "w_branch_na",
        "w_branch_ml", "w_out", "ln1_g", "ln1_b", "ffn_w_up", "ffn_conv_w", "ffn_conv_b", "ffn_w_down", "ln2_g", "ln2_b"]


def shape_constants():
    c = np.zeros((P, 3 * P + NJ * 256), np.float32)
    c[:, 0:P] = np.eye(P)
    a, b = np.arange(P)[:, None], np.arange(P)[None, :]
    c[:, P:2 * P] = np.where(a <= b, 0.0, NEG)
    c[:, 2 * P:3 * P] = np.where(a >= b, 0.0, NEG)
    for j in range(NJ):
        p, f = np.arange(P)[:, None], np.arange(256)[None, :]
        q = QCOLS * j + STRIP * (p // (ROWS * STRIP)) + STRIP - 1 - p % STRIP
        k = KSTART[j] + STRIP * (f // (ROWS * STRIP)) + f % STRIP
        w = np.clip(q - WIN_COLS // 2, 0, GRID_W - WIN_COLS)
        c[:, 3 * P + j * 256:3 * P + (j + 1) * 256] = np.where((k >= w) & (k < w + WIN_COLS), 3e38, NEG)
    return c


def kernel(**inputs):
    import concourse.bacc as bacc
    from concourse.bass_utils import run_bass_kernel_spmd

    nc = bacc.Bacc("TRN2", target_bir_lowering=False, num_devices=1)
    arrays, args = {}, []
    for name in _INS:
        a = np.ascontiguousarray(inputs[name])
        arrays["in_" + name] = a
        args.append(nc.dram_tensor("in_" + name, a.shape, mybir.dt.from_np(a.dtype), kind="ExternalInput").ap())
    consts = shape_constants()
    arrays["in_consts"] = consts
    args.append(nc.dram_tensor("in_consts", consts.shape, F32, kind="ExternalInput").ap())
    out = nc.dram_tensor("out_0", (1, S, D), F32, kind="ExternalOutput").ap()
    build(nc, *args, out)
    r = run_bass_kernel_spmd(nc, [arrays], core_ids=[0])
    return r.results[0]["out_0"]
```
